# Optimizing a Trainium2 kernel written in Bass

```python
import math
import jax
import jax.numpy as jnp
from jax import lax
import numpy as np

D_MODEL = 1024
BATCH = 1
SEQ = 512
DEPTH = 2
DEC_BATCH = 1
DEC_SEQ = 32
PAST_LEN = 512

CHUNK = 64
Q_BLOCK = 128
HEAD_DIM = 64
FOX_HEADS = 8
DIFF_HEADS = 4
RWKV_HEADS = 8
FOX_W = FOX_HEADS * HEAD_DIM
DIFF_W = DIFF_HEADS * 2 * HEAD_DIM
RWKV_W = RWKV_HEADS * HEAD_DIM
BRANCH_W = 512
N_BRANCH = 3
DECAY_LORA = 64
AAA_LORA = 64
GATE_LORA = 128
RWKV_IN = 3 * RWKV_W + DECAY_LORA + AAA_LORA + GATE_LORA
ROT_DIM = HEAD_DIM // 4
ROPE_THETA = 500000.0
N_MEM = 256
XATTN_HEADS = 4
XATTN_HEAD_DIM = 128
XATTN_W = XATTN_HEADS * XATTN_HEAD_DIM
FFN_HIDDEN = -(-8 * D_MODEL // (3 * 256)) * 256
IN_SPLITS = (FOX_W, FOX_W, FOX_W, FOX_HEADS, DIFF_W, DIFF_W, DIFF_W, RWKV_IN, N_BRANCH * D_MODEL)
IN_WIDTH = sum(IN_SPLITS)
RWKV_SPLITS = (RWKV_W, RWKV_W, RWKV_W, DECAY_LORA, AAA_LORA, GATE_LORA)
FORGET_BIAS_MEAN = 2.0
RMS_EPS = 1e-6
RWKV_GN_EPS = 64e-5

kernel_name = 'hybrid_fox_diff_rwkv7_stream_step'

def _rmsnorm(x, g):
    x32 = x.astype(jnp.float32)
    y = x32 * lax.rsqrt(jnp.mean(x32 * x32, axis=-1, keepdims=True) + RMS_EPS)
    return (y * g.astype(jnp.float32)).astype(x.dtype)

def _split_cols(a, sizes):
    return jnp.split(a, np.cumsum(sizes)[:-1].tolist(), axis=-1)

def _rotary(x, pos):
    half = ROT_DIM // 2
    inv = ROPE_THETA ** (-jnp.arange(half, dtype=jnp.float32) / half)
    ang = pos.astype(jnp.float32)[:, None] * inv[None, :]
    shape = (1, pos.shape[0]) + (1,) * (x.ndim - 3) + (half,)
    cos, sin = jnp.cos(ang).reshape(shape), jnp.sin(ang).reshape(shape)
    x1 = x[..., :half].astype(jnp.float32)
    x2 = x[..., half:ROT_DIM].astype(jnp.float32)
    rot = jnp.concatenate([x1 * cos - x2 * sin, x2 * cos + x1 * sin], axis=-1).astype(x.dtype)
    return jnp.concatenate([rot, x[..., ROT_DIM:]], axis=-1)

def _over_query_blocks(fn, *qs):
    b, t = qs[0].shape[:2]
    if t <= Q_BLOCK:
        return fn(*qs)
    nb = t // Q_BLOCK
    blocks = tuple(jnp.moveaxis(a.reshape((b, nb, Q_BLOCK) + a.shape[2:]), 1, 0) for a in qs)
    out = lax.map(lambda args: fn(*args), blocks)
    return jnp.moveaxis(out, 0, 1).reshape((b, t) + out.shape[3:])

def _fox_attention(q, k_all, v_all, d_q, d_all, qpos, kpos):
    scale = HEAD_DIM ** -0.5
    d_k = jnp.swapaxes(d_all, 1, 2)

    def block(qb, dqb, pb):
        s = jnp.einsum('bqhd,bkhd->bhqk', qb, k_all).astype(jnp.float32) * scale
        s = s + jnp.swapaxes(dqb, 1, 2)[:, :, :, None] - d_k[:, :, None, :]
        mask = kpos[None, None, None, :] <= pb[:, None, :, None]
        p = jax.nn.softmax(jnp.where(mask, s, -jnp.inf), axis=-1)
        return jnp.einsum('bhqk,bkhd->bqhd', p.astype(v_all.dtype), v_all)

    return _over_query_blocks(block, q, d_q, qpos)

def _diff_attention(q, k_all, v_all, qpos, kpos, lam):
    scale = HEAD_DIM ** -0.5
    kchunk = kpos // CHUNK

    def block(qb, pb):
        s = jnp.einsum('bqhcd,bkhcd->bhcqk', qb, k_all).astype(jnp.float32) * scale
        mask = kchunk[None, None, None, None, :] <= (pb // CHUNK)[:, None, None, :, None]
        p = jax.nn.softmax(jnp.where(mask, s, -jnp.inf), axis=-1)
        pd = p[:, :, 0] - lam * p[:, :, 1]
        return jnp.einsum('bhqk,bkhv->bqhv', pd.astype(v_all.dtype), v_all)

    return _over_query_blocks(block, q, qpos)

def _rwkv7_scan(r, w, k, v, kk, a, s0):
    def step(S, xs):
        rt, wt, kt, vt, kkt, at = xs
        sa = jnp.einsum('bhvk,bhk->bhv', S, -kkt)
        S = S * wt[:, :, None, :] + sa[..., None] * (kkt * at)[:, :, None, :] + vt[..., None] * kt[:, :, None, :]
        return S, jnp.einsum('bhvk,bhk->bhv', S, rt)

    xs = tuple(jnp.swapaxes(z.astype(jnp.float32), 0, 1) for z in (r, w, k, v, kk, a))
    s_fin, y = lax.scan(step, s0.astype(jnp.float32), xs)
    return jnp.swapaxes(y, 0, 1), s_fin

def _mixer_sublayer(h, past, l, mw):
    (w_in, fox_forget_bias, diff_lambda, diff_subln, rwkv_mu, rwkv_w0, rwkv_w2, rwkv_a0, rwkv_a2,
     rwkv_g2, rwkv_kk_scale, rwkv_ka, rwkv_rk, rwkv_ln_gain, rwkv_ln_bias, w_branch, w_out) = mw
    fox_k0, fox_v0, fox_lf0, diff_k0, diff_v0, rwkv_s0, rwkv_prev0 = past
    f32 = jnp.float32
    b, t, _ = h.shape
    p_len = fox_k0.shape[1]
    qpos1 = p_len + jnp.arange(t, dtype=jnp.int32)
    kpos = jnp.arange(p_len + t, dtype=jnp.int32)
    qpos = jnp.broadcast_to(qpos1, (b, t))
    a_q, a_k, a_v, a_f, b_q, b_k, b_v, c_in, gate_in = _split_cols(h @ w_in, IN_SPLITS)

    fq = a_q.reshape(b, t, FOX_HEADS, HEAD_DIM)
    fk = a_k.reshape(b, t, FOX_HEADS, HEAD_DIM)
    fv = a_v.reshape(b, t, FOX_HEADS, HEAD_DIM)
    log_f = jax.nn.log_sigmoid((a_f + fox_forget_bias).astype(f32))
    d_all = jnp.cumsum(jnp.concatenate([fox_lf0.astype(f32), log_f], axis=1), axis=1)
    out_a = _fox_attention(fq, jnp.concatenate([fox_k0, fk], axis=1), jnp.concatenate([fox_v0, fv], axis=1),
                           d_all[:, p_len:], d_all, qpos, kpos).reshape(b, t, FOX_W)

    dq = _rotary(b_q.reshape(b, t, DIFF_HEADS, 2, HEAD_DIM), qpos1)
    dk = _rotary(b_k.reshape(b, t, DIFF_HEADS, 2, HEAD_DIM), qpos1)
    dv = b_v.reshape(b, t, DIFF_HEADS, 2 * HEAD_DIM)
    lam_init = 0.8 - 0.6 * math.exp(-0.3 * l)
    lq1, lk1, lq2, lk2 = diff_lambda.astype(f32)
    lam = jnp.exp(jnp.sum(lq1 * lk1)) - jnp.exp(jnp.sum(lq2 * lk2)) + lam_init
    o_b = _diff_attention(dq, jnp.concatenate([diff_k0, dk], axis=1), jnp.concatenate([diff_v0, dv], axis=1),
                          qpos, kpos, lam)
    out_b = (_rmsnorm(o_b, diff_subln) * (1.0 - lam_init)).reshape(b, t, DIFF_W)

    prev = jnp.concatenate([rwkv_prev0[:, None].astype(c_in.dtype), c_in[:, :-1]], axis=1)
    xs = c_in + rwkv_mu * (prev - c_in)
    cr, ck, cv, xw, xa, xg = _split_cols(xs, RWKV_SPLITS)
    heads = lambda z: z.reshape(b, t, RWKV_HEADS, HEAD_DIM)
    w_raw = -jax.nn.softplus(-(rwkv_w0 + jnp.tanh(xw) @ rwkv_w2).astype(f32)) - 0.5
    decay = jnp.exp(-jnp.exp(w_raw))
    a = jax.nn.sigmoid((rwkv_a0 + xa @ rwkv_a2).astype(f32))
    g = jax.nn.sigmoid(xg) @ rwkv_g2
    kk = heads(ck * rwkv_kk_scale).astype(f32)
    kk = kk / jnp.maximum(jnp.sqrt(jnp.sum(kk * kk, axis=-1, keepdims=True)), 1e-12)
    kmod = ck.astype(f32) * (1.0 + (a - 1.0) * rwkv_ka.astype(f32))
    y_c, s_new = _rwkv7_scan(heads(cr), heads(decay), heads(kmod), heads(cv), kk, heads(a), rwkv_s0)
    mu = jnp.mean(y_c, axis=-1, keepdims=True)
    var = jnp.mean(jnp.square(y_c - mu), axis=-1, keepdims=True)
    y_n = ((y_c - mu) * lax.rsqrt(var + RWKV_GN_EPS)).reshape(b, t, RWKV_W)
    y_n = y_n * rwkv_ln_gain.astype(f32) + rwkv_ln_bias.astype(f32)
    bonus = jnp.sum(heads(cr).astype(f32) * heads(kmod) * rwkv_rk.astype(f32), axis=-1, keepdims=True) * heads(cv).astype(f32)
    out_c = ((y_n + bonus.reshape(b, t, RWKV_W)) * g.astype(f32)).astype(h.dtype)

    branches = jnp.stack([out_a, out_b, out_c], axis=2)
    proj = jnp.einsum('btiw,iwd->btid', branches, w_branch)
    gates = jax.nn.sigmoid(gate_in.reshape(b, t, N_BRANCH, D_MODEL))
    y = jnp.sum(gates * proj, axis=2) @ w_out
    new_state = (fk, fv, log_f, dk, dv, s_new, c_in[:, -1])
    return y, new_state

def _memory_kv(mem, g, w_xkv):
    m = _rmsnorm(mem, g) @ w_xkv
    mk, mv = jnp.split(m, 2, axis=-1)
    b, n, _ = mem.shape
    return mk.reshape(b, n, XATTN_HEADS, XATTN_HEAD_DIM), mv.reshape(b, n, XATTN_HEADS, XATTN_HEAD_DIM)

def _cross_attention(h, mem_k, mem_v, w_xq, w_xo):
    b, t, _ = h.shape
    q = (h @ w_xq).reshape(b, t, XATTN_HEADS, XATTN_HEAD_DIM)
    s = jnp.einsum('bqhd,bkhd->bhqk', q, mem_k).astype(jnp.float32) * XATTN_HEAD_DIM ** -0.5
    p = jax.nn.softmax(s, axis=-1)
    o = jnp.einsum('bhqk,bkhd->bqhd', p.astype(mem_v.dtype), mem_v).reshape(b, t, XATTN_W)
    return o @ w_xo

def _swiglu(h, w_ffn_in, w_ffn_out):
    u, v = jnp.split(h @ w_ffn_in, 2, axis=-1)
    return (jax.nn.silu(u) * v) @ w_ffn_out

def _layer(x, past, mem_k, mem_v, l, mw, ow):
    (norm_mix_pre, norm_mix_post, norm_x_pre, norm_x_post, w_xq, w_xo,
     norm_ffn_pre, norm_ffn_post, w_ffn_in, w_ffn_out) = ow
    y, new_state = _mixer_sublayer(_rmsnorm(x, norm_mix_pre), past, l, mw)
    x = x + _rmsnorm(y, norm_mix_post)
    x = x + _rmsnorm(_cross_attention(_rmsnorm(x, norm_x_pre), mem_k, mem_v, w_xq, w_xo), norm_x_post)
    x = x + _rmsnorm(_swiglu(_rmsnorm(x, norm_ffn_pre), w_ffn_in, w_ffn_out), norm_ffn_post)
    return x, new_state

def setup_inputs(seed: int = 0) -> dict:
    key = jax.random.key(seed)
    ks = iter(jax.random.split(key, 64))
    f32 = jnp.float32
    L = DEPTH

    def nrm(shape, scale=1.0):
        return jax.random.normal(next(ks), shape, f32) * scale

    def gain(width):
        return 1.0 + nrm((L, width), 0.05)

    return {
        'x_prompt': nrm((BATCH, SEQ, D_MODEL)),
        'x_sample': nrm((DEC_BATCH, DEC_SEQ, D_MODEL)),
        'mem_prompt': nrm((BATCH, N_MEM, D_MODEL)),
        'cache_fox_k': nrm((L, DEC_BATCH, PAST_LEN, FOX_HEADS, HEAD_DIM)),
        'cache_fox_v': nrm((L, DEC_BATCH, PAST_LEN, FOX_HEADS, HEAD_DIM)),
        'cache_fox_logf': jax.nn.log_sigmoid(FORGET_BIAS_MEAN + nrm((L, DEC_BATCH, PAST_LEN, FOX_HEADS))),
        'cache_diff_k': nrm((L, DEC_BATCH, PAST_LEN, DIFF_HEADS, 2, HEAD_DIM)),
        'cache_diff_v': nrm((L, DEC_BATCH, PAST_LEN, DIFF_HEADS, 2 * HEAD_DIM)),
        'state_rwkv': nrm((L, DEC_BATCH, RWKV_HEADS, HEAD_DIM, HEAD_DIM)),
        'state_rwkv_shift': nrm((L, DEC_BATCH, RWKV_IN)),
        'cache_mem_k': nrm((L, DEC_BATCH, N_MEM, XATTN_HEADS, XATTN_HEAD_DIM)),
        'cache_mem_v': nrm((L, DEC_BATCH, N_MEM, XATTN_HEADS, XATTN_HEAD_DIM)),
        'norm_mix_pre': gain(D_MODEL),
        'norm_mix_post': gain(D_MODEL),
        'w_in': nrm((L, D_MODEL, IN_WIDTH), D_MODEL ** -0.5),
        'fox_forget_bias': FORGET_BIAS_MEAN + nrm((L, FOX_HEADS), 0.3),
        'diff_lambda': nrm((L, 4, HEAD_DIM), 0.1),
        'diff_subln': gain(2 * HEAD_DIM),
        'rwkv_mu': jax.random.uniform(next(ks), (L, RWKV_IN), f32),
        'rwkv_w0': nrm((L, RWKV_W), 0.5),
        'rwkv_w2': nrm((L, DECAY_LORA, RWKV_W), DECAY_LORA ** -0.5),
        'rwkv_a0': nrm((L, RWKV_W), 0.5),
        'rwkv_a2': nrm((L, AAA_LORA, RWKV_W), AAA_LORA ** -0.5),
        'rwkv_g2': nrm((L, GATE_LORA, RWKV_W), GATE_LORA ** -0.5),
        'rwkv_kk_scale': 0.85 + nrm((L, RWKV_W), 0.05),
        'rwkv_ka': 1.0 + nrm((L, RWKV_W), 0.05),
        'rwkv_rk': nrm((L, RWKV_HEADS, HEAD_DIM), 0.1),
        'rwkv_ln_gain': gain(RWKV_W),
        'rwkv_ln_bias': nrm((L, RWKV_W), 0.02),
        'w_branch': nrm((L, N_BRANCH, BRANCH_W, D_MODEL), BRANCH_W ** -0.5),
        'w_out': nrm((L, D_MODEL, D_MODEL), D_MODEL ** -0.5),
        'norm_x_pre': gain(D_MODEL),
        'norm_x_post': gain(D_MODEL),
        'norm_mem': gain(D_MODEL),
        'w_xq': nrm((L, D_MODEL, XATTN_W), D_MODEL ** -0.5),
        'w_xkv': nrm((L, D_MODEL, 2 * XATTN_W), D_MODEL ** -0.5),
        'w_xo': nrm((L, XATTN_W, D_MODEL), XATTN_W ** -0.5),
        'norm_ffn_pre': gain(D_MODEL),
        'norm_ffn_post': gain(D_MODEL),
        'w_ffn_in': nrm((L, D_MODEL, 2 * FFN_HIDDEN), D_MODEL ** -0.5),
        'w_ffn_out': nrm((L, FFN_HIDDEN, D_MODEL), FFN_HIDDEN ** -0.5),
    }

def reference(x_prompt, x_sample, mem_prompt, cache_fox_k, cache_fox_v, cache_fox_logf, cache_diff_k,
              cache_diff_v, state_rwkv, state_rwkv_shift, cache_mem_k, cache_mem_v, norm_mix_pre, norm_mix_post,
              w_in, fox_forget_bias, diff_lambda, diff_subln, rwkv_mu, rwkv_w0, rwkv_w2, rwkv_a0, rwkv_a2,
              rwkv_g2, rwkv_kk_scale, rwkv_ka, rwkv_rk, rwkv_ln_gain, rwkv_ln_bias, w_branch, w_out,
              norm_x_pre, norm_x_post, norm_mem, w_xq, w_xkv, w_xo, norm_ffn_pre, norm_ffn_post,
              w_ffn_in, w_ffn_out):
    mixer_w = (w_in, fox_forget_bias, diff_lambda, diff_subln, rwkv_mu, rwkv_w0, rwkv_w2, rwkv_a0, rwkv_a2,
               rwkv_g2, rwkv_kk_scale, rwkv_ka, rwkv_rk, rwkv_ln_gain, rwkv_ln_bias, w_branch, w_out)
    other_w = (norm_mix_pre, norm_mix_post, norm_x_pre, norm_x_post, w_xq, w_xo,
               norm_ffn_pre, norm_ffn_post, w_ffn_in, w_ffn_out)
    b, dt = x_prompt.shape[0], x_prompt.dtype
    past_prompt = (jnp.zeros((b, 0, FOX_HEADS, HEAD_DIM), dt), jnp.zeros((b, 0, FOX_HEADS, HEAD_DIM), dt),
                   jnp.zeros((b, 0, FOX_HEADS), jnp.float32), jnp.zeros((b, 0, DIFF_HEADS, 2, HEAD_DIM), dt),
                   jnp.zeros((b, 0, DIFF_HEADS, 2 * HEAD_DIM), dt),
                   jnp.zeros((b, RWKV_HEADS, HEAD_DIM, HEAD_DIM), jnp.float32), jnp.zeros((b, RWKV_IN), dt))
    xp, xs = x_prompt, x_sample
    p_new, s_new, p_mk, p_mv = [], [], [], []
    for l in range(DEPTH):
        mw = tuple(w[l] for w in mixer_w)
        ow = tuple(w[l] for w in other_w)
        mk, mv = _memory_kv(mem_prompt, norm_mem[l], w_xkv[l])
        xp, st_p = _layer(xp, past_prompt, mk, mv, l, mw, ow)
        past_s = (cache_fox_k[l], cache_fox_v[l], cache_fox_logf[l], cache_diff_k[l], cache_diff_v[l],
                  state_rwkv[l], state_rwkv_shift[l])
        xs, st_s = _layer(xs, past_s, cache_mem_k[l], cache_mem_v[l], l, mw, ow)
        p_new.append(st_p)
        s_new.append(st_s)
        p_mk.append(mk)
        p_mv.append(mv)
    p_fox_k, p_fox_v, p_fox_logf, p_diff_k, p_diff_v, p_rwkv_state, p_rwkv_shift = (jnp.stack(e) for e in zip(*p_new))
    s_fox_k, s_fox_v, s_fox_logf, s_diff_k, s_diff_v, s_rwkv_state, s_rwkv_shift = (jnp.stack(e) for e in zip(*s_new))
    p_mem_k = jnp.stack(p_mk)
    p_mem_v = jnp.stack(p_mv)
    return (xp, xs, p_fox_k, p_fox_v, p_fox_logf, p_diff_k, p_diff_v, p_rwkv_state, p_rwkv_shift, p_mem_k, p_mem_v,
            s_fox_k, s_fox_v, s_fox_logf, s_diff_k, s_diff_v, s_rwkv_state, s_rwkv_shift)


_drawn_inputs = setup_inputs


def setup_inputs(seed=0):
    import zlib

    import numpy as np

    out = dict(_drawn_inputs(seed))
    spreads = {}
    factors = {'rwkv_kk_scale': 3.068, 'rwkv_ln_bias': 4.948}
    for name, (base, spread) in spreads.items():
        noise = np.random.default_rng([zlib.crc32(name.encode()), seed]).standard_normal(out[name].shape)
        drawn = base * np.exp(spread * noise) if base else spread * noise
        out[name] = jnp.asarray(drawn.astype(out[name].dtype))
    for name, factor in factors.items():
        out[name] = (out[name] * factor).astype(out[name].dtype)
    return out
```

```python
from contextlib import ExitStack
import math

import numpy as np

import concourse.bass as bass
from concourse import mybir

F32 = mybir.dt.float32
BF16 = mybir.dt.bfloat16
ACT = mybir.ActivationFunctionType
ALU = mybir.AluOpType
AX = mybir.AxisListType
ds = bass.ds

D_MODEL, SEQ, DEPTH, DEC_SEQ, PAST = 1024, 512, 2, 32, 512
CHUNK, HEAD_DIM, FOX_HEADS, DIFF_HEADS, RWKV_HEADS = 64, 64, 8, 4, 8
BRANCH_W, N_MEM, X_HEADS, X_DIM = 512, 256, 4, 128
FFN = -(-8 * D_MODEL // (3 * 256)) * 256
RWKV_IN = 3 * 512 + 64 + 64 + 128
IN_WIDTH = 3 * 512 + FOX_HEADS + 3 * 512 + RWKV_IN + 3 * D_MODEL
ROPE_THETA, RMS_EPS, GN_EPS = 500000.0, 1e-6, 64e-5
P = 128
T = SEQ + DEC_SEQ
HT = T // 2
KM = D_MODEL // P
TP = 9 * CHUNK
KF = FFN // P

RING = 4
S_IN, S_MERGE, S_OUT, S_MEM, S_XQ, S_XO, S_FFI, S_FFO = 20, 24, 4, 4, 2, 4, 22, 16
SLOTS = S_IN + S_MERGE + S_OUT + S_MEM + S_XQ + S_XO + S_FFI + S_FFO
USES = SLOTS // RING
FFO_SPLIT = (6, 6, 5, 5)

N_IN, N_MERGE, N_OUT, N_MEMKV, N_XQ, N_XO, N_FFI, N_FFO = 39, 48, 8, 8, 4, 8, 44, 8
G_IN = 0
G_MERGE = G_IN + N_IN
G_OUT = G_MERGE + N_MERGE
G_MEM = G_OUT + N_OUT
G_XQ = G_MEM + N_MEMKV
G_XO = G_XQ + N_XQ
G_FFI = G_XO + N_XO
G_FFO = G_FFI + N_FFI
TILES = G_FFO + N_FFO

R_FQ, R_FK, R_FV, R_DQ, R_DK, R_DV = (i * 512 for i in range(6))
R_RW = 3072
R_LW = R_RW + RWKV_IN
R_END = R_LW + 3 * 512

_c = {}
_n = 0
for _name, _w in (("ident", 128), ("stack", 192), ("bdones", 128), ("rot", 128), ("mfox", 128), ("mdiff", 128),
                  ("up_d", 192), ("up_s", 192), ("up_i", 192), ("lo_d", 192), ("lo_o", 192), ("reset", TP), ("lam", 4)):
    _c[_name] = (_n, _n + _w)
    _n += _w
NCONST = _n

_v = {}
NVEC_OF = {}
_n = 0
for _name, _w in (("norm_mix_pre", 8), ("norm_mix_post", 8), ("norm_x_pre", 8), ("norm_x_post", 8), ("norm_mem", 8),
                  ("norm_ffn_pre", 8), ("norm_ffn_post", 8), ("rwkv_mu", 14), ("rwkv_w0", 4), ("rwkv_a0", 4),
                  ("rwkv_kk_scale", 4), ("rwkv_ka", 4), ("rwkv_rk", 4), ("rwkv_ln_gain", 4), ("rwkv_ln_bias", 4),
                  ("diff_subln", 1), ("state_rwkv_shift", 14)):
    _v[_name], NVEC_OF[_name] = _n, _w
    _n += _w
NVEC = _n
RW_LOADS = 11


def constants():
    c = np.zeros((P, NCONST), np.float32)

    def put(name, a):
        c[:, _c[name][0]:_c[name][1]] = a

    i64 = np.eye(64, dtype=np.float32)
    put("ident", np.eye(P))
    put("stack", np.tile(np.vstack([i64, i64]), (1, 3)))
    put("bdones", np.kron(np.eye(2), np.ones((64, 64))))
    rot = np.zeros((P, P), np.float32)
    for b in (0, 64):
        for j in range(8):
            rot[b + j + 8, b + j] = -1.0
            rot[b + j, b + j + 8] = 1.0
    put("rot", rot)
    q, k = np.arange(P)[:, None], np.arange(P)[None, :]
    put("mfox", np.where(k <= q, 0.0, -1e30))
    put("mdiff", np.where(k // CHUNK <= q // CHUNK, 0.0, -1e30))
    r, s = np.arange(64)[:, None], np.arange(64)[None, :]
    same = r // 16 == s // 16
    for name, m in (("up_d", -1.0 * ((r < s) & same)), ("up_s", r < s), ("up_i", r <= s),
                    ("lo_d", -1.0 * ((r > s) & same)), ("lo_o", (r > s) & ~same)):
        put(name, np.tile(np.vstack([m, m]), (1, 3)))
    put("reset", (np.arange(TP) % CHUNK != 0)[None, :])
    lam = [0.8 - 0.6 * math.exp(-0.3 * l) for l in range(DEPTH)]
    put("lam", np.array([lam[0], lam[1], 1 - lam[0], 1 - lam[1]])[None, :])
    half = 8
    inv = (np.float32(ROPE_THETA) ** (-np.arange(half, dtype=np.float32) / np.float32(half))).astype(np.float32)
    pos = np.concatenate([np.arange(SEQ), PAST + np.arange(DEC_SEQ)]).astype(np.float32)
    ang = (pos[None, :] * inv[:, None]).astype(np.float32)
    rope = np.zeros((P, 2, T), np.float32)
    rope[:, 0] = 1.0
    for b in (0, 8, 64, 72):
        rope[b:b + 8, 0] = np.cos(ang)
        rope[b:b + 8, 1] = np.sin(ang)
    return c, rope


def build_program(nc, A, C_const, C_rope, O):
    (y_prompt, y_sample, p_fox_k, p_fox_v, p_fox_logf, p_diff_k, p_diff_v, p_state, p_shift, p_mem_k, p_mem_v,
     s_fox_k, s_fox_v, s_fox_logf, s_diff_k, s_diff_v, s_state, s_shift) = O
    proj_d = nc.dram_tensor("proj_scratch", (R_END, T), F32).ap()
    memn_d = nc.dram_tensor("memn_scratch", (P, KM * N_MEM), F32).ap()
    dcum_d = nc.dram_tensor("dcum_scratch", (2, FOX_HEADS, T + PAST), F32).ap()

    with ExitStack() as ctx:
        def sb(name, shape, dt=F32):
            return ctx.enter_context(nc.sbuf_tensor(name, shape, dt))

        def sem(name):
            return ctx.enter_context(nc.semaphore(name))

        xT = sb("xT", [P, KM, T])
        hT = sb("hT", [P, KM, T])
        ring = sb("ring", [P, RING, 8, 256])
        brT = sb("brT", [P, 12, T])
        CB = sb("CB", [P, NCONST])
        identb = sb("identb", [P, P], BF16)
        mfoxb = sb("mfoxb", [P, P], BF16)
        mdiffb = sb("mdiffb", [P, P], BF16)
        ones = sb("ones", [P, P])
        VT = sb("VT", [P, P])
        small = sb("small", [P, 64])
        eps = sb("eps", [P, 4])
        lam4 = sb("lam4", [P, 4, HEAD_DIM])
        lamp = sb("lamp", [P, 2, HEAD_DIM])
        NU = 25990
        U = sb("U", [P, NU])
        PS = ctx.enter_context(nc.psum_tensor("PS", [P, 8, 512], F32))

        def const(name):
            return CB[:, _c[name][0]:_c[name][1]]

        def vec(name, i):
            return VT[:, _v[name] + i:_v[name] + i + 1]

        def pair(q):
            return PS[:, 2 * q:2 * q + 2, :].rearrange("p a n -> p (a n)")

        def carver(start=0):
            at = [start]

            def carve(*dims):
                n = int(np.prod(dims))
                v = U[:, at[0]:at[0] + n]
                at[0] += n
                assert at[0] <= NU, at[0]
                if len(dims) == 1:
                    return v
                names = " ".join("abc"[:len(dims)])
                return v.rearrange(f"p ({names}) -> p {names}", **{"abc"[i]: d for i, d in enumerate(dims)})
            return carve

        cv = carver(0)
        SQ, RS = cv(KM, T), cv(T)
        xtok = cv(5, D_MODEL)
        mtok = cv(2, D_MODEL)
        mnT = cv(KM, N_MEM)
        cv = carver(KM * T + T)
        EST = cv(2, 2, T)
        AF = cv(T)
        DC = cv(T + PAST)
        LFT = cv(5, 8)
        PLF = cv(4, 8)
        LFX = cv(T + PAST)
        NDC = cv(T + PAST)
        VR = cv(P)
        TZ = cv(2, T)
        ONES = cv(SEQ)
        cv = carver(0)
        FQ, FK = cv(2, T), cv(2, T + PAST)
        FVR, FPK = cv(2, T), cv(2, 4, HEAD_DIM)
        FVT, FKT = cv(2, 9, HEAD_DIM), cv(2, 5, HEAD_DIM)
        FP, FPT = cv(2, T), cv(2, 5 * P)
        FST = cv(2, 4)
        cv = carver(0)
        ROPE = cv(2, T)
        DQ, DK = cv(2, T), cv(2, T + PAST)
        DVR, DPK = cv(2, T), cv(2, 4, P)
        DVT, DKT = cv(2, 9, P), cv(2, 5, P)
        DPB = cv(2, 2, T)
        DPT = cv(2, 5 * P)
        DTMP, DO, DRS = cv(T), cv(T), cv(T)
        DST = cv(2, 8)
        cv = carver(0)
        LX = cv(2, T + 2)
        LT = cv(2, T + 1)
        LXS = cv(2, T)
        LW2, LG2 = cv(512), cv(512)
        LO = cv(12, T)
        cv = carver(0)
        W_RAW = cv(3, TP)
        Rx, Kx, Vx, LWx, Ax, Gx = (cv(TP) for _ in range(6))
        KR = cv(9, 2 * CHUNK)
        BE, KH = cv(9, CHUNK), cv(9, CHUNK)
        PL = [[cv(3, CHUNK) for _ in range(7)] for _ in range(3)]
        PZA, WWA = cv(2, TP), cv(2, TP)
        PZ, WW = ([a.rearrange("p a b -> p (a b)")[:, g * 384:(g + 1) * 384].rearrange("p (c n) -> p c n", c=3)
                   for g in range(3)] for a in (PZA, WWA))
        DCOL = cv(9)
        XS = W_RAW[:, 1, 0:2 * P].rearrange("p (a b) -> p a b", a=2)
        bd_words = 27 * 3 * P + 12 * P
        BDALL = cv(bd_words)
        BD = [[BDALL[:, (g * 9 + s) * 3 * P:(g * 9 + s + 1) * 3 * P].rearrange("p (c n) -> p c n", c=3)
               for s in range(9)] for g in range(3)]
        BDS = BDALL[:, 27 * 3 * P:].rearrange("p (c n) -> p c n", c=12)
        Yx = Kx
        cv = carver(KM * T + T)
        YT = cv(KM, T)
        SG = cv(4, T)
        TM = cv(2, T)
        cv = carver(KM * T + T)
        MNT = cv(KM, N_MEM)
        MKV = cv(2, 2 * 512)
        CKT, CVT = cv(2, 512), cv(2, 512)
        MKT = cv(2, X_HEADS, N_MEM)
        QX = cv(X_HEADS, T)
        OX = cv(X_HEADS, T)
        XP, XPT = cv(2, N_MEM), cv(2, 2 * P)
        XST = cv(2, 4)
        cv = carver(KM * T + T)
        GT = cv(KF, T)
        SGF = cv(4, T)
        cv = carver(0)
        otok = cv(5, D_MODEL)

        consts_loaded, x_loaded, x_put_act, x_put_dve, setup_pe, setup_act, memn_stored = (
            sem(n) for n in ("consts_loaded", "x_loaded", "x_put_act", "x_put_dve", "setup_pe", "setup_act", "memn_stored"))
        consts_ready = sem("consts_ready")
        mem_scaled = sem("mem_scaled")
        slot_loaded = [sem(f"slot_loaded{i}") for i in range(RING)]
        slot_used = [sem(f"slot_used{i}") for i in range(RING - 1)]
        tile_done, tile_freed_act, tile_freed_dve = sem("tile_done"), sem("tile_freed_act"), sem("tile_freed_dve")
        bar = sem("phase_ended")
        vec_loaded, vec_turned, vec_ready = sem("vec_loaded"), sem("vec_turned"), sem("vec_ready")
        sq_act, sq_dve, sums_done, rstd_ready, h_ready = (
            sem(n) for n in ("sq_act", "sq_dve", "sums_done", "rstd_ready", "h_ready"))
        est_stored = [sem("est_stored0"), sem("est_stored1")]
        lf_ready, lf_turned, lf_put, lf_stored, dc_ready = (
            sem(n) for n in ("lf_ready", "lf_turned", "lf_put", "lf_stored", "dc_ready"))
        plf_loaded = sem("plf_loaded")
        fx_loaded = [sem("fx_loaded0"), sem("fx_loaded1")]
        fx_stored = [sem("fx_stored0"), sem("fx_stored1")]
        fx_scaled, fx_scores, fx_max, fx_exp, fx_norm, fx_turned, fx_put, fx_out, fx_evac = (
            sem("fx_" + n) for n in ("scaled", "scores", "max", "exp", "norm", "turned", "put", "out", "evac"))
        rope_loaded = sem("rope_loaded")
        df_loaded = [sem("df_loaded0"), sem("df_loaded1")]
        df_stored = [sem("df_stored0"), sem("df_stored1")]
        (df_rot, df_rotated, df_scores, df_max, df_exp, df_comb, df_turned, df_put, df_out, df_sq, df_sum, df_rs,
         df_evac) = (sem("df_" + n) for n in ("rot", "rotated", "scores", "max", "exp", "comb", "turned", "put",
                                             "out", "sq", "sum", "rs", "evac"))
        lo_loaded, lo_mixed, lo_act, lo_done, lo_evac_act, lo_evac_dve, lo_stored = (
            sem("lo_" + n) for n in ("loaded", "mixed", "act", "done", "evac_act", "evac_dve", "stored"))
        (rw_loaded, rw_in, rw_sum, rw_clip, rw_exps, rw_bd, rw_chain, rw_state, rw_final, rw_fin, rw_stored) = (
            sem("rw_" + n) for n in ("loaded", "in", "sum", "clip", "exps", "bd", "chain", "state", "final", "fin",
                                     "stored"))
        rp_y, rp_mean, rp_yc, rp_sq, rp_var, rp_rs, rp_done = (
            sem("rp_" + n) for n in ("y", "mean", "yc", "sq", "var", "rs", "done"))
        rw_mm, rw_ev, rw_eva = ([sem(f"rw_{n}{g}") for g in range(3)] for n in ("mm", "ev", "eva"))
        xa_loaded, xa_stored, xa_scores, xa_max, xa_exp, xa_norm, xa_turned, xa_put, xa_out, xa_evac = (
            sem("xa_" + n) for n in ("loaded", "stored", "scores", "max", "exp", "norm", "turned", "put", "out",
                                     "evac"))
        end_turned, end_put, end_stored, end_put2 = (
            sem("end_" + n) for n in ("turned", "put", "stored", "put2"))
        fx_rows, shift_stored, memn_loaded, lo_w_loaded = (
            sem(n) for n in ("fx_rows", "shift_stored", "memn_loaded", "lo_w_loaded"))
        lam_summed, lf_ready_z, x_updated = sem("lam_summed"), sem("lf_ready_z"), sem("x_updated")
        y_ready, g_ready, x_done = sem("y_ready"), sem("g_ready"), sem("x_done")

        settled = sem("settled")
        NBAR = 10

        def settle(eng):
            eng.sem_inc(settled, 1)

        def phase_end(eng, l, k):
            settle(eng)
            eng.drain().then_inc(bar, 1)
            eng.wait_ge(bar, (l * NBAR + k + 1) * 4)
            settle(eng)

        def half(t, h):
            return t[:, h * HT:(h + 1) * HT]

        def mid(ap, n):
            return ap.rearrange("p (a n) -> p a n", a=1)

        block = ctx.enter_context(nc.Block())

        @block.sync
        def _(sp):
            with sp.Fori(0, DEPTH) as l:
                n = [0]
                last_use = [(tile_done, l * TILES)] * RING

                def slot(name, rows, kn, cols, width, use):
                    pos = n[0] % RING
                    n[0] += 1
                    sp.wait_ge(*last_use[pos])
                    last_use[pos] = use
                    w = A[name][ds(l, 1)] if name != "w_branch" else None
                    if w is None:
                        i, rows = rows
                        src = A[name][ds(l, 1), i:i + 1].rearrange("l i (k p) n -> p (l i k) n", p=P)
                    else:
                        src = w.rearrange("l (k p) n -> p (l k) n", p=P)
                    sp.dma_start(ring[:, pos, 0:kn, 0:width],
                                 src[:, rows:rows + kn, cols:cols + width]).then_inc(slot_loaded[pos], 16)

                def tiles(g):
                    return tile_done, l * TILES + g

                for j in range(19):
                    slot("w_in", 0, 8, 256 * j + (8 if j >= 6 else 0), 256, tiles(G_IN + 2 * j + 2))
                slot("w_in", 0, 8, 1536, 8, tiles(G_IN + 39))
                gates = IN_WIDTH - 3 * D_MODEL
                for j in range(4):
                    for i in range(3):
                        g = G_MERGE + 12 * j + 4 * i
                        slot("w_in", 0, 8, gates + i * D_MODEL + 256 * j, 256, tiles(g + 2))
                        slot("w_branch", (i, 0), 4, 256 * j, 256, tiles(g + 4))
                for j in range(4):
                    slot("w_out", 0, 8, 256 * j, 256, tiles(G_OUT + 2 * j + 2))
                for j in range(4):
                    slot("w_xkv", 0, 8, 256 * j, 256, tiles(G_MEM + 2 * j + 2))
                for j in range(2):
                    slot("w_xq", 0, 8, 256 * j, 256, tiles(G_XQ + 2 * j + 2))
                for j in range(4):
                    slot("w_xo", 0, 4, 256 * j, 256, tiles(G_XO + 2 * j + 2))
                for j in range(11):
                    slot("w_ffn_in", 0, 8, 256 * j, 256, tiles(G_FFI + 4 * j + 2))
                    slot("w_ffn_in", 0, 8, FFN + 256 * j, 256, tiles(G_FFI + 4 * j + 4))
                for j in range(4):
                    k = 0
                    for part, kn in enumerate(FFO_SPLIT):
                        slot("w_ffn_out", k, kn, 256 * j, 256,
                             tiles(G_FFO + 2 * j + 2) if part == 3 else (slot_used[part], l * 4 + j + 1))
                        k += kn
                assert n[0] == SLOTS

        @block.tensor
        def _(pe):
            mm, tr = pe.matmul, pe.transpose
            pe.wait_ge(consts_loaded, 16)
            pe.wait_ge(consts_ready, 1)
            ident = const("ident")

            def setup():
                pe.wait_ge(x_loaded, 48)
                for a in range(KM):
                    if a >= 4:
                        pe.wait_ge(x_put_act, a - 3)
                        pe.wait_ge(x_put_dve, a - 3)
                    q = 2 * (a % 4)
                    for b in range(4):
                        tr(PS[:, q + b // 2, b % 2 * P:(b % 2 + 1) * P], xtok[:, b, a * P:(a + 1) * P], ident)
                    tr(PS[:, q + 1, 2 * P:2 * P + DEC_SEQ], xtok[0:DEC_SEQ, 4, a * P:(a + 1) * P],
                       ident[0:DEC_SEQ, 0:DEC_SEQ]).then_inc(setup_pe, 1)
                pe.wait_ge(mem_scaled, 1)
                for a in range(KM):
                    pe.wait_ge(x_put_act, KM + a - 3)
                    pe.wait_ge(x_put_dve, KM + a - 3)
                    for b in range(2):
                        ins = tr(PS[:, 2 * (a % 4) + b, 0:P], mtok[:, b, a * P:(a + 1) * P], ident)
                    ins.then_inc(setup_pe, 1)

            setup()

            def norm_sums(l, k):
                for h in range(2):
                    for a in range(KM):
                        if h == 0 and a % 2 == 0:
                            pe.wait_ge(sq_act, l * 24 + 4 * k + a // 2 + 1)
                        if h == 0 and a % 2 == 1:
                            pe.wait_ge(sq_dve, l * 24 + 4 * k + a // 2 + 1)
                        ins = mm(half(PS[:, h, :], 0), ones[:, :], half(SQ[:, a, :], h),
                                 start=(a == 0), stop=(a == KM - 1))
                ins.then_inc(sums_done, 1)

            def use_slot(l, n, it=0, per=0):
                pe.wait_ge(slot_loaded[n % RING], 16 * (l * USES + n // RING + 1 + it * (per // RING)))

            def dense(l, g, q, slot, mo, kn, rhs, first=True, last=True, it=0, per=0, width=P, lead=0, used=None):
                if first:
                    pe.wait_ge(tile_freed_act, l * TILES + g + 1 + lead + it * per)
                    pe.wait_ge(tile_freed_dve, l * TILES + g + 1 + lead + it * per)
                for k in range(kn):
                    for h in range(2):
                        ins = mm(PS[0:width, 2 * q + h, 0:HT], ring[:, slot % RING, k, mo * P:mo * P + width],
                                 rhs(k, h), start=(first and k == 0), stop=(last and k == kn - 1))
                if last:
                    ins.then_inc(tile_done, 1)
                elif used:
                    ins.then_inc(slot_used[slot % RING], 1)

            def of_h(k, h):
                return half(hT[:, k, :], h)

            with pe.Fori(0, DEPTH) as l:
                pe.wait_ge(vec_loaded, (l + 1) * 16 * 19)
                tr(PS[:, 7, 0:NVEC], VR[0:NVEC, :], ident[0:NVEC, 0:NVEC]).then_inc(vec_turned, 1)
                norm_sums(l, 0)
                pe.wait_ge(h_ready, l * 24 + 8)
                phase_end(pe, l, 0)

                def in_tiles(l, it, j0, n):
                    for j in range(n):
                        use_slot(l, j0 + j, it, 4)
                        for m in range(2):
                            ins = dense(l, G_IN + 2 * (j0 + j) + m, (2 * j + m) % 4, j0 + j, m, 8, of_h, it=it,
                                        per=8)

                with pe.Fori(0, 4) as it:
                    in_tiles(l, it, 0, 4)
                in_tiles(l, 0, 16, 3)
                use_slot(l, 19)
                dense(l, G_IN + 38, 2, 19, 0, 8, of_h, width=8)
                pe.wait_ge(tile_freed_act, l * TILES + G_IN + 36 + 5)
                pe.wait_ge(tile_freed_dve, l * TILES + G_IN + 36 + 5)
                pe.wait_ge(plf_loaded, 16 * (l + 1))
                for b in range(4):
                    ins = tr(PS[0:8, 0, b * P:(b + 1) * P], PLF[:, b, :], ident)
                ins.then_inc(lf_turned, 1)
                pe.wait_ge(lf_ready, l + 1)
                settle(pe)
                for b in range(4):
                    tr(PS[:, 1, b * 8:(b + 1) * 8], AF[0:8, b * P:(b + 1) * P], ident[0:8, 0:8])
                tr(PS[0:DEC_SEQ, 1, 32:40], AF[0:8, SEQ:T], ident[0:8, 0:8]).then_inc(lf_turned, 1)
                phase_end(pe, l, 1)

                with pe.Fori(0, FOX_HEADS // 2) as it:
                    g = pe.snap(l * 4 + it)
                    job = [0]

                    def put_bank():
                        j = job[0]
                        job[0] += 1
                        pe.wait_ge(fx_put, g * 16 + j + 1)
                        settle(pe)
                        return PS[:, 4 + j % 2, :]

                    def fox_prologue(h):
                        pe.wait_ge(fx_loaded[h], (g + 1) * 16 * 7)
                        b = put_bank()
                        for t in range(5):
                            w = P if t < 4 else DEC_SEQ
                            ins = tr(b[0:w, t * 64:(t + 1) * 64], FVR[0:64, h, t * P:t * P + w], ident[0:64, 0:64])
                        ins.then_inc(fx_turned, 1)
                        b = put_bank()
                        for t in range(5):
                            w = P if t < 4 else DEC_SEQ
                            ins = tr(b[0:w, t * 64:(t + 1) * 64], FK[0:64, h, t * P:t * P + w], ident[0:64, 0:64])
                        ins.then_inc(fx_turned, 1)
                        b = put_bank()
                        for t in range(4):
                            ins = tr(b[0:64, t * P:(t + 1) * P], FPK[:, h, t, :], ident)
                        ins.then_inc(fx_turned, 1)

                    def fox_scores(k):
                        h, i = divmod(k, 5)
                        if i == 0:
                            pe.wait_ge(fx_scaled, g * 2 + h + 1)
                            pe.wait_ge(fx_put, g * 16 + (3, 8)[h] + 2)
                        if k >= 2:
                            pe.wait_ge(fx_exp, g * 10 + k - 1)
                        b = 2 * (k % 2)
                        if i < 4:
                            n = (i + 1) * P
                            q = FQ[0:66, h, i * P:(i + 1) * P]
                            mm(PS[:, b, 0:n], q, FK[0:66, h, 0:n], start=True, stop=False)
                            ins = mm(PS[:, b, n - P:n], identb[:, :], mfoxb[:, :], start=False, stop=True)
                        else:
                            q = FQ[0:66, h, SEQ:T]
                            mm(PS[0:32, b, :], q, FK[0:66, h, T:T + PAST], start=True, stop=True)
                            mm(PS[0:32, b + 1, 0:32], q, FK[0:66, h, SEQ:T], start=True, stop=False)
                            ins = mm(PS[0:32, b + 1, 0:32], identb[0:32, 0:32], mfoxb[0:32, 0:32], start=False,
                                     stop=True)
                        ins.then_inc(fx_scores, 1)

                    def fox_turn(k):
                        i = k % 5
                        pe.wait_ge(fx_norm, g * 10 + k + 1)
                        b = put_bank()
                        if i < 4:
                            for t in range(i + 1):
                                ins = tr(b[:, t * P:(t + 1) * P], FP[:, k % 2, t * P:(t + 1) * P], ident)
                        else:
                            for t in range(5):
                                w = P if t < 4 else DEC_SEQ
                                ins = tr(b[0:w, t * 32:(t + 1) * 32], FP[0:32, k % 2, t * P:t * P + w],
                                         ident[0:32, 0:32])
                        ins.then_inc(fx_turned, 1)

                    jobs_of = []

                    def fox_values(k):
                        h, i = divmod(k, 5)
                        pe.wait_ge(fx_put, g * 16 + jobs_of[k] + 1 + 2)
                        if i == 0:
                            pe.wait_ge(fx_evac, g * 2 + h + 1)
                        o = slice(64 * h, 64 * h + 64)
                        if i < 4:
                            for t in range(i + 1):
                                ins = mm(PS[o, 6, i * P:(i + 1) * P], FVT[:, h, t, :],
                                         FPT[:, k % 2, t * P:(t + 1) * P], start=(t == 0), stop=(t == i))
                        else:
                            for t in range(4):
                                mm(PS[o, 7, 0:32], FVT[:, h, 5 + t, :], FPT[:, k % 2, t * 32:(t + 1) * 32],
                                   start=(t == 0), stop=False)
                            ins = mm(PS[o, 7, 0:32], FVT[0:32, h, 4, :], FPT[0:32, k % 2, 128:160], start=False,
                                     stop=True)
                            ins.then_inc(fx_out, 1)

                    for k in range(12):
                        if k == 0:
                            fox_prologue(0)
                        if k == 3:
                            fox_prologue(1)
                        if k < 10:
                            fox_scores(k)
                        if 1 <= k <= 10:
                            jobs_of.append(job[0])
                            fox_turn(k - 1)
                        if k >= 2:
                            fox_values(k - 2)
                phase_end(pe, l, 2)

                with pe.Fori(0, DIFF_HEADS // 2) as it:
                    g = pe.snap(l * 2 + it)
                    for h in range(2):
                        pe.wait_ge(df_loaded[h], (g + 1) * 16 * 5)
                        for i, src in enumerate((DQ, DK)):
                            if i == 0:
                                pe.wait_ge(df_evac, g * 2 + h + 1)
                            for s in range(2):
                                ins = mm(PS[:, 2 * i + s, 0:HT], const("rot"), half(src[:, h, :], s), start=True,
                                         stop=True)
                            ins.then_inc(df_rot, 1)
                        for t in range(4):
                            ins = tr(PS[:, 4, t * P:(t + 1) * P], DVR[:, h, t * P:(t + 1) * P], ident)
                        ins.then_inc(df_turned, 1)
                        for t in range(4):
                            ins = tr(PS[:, 5, t * P:(t + 1) * P], DPK[:, h, t, :], ident)
                        ins.then_inc(df_turned, 1)
                        pe.wait_ge(df_rotated, g * 4 + 2 * h + 2)
                        pe.wait_ge(df_put, g * 18 + 9 * h + 1)
                        for t in range(4):
                            ins = tr(PS[:, 4, t * P:(t + 1) * P], DK[:, h, t * P:(t + 1) * P], ident)
                        ins.then_inc(df_turned, 1)
                        pe.wait_ge(df_put, g * 18 + 9 * h + 2)
                        tr(PS[0:32, 5, 0:P], DVR[:, h, SEQ:T], ident)
                        tr(PS[0:32, 5, P:2 * P], DK[:, h, SEQ:T], ident).then_inc(df_turned, 1)
                        pe.wait_ge(df_put, g * 18 + 9 * h + 4)

                        def scores(i):
                            if i >= 1:
                                pe.wait_ge(df_exp, g * 20 + 10 * h + 2 * i)
                                settle(pe)
                            for c in range(2):
                                r = slice(64 * c, 64 * c + 64)
                                b = 2 * c
                                if i < 4:
                                    n = (i + 1) * P
                                    mm(PS[:, b, 0:n], DQ[r, h, i * P:(i + 1) * P], DK[r, h, 0:n], start=True,
                                       stop=False)
                                    ins = mm(PS[:, b, n - P:n], identb[:, :], mdiffb[:, :], start=False, stop=True)
                                else:
                                    mm(PS[0:32, b, :], DQ[r, h, SEQ:T], DK[r, h, T:T + PAST], start=True, stop=True)
                                    ins = mm(PS[0:32, b + 1, 0:32], DQ[r, h, SEQ:T], DK[r, h, SEQ:T], start=True,
                                             stop=True)
                                ins.then_inc(df_scores, 1)

                        def turn(i):
                            pe.wait_ge(df_comb, g * 10 + 5 * h + i + 1)
                            pe.wait_ge(df_put, g * 18 + 9 * h + 4 + max(i - 1, 0))
                            settle(pe)
                            b = PS[:, 4 + i % 2, :]
                            if i < 4:
                                for t in range(i + 1):
                                    ins = tr(b[:, t * P:(t + 1) * P], DPB[:, i % 2, 0, t * P:(t + 1) * P], ident)
                            else:
                                for t in range(5):
                                    w = P if t < 4 else DEC_SEQ
                                    ins = tr(b[0:w, t * 32:(t + 1) * 32], DPB[0:32, 0, 0, t * P:t * P + w],
                                             ident[0:32, 0:32])
                            ins.then_inc(df_turned, 1)

                        def values(i):
                            pe.wait_ge(df_put, g * 18 + 9 * h + 4 + i + 1)
                            if i < 4:
                                for t in range(i + 1):
                                    ins = mm(PS[:, 6, i * P:(i + 1) * P], DVT[:, h, t, :],
                                             DPT[:, i % 2, t * P:(t + 1) * P], start=(t == 0), stop=(t == i))
                            else:
                                for t in range(4):
                                    mm(PS[:, 7, 0:32], DVT[:, h, 5 + t, :], DPT[:, 0, t * 32:(t + 1) * 32],
                                       start=(t == 0), stop=False)
                                ins = mm(PS[:, 7, 0:32], DVT[0:32, h, 4, :], DPT[0:32, 0, 128:160], start=False,
                                         stop=True)
                                ins.then_inc(df_out, 1)

                        for k in range(7):
                            if k < 5:
                                scores(k)
                            if 1 <= k <= 5:
                                turn(k - 1)
                            if k >= 2:
                                values(k - 2)
                        pe.wait_ge(df_sq, g * 2 + h + 1)
                        for s in range(2):
                            ins = mm(PS[:, s, 0:HT], ones[:, :], half(DTMP, s), start=True, stop=True)
                        ins.then_inc(df_sum, 1)
                phase_end(pe, l, 3)

                pe.wait_ge(lo_act, l + 1)
                pe.wait_ge(lo_loaded, (l + 1) * 16 * 5)
                pe.wait_ge(lo_w_loaded, (l + 1) * 16)
                for p in range(4):
                    c = slice(p * P, (p + 1) * P)
                    for i, (w, x) in enumerate(((LW2[0:64, c], LXS[0:64, 0, :]), (LW2[64:128, c], LXS[64:128, 0, :]),
                                                (LG2[:, c], LXS[:, 1, :]))):
                        j = 3 * p + i
                        if j >= 4:
                            pe.wait_ge(lo_evac_act, l * 12 + j - 3)
                        for s in range(2):
                            ins = mm(PS[:, 2 * (j % 4) + s, 0:HT], w, half(x, s), start=True, stop=True)
                        ins.then_inc(lo_done, 1)
                phase_end(pe, l, 4)

                with pe.Fori(0, RWKV_HEADS // 2) as it:
                    g = pe.snap(l * 4 + it)
                    hp = TP // 2

                    def sums(src):
                        for s in range(2):
                            ins = mm(PS[:, 6 + s, 0:hp], const("bdones"), src[:, s * hp:(s + 1) * hp], start=True,
                                     stop=True)
                        return ins

                    pe.wait_ge(rw_in, g * 2 + 1)
                    sums(W_RAW[:, 0, :]).then_inc(rw_sum, 1)
                    pe.wait_ge(rw_in, g * 2 + 2)
                    sums(W_RAW[:, 2, :]).then_inc(rw_sum, 1)

                    def three(gr, bank, at, step, pairs):
                        for c in range(3):
                            for n, (w, x) in enumerate(pairs):
                                x_c = x(c)
                                ins = mm(PS[:, bank, at + step * c:at + step * c + x_c.shape[-1]], w(c), x_c,
                                         start=(n == 0), stop=(n == len(pairs) - 1))
                        return ins

                    def stage(s, gr):
                        bd = lambda i: (lambda c: BD[gr][i][:, c, :])
                        pl = lambda i: (lambda c: PL[gr][i][:, c, :])
                        X1, X2, Ao, GTt, HTt, Vt, Bt = range(7)
                        rt = X2
                        b0, b1 = 2 * gr, 2 * gr + 1
                        ch = lambda c: 3 * gr + c
                        pe.wait_ge(rw_ev[gr], g * 12 + s)
                        pe.wait_ge(rw_eva[gr], g * 12 + s)
                        if s == 1:
                            pe.wait_ge(rw_bd, g * 3 + gr + 1)
                            three(gr, b0, 0, 128, [(bd(0), lambda c: KR[:, ch(c), :])])
                            ins = three(gr, b1, 0, 128, [(bd(1), lambda c: KR[:, ch(c), :])])
                        st = lambda c: const("stack")[:, 0:64]
                        if s == 2:
                            three(gr, b0, 0, 64, [(bd(2), lambda c: BE[:, ch(c), :])])
                            three(gr, b0, 192, 64, [(bd(3), st)])
                            three(gr, b1, 0, 64, [(bd(2), st)])
                            ins = three(gr, b1, 192, 64, [(bd(0), st)])
                        if s == 3:
                            three(gr, b0, 0, 64, [(bd(5), pl(Vt))])
                            three(gr, b0, 192, 64, [(bd(1), st)])
                            three(gr, b1, 0, 64, [(bd(3), pl(X1))])
                            ins = three(gr, b1, 192, 64, [(bd(0), pl(X2))])
                        if s == 4:
                            three(gr, b0, 0, 128, [(bd(3), lambda c: PZ[gr][:, c, :])])
                            ins = three(gr, b1, 0, 64, [(bd(2), pl(X2))])
                        if s == 5:
                            three(gr, b0, 0, 64, [(bd(1), lambda c: PZ[gr][:, c, 64:128])])
                            ins = three(gr, b1, 0, 64, [(bd(0), pl(X2))])
                        if s == 6:
                            ins = three(gr, b0, 0, 64, [(bd(2), lambda c: PZ[gr][:, c, 64:128])])
                        if s == 7:
                            three(gr, b0, 0, 64, [(bd(4), lambda c: PZ[gr][:, c, 64:128])])
                            three(gr, b0, 192, 64, [(bd(0), pl(Ao))])
                            ins = three(gr, b1, 0, 128, [(bd(0), lambda c: WW[gr][:, c, :])])
                        if s == 8:
                            three(gr, b0, 0, 64, [(bd(2), pl(X1))])
                            ins = three(gr, b1, 0, 128, [(bd(1), lambda c: WW[gr][:, c, :])])
                        if s == 9:
                            ins = three(gr, b1, 0, 128, [(bd(3), lambda c: WW[gr][:, c, :])])
                        if s == 10:
                            three(gr, b0, 0, 64, [(bd(0), pl(GTt))])
                            ins = three(gr, b0, 192, 64, [(bd(0), pl(Bt))])
                        if s == 11:
                            ins = three(gr, b1, 0, 64, [(bd(1), pl(GTt)), (bd(7), pl(HTt)),
                                                        (lambda c: BDS[:, ch(c), :], pl(rt))])
                        ins.then_inc(rw_mm[gr], 1)

                    for s in range(1, 11):
                        for gr in range(3):
                            stage(s, gr)
                    tr(PS[:, 7, 256:384], BDS[:, 11, :], ident).then_inc(rw_state, 1)
                    for c in range(9):
                        gr, cc = divmod(c, 3)
                        if cc == 0:
                            pe.wait_ge(rw_ev[gr], g * 12 + 11)
                            pe.wait_ge(rw_eva[gr], g * 12 + 11)
                        if c >= 1:
                            pe.wait_ge(rw_chain, g * 10 + c)
                        o = PS[:, 6 + c % 2, 0:P]
                        mm(o, BD[gr][6][:, cc, :], BD[gr][1][:, cc, :], start=True, stop=False)
                        mm(o, BD[gr][8][:, cc, :], BD[gr][7][:, cc, :], start=False, stop=False)
                        if 1 <= c < 8:
                            pe.wait_ge(rw_chain, g * 10 + c + 1)
                        mm(o, BD[gr][2][:, cc, :], BDS[:, c, :], start=False, stop=True).then_inc(rw_state, 1)
                    for gr in range(3):
                        stage(11, gr)
                    pe.wait_ge(rw_chain, g * 10 + 10)
                    tr(PS[:, 7, 0:P], BDS[:, 9, :], ident)
                    tr(PS[:, 7, P:2 * P], BDS[:, 10, :], ident).then_inc(rw_final, 1)
                    pe.wait_ge(rw_fin, g + 1)
                    pe.wait_ge(rp_y, g + 1)
                    sums(Yx).then_inc(rp_mean, 1)
                    pe.wait_ge(rp_sq, g + 1)
                    sums(W_RAW[:, 0, :]).then_inc(rp_var, 1)
                    pe.wait_ge(rp_done, g + 1)
                phase_end(pe, l, 5)

                with pe.Fori(0, 2) as it:
                    for s in range(12):
                        use_slot(l, S_IN + s, it, 12)
                        i = s % 6 // 2
                        for m in range(2):
                            n = 2 * s + m
                            if s % 2 == 0:
                                dense(l, G_MERGE + n, n % 4, s, m, 8, of_h, it=it, per=24)
                            else:
                                dense(l, G_MERGE + n, n % 4, s, m, 4,
                                      lambda k, h: half(brT[:, 4 * i + k, :], h), it=it, per=24)
                pe.wait_ge(y_ready, l + 1)
                for s in range(4):
                    use_slot(l, S_IN + S_MERGE + s)
                    for m in range(2):
                        n = 2 * s + m
                        dense(l, G_OUT + n, n % 4, s, m, 8, lambda k, h: half(YT[:, k, :], h))
                phase_end(pe, l, 6)
                norm_sums(l, 1)
                pe.wait_ge(rstd_ready, l * 6 + 2)
                norm_sums(l, 2)

                base = S_IN + S_MERGE + S_OUT
                pe.wait_ge(mem_scaled, l + 2)
                pe.wait_ge(h_ready, l * 24 + 16)
                for s in range(4):
                    use_slot(l, base + s)
                    for t in range(2):
                        n = 2 * s + t
                        q = n % 4
                        pe.wait_ge(tile_freed_act, l * TILES + G_MEM + n + 1)
                        pe.wait_ge(tile_freed_dve, l * TILES + G_MEM + n + 1)
                        for k in range(8):
                            ins = mm(PS[:, 2 * q, 0:256], MNT[:, k, t * P:(t + 1) * P], ring[:, s, k, :],
                                     start=(k == 0), stop=(k == 7))
                        ins.then_inc(tile_done, 1)
                for s in range(2):
                    use_slot(l, base + 4 + s)
                    for m in range(2):
                        n = 2 * s + m
                        dense(l, G_XQ + n, n % 4, base + 4 + s, m, 8, of_h)
                phase_end(pe, l, 7)
                pe.wait_ge(xa_loaded, (l + 1) * 32)
                for j in range(8):
                    grp, h = divmod(j, 4)
                    if j >= 2:
                        pe.wait_ge(xa_put, l * 28 + j - 1)
                    for t in range(2):
                        src = MKV[:, t, h * P:(h + 1) * P] if grp == 0 else CKT[:, t, h * P:(h + 1) * P]
                        ins = tr(PS[:, 4 + j % 2, t * P:(t + 1) * P], src, ident)
                    ins.then_inc(xa_turned, 1)
                pe.wait_ge(xa_put, l * 28 + 8)

                def x_scores(k):
                    h, i = divmod(k, 5)
                    if k >= 2:
                        pe.wait_ge(xa_exp, l * 20 + k - 1)
                    b, m = 2 * (k % 2), (P if i < 4 else DEC_SEQ)
                    mm(PS[0:m, b, 0:N_MEM], QX[:, h, i * P:i * P + m], MKT[:, i // 4, h, :], start=True,
                       stop=True).then_inc(xa_scores, 1)

                def x_turn(k):
                    pe.wait_ge(xa_norm, l * 20 + k + 1)
                    pe.wait_ge(xa_put, l * 28 + 8 + max(k - 1, 0))
                    settle(pe)
                    m = P if k % 5 < 4 else DEC_SEQ
                    for t in range(2):
                        ins = tr(PS[:, 4 + k % 2, t * P:t * P + m], XP[0:m, k % 2, t * P:(t + 1) * P],
                                 ident[0:m, 0:m])
                    ins.then_inc(xa_turned, 1)

                def x_values(k):
                    h, i = divmod(k, 5)
                    pe.wait_ge(xa_put, l * 28 + 8 + k + 1)
                    if i == 0 and h >= 1:
                        pe.wait_ge(xa_evac, l * 4 + h)
                    m = P if i < 4 else DEC_SEQ
                    for t in range(2):
                        v = MKV[:, t, 512 + h * P:512 + (h + 1) * P] if i < 4 else CVT[:, t, h * P:(h + 1) * P]
                        ins = mm(PS[:, 6 + i // 4, (i % 4) * P:(i % 4) * P + m], v, XPT[:, k % 2, t * P:t * P + m],
                                 start=(t == 0), stop=(t == 1))
                    if i == 4:
                        ins.then_inc(xa_out, 1)

                for k in range(22):
                    if k < 20:
                        x_scores(k)
                    if 1 <= k <= 20:
                        x_turn(k - 1)
                    if k >= 2:
                        x_values(k - 2)
                pe.wait_ge(xa_evac, l * 4 + 4)
                for s in range(4):
                    use_slot(l, base + 6 + s)
                    for m in range(2):
                        n = 2 * s + m
                        dense(l, G_XO + n, n % 4, base + 6 + s, m, 4, lambda k, h: half(OX[:, k, :], h))
                phase_end(pe, l, 8)
                norm_sums(l, 3)
                pe.wait_ge(rstd_ready, l * 6 + 4)
                norm_sums(l, 4)

                base = base + 10
                pe.wait_ge(h_ready, l * 24 + 24)
                settle(pe)

                def ffn_in(it, s0, n_slots):
                    for s in range(s0, s0 + n_slots):
                        use_slot(l, base + s, it, 4)
                        for m in range(2):
                            n = 2 * s + m
                            dense(l, G_FFI + n, n % 4, base + s, m, 8, of_h, it=it, per=8)

                with pe.Fori(0, 5) as it:
                    ffn_in(it, 0, 4)
                ffn_in(0, 20, 2)
                base = base + S_FFI
                pe.wait_ge(g_ready, l + 1)
                settle(pe)
                with pe.Fori(0, 4) as it:
                    k0 = 0
                    for part, kn in enumerate(FFO_SPLIT):
                        use_slot(l, base + part, it, 4)
                        for m in range(2):
                            dense(l, G_FFO + m, m, base + part, m, kn,
                                  lambda k, h, k0=k0: half(GT[:, k0 + k, :], h), first=(part == 0),
                                  last=(part == 3), it=it, per=2, lead=2,
                                  used=(m == 1 and part < 3))
                        k0 += kn
                phase_end(pe, l, 9)
                norm_sums(l, 5)
                pe.wait_ge(x_done, l + 1)
                settle(pe)

            for b in range(5):
                w = P if b < 4 else DEC_SEQ
                for c in range(2):
                    j = 2 * b + c
                    if j >= 4:
                        pe.wait_ge(end_put, j - 3)
                    for a in range(4):
                        ins = tr(PS[0:w, j % 4, a * P:(a + 1) * P], xT[:, 4 * c + a, b * P:b * P + w], ident)
                    ins.then_inc(end_turned, 1)

        @block.scalar
        def _(act):
            def f(out, in_, func, **kw):
                return act.activation(out, in_, func, **kw)

            def copy(out, in_):
                return act.copy(out, in_)

            act.sem_inc(tile_freed_act, 4)
            act.sem_inc(fx_put, 2)
            act.wait_ge(consts_ready, 1)
            act.wait_ge(x_loaded, 48)
            for t in range(2):
                f(SQ[:, 2 * t, :], mtok[:, t, 0:T], ACT.Square,
                  accum_out=small[:, 2 * t:2 * t + 1])
                f(SQ[:, 2 * t + 1, 0:D_MODEL - T], mtok[:, t, T:D_MODEL], ACT.Square,
                  accum_out=small[:, 2 * t + 1:2 * t + 2])
            act.drain().then_inc(setup_act, 1)
            act.wait_ge(setup_act, 2)
            f(small[:, 6:8], small[:, 4:6], ACT.Ln, scale=1.0 / D_MODEL, bias=eps[:, 0:1])
            act.drain()
            f(small[:, 8:10], small[:, 6:8], ACT.Exp, scale=-0.5)
            act.drain().then_inc(setup_act, 1)
            for a in range(KM):
                act.wait_ge(setup_pe, a + 1)
                copy(xT[:, a, 0:2 * P], PS[:, 2 * (a % 4), 0:2 * P]).then_inc(x_put_act, 1)
            for a in range(KM):
                act.wait_ge(setup_pe, KM + a + 1)
                copy(mnT[:, a, 0:P], PS[:, 2 * (a % 4), 0:P]).then_inc(x_put_act, 1)

            def norm_squares(l, k, src):
                for a in range(0, KM, 2):
                    f(SQ[:, a, :], src[:, a, :], ACT.Square).then_inc(sq_act, 1)

            def norm_rstd(l, k):
                act.wait_ge(sums_done, l * 6 + k + 1)
                for h in range(2):
                    f(half(RS, h), PS[:, h, 0:HT], ACT.Ln, scale=1.0 / D_MODEL, bias=eps[:, 0:1])
                act.drain()
                f(RS, RS, ACT.Exp, scale=-0.5)
                act.drain().then_inc(rstd_ready, 1)

            def tile(l, g, it=0, per=0):
                act.wait_ge(tile_done, l * TILES + g + 1 + it * per)

            with act.Fori(0, DEPTH) as l:
                act.wait_ge(vec_turned, l + 1)
                copy(VT[:, 0:NVEC], PS[:, 7, 0:NVEC])
                act.wait_ge(lam_summed, l + 1)
                f(small[:, 14:16], small[:, 12:14], ACT.Exp)
                act.drain().then_inc(vec_ready, 1)
                norm_squares(l, 0, xT)
                norm_rstd(l, 0)
                phase_end(act, l, 0)
                def in_tiles(it, j0, n):
                    for j in range(n):
                        s = j % 2
                        act.wait_ge(est_stored[s], 16 * (l * (10 - s) + (j0 + j) // 2 + it * 2))
                        for m in range(2):
                            n_ = 2 * (j0 + j) + m
                            tile(l, G_IN + n_, it, 8)
                            copy(half(EST[:, s, m, :], 0), PS[:, 2 * ((2 * j + m) % 4), 0:HT]) \
                                .then_inc(tile_freed_act, 1)

                with act.Fori(0, 4) as it:
                    in_tiles(it, 0, 4)
                in_tiles(0, 16, 3)
                act.wait_ge(lf_ready_z, l + 1)
                f(TZ[0:8, 1, :], TZ[0:8, 0, :], ACT.Abs)
                act.drain()
                f(TZ[0:8, 1, :], TZ[0:8, 1, :], ACT.Exp, scale=-1.0)
                act.drain()
                f(TZ[0:8, 1, :], TZ[0:8, 1, :], ACT.Ln, bias=1.0)
                act.drain().then_inc(tile_freed_act, 1)
                act.wait_ge(lf_turned, 2 * l + 2)
                copy(LFT[:, 0:4, :].rearrange("p a b -> p (a b)"), PS[:, 1, 0:32])
                copy(LFT[0:DEC_SEQ, 4, :], PS[0:DEC_SEQ, 1, 32:40])
                act.drain().then_inc(lf_put, 1)
                phase_end(act, l, 1)

                with act.Fori(0, FOX_HEADS // 2) as it:
                    g = act.snap(l * 4 + it)
                    job = [0]

                    def next_job():
                        j = job[0]
                        job[0] += 1
                        act.wait_ge(fx_turned, g * 16 + j + 1)
                        return PS[:, 4 + j % 2, :]

                    def fox_prologue(h):
                        for to in (FVT, FKT):
                            b = next_job()
                            copy(to[:, h, 0:4, :].rearrange("p a b -> p (a b)"), b[:, 0:256])
                            copy(to[0:DEC_SEQ, h, 4, :], b[0:DEC_SEQ, 256:320])
                            act.drain().then_inc(fx_put, 1)
                        b = next_job()
                        copy(FK[0:64, h, T:T + PAST], b[0:64, :]).then_inc(fx_put, 1)

                    def fox_exp(k):
                        i = k % 5
                        act.wait_ge(fx_max, g * 10 + k + 1)
                        m, n = (P, (i + 1) * P) if i < 4 else (DEC_SEQ, T)
                        f(FP[0:m, k % 2, 0:n], pair(k % 2)[0:m, 0:n], ACT.Exp, bias=FST[0:m, k % 2, 0:1],
                          accum_out=FST[0:m, k % 2, 1:2])
                        act.drain().then_inc(fx_exp, 1)

                    def fox_put(k):
                        i = k % 5
                        b = next_job()
                        if i < 4:
                            copy(FPT[:, k % 2, 0:(i + 1) * P], b[:, 0:(i + 1) * P]).then_inc(fx_put, 1)
                        else:
                            copy(FPT[:, k % 2, 0:P], b[:, 0:P])
                            copy(FPT[0:32, k % 2, P:P + 32], b[0:32, P:P + 32])
                            act.drain().then_inc(fx_put, 1)

                    for k in range(11):
                        if k == 0:
                            fox_prologue(0)
                        if k == 3:
                            fox_prologue(1)
                        if k < 10:
                            fox_exp(k)
                        if k >= 1:
                            fox_put(k - 1)
                phase_end(act, l, 2)

                with act.Fori(0, DIFF_HEADS // 2) as it:
                    g = act.snap(l * 2 + it)
                    for h in range(2):
                        act.wait_ge(df_turned, g * 18 + 9 * h + 1)
                        copy(DVT[:, h, 0:4, :].rearrange("p a b -> p (a b)"), PS[:, 4, :]).then_inc(df_put, 1)
                        act.wait_ge(df_turned, g * 18 + 9 * h + 2)
                        copy(DK[:, h, T:T + PAST], PS[:, 5, :]).then_inc(df_put, 1)
                        act.wait_ge(df_turned, g * 18 + 9 * h + 3)
                        copy(DKT[:, h, 0:4, :].rearrange("p a b -> p (a b)"), PS[:, 4, :]).then_inc(df_put, 1)
                        act.wait_ge(df_turned, g * 18 + 9 * h + 4)
                        copy(DVT[0:32, h, 4, :], PS[0:32, 5, 0:P])
                        copy(DKT[0:32, h, 4, :], PS[0:32, 5, P:2 * P])
                        act.drain().then_inc(df_put, 1)
                        for k in range(6):
                            if k < 5:
                                m, n = (P, (k + 1) * P) if k < 4 else (DEC_SEQ, T)
                                for c in range(2):
                                    act.wait_ge(df_max, g * 20 + 10 * h + 2 * k + c + 1)
                                    f(DPB[0:m, k % 2, c, 0:n], pair(c)[0:m, 0:n], ACT.Exp,
                                      bias=DST[0:m, k % 2, c:c + 1], accum_out=DST[0:m, k % 2, 2 + c:3 + c])
                                    act.drain().then_inc(df_exp, 1)
                            if k >= 1:
                                i = k - 1
                                act.wait_ge(df_turned, g * 18 + 9 * h + 4 + k)
                                b = PS[:, 4 + i % 2, :]
                                if i < 4:
                                    copy(DPT[:, i % 2, 0:(i + 1) * P], b[:, 0:(i + 1) * P]).then_inc(df_put, 1)
                                else:
                                    copy(DPT[:, 0, 0:P], b[:, 0:P])
                                    copy(DPT[0:32, 0, P:P + 32], b[0:32, P:P + 32])
                                    act.drain().then_inc(df_put, 1)
                        act.wait_ge(df_out, g * 2 + h + 1)
                        f(DTMP, pair(3)[:, 0:T], ACT.Square).then_inc(df_sq, 1)
                        act.wait_ge(df_sum, g * 2 + h + 1)
                        for s in range(2):
                            f(half(DRS, s), PS[:, s, 0:HT], ACT.Ln, scale=1.0 / P, bias=eps[:, 0:1])
                        act.drain()
                        f(DRS, DRS, ACT.Exp, scale=-0.5)
                        act.drain().then_inc(df_rs, 1)
                phase_end(act, l, 3)

                act.wait_ge(lo_mixed, l + 1)
                f(LXS[0:64, 0, :], LXS[0:64, 0, :], ACT.Tanh)
                f(LXS[:, 1, :], LXS[:, 1, :], ACT.Sigmoid)
                act.drain().then_inc(lo_act, 1)
                for p in range(4):
                    for i in range(3):
                        j = 3 * p + i
                        act.wait_ge(lo_done, l * 12 + j + 1)
                        for s in range(2):
                            src, to = PS[:, 2 * (j % 4) + s, 0:HT], half(LO[:, 4 * i + p, :], s)
                            if i == 0:
                                f(to, src, ACT.Sigmoid, bias=vec("rwkv_w0", p))
                            elif i == 1:
                                f(to, src, ACT.Sigmoid, bias=vec("rwkv_a0", p))
                            else:
                                copy(to, src)
                        act.drain().then_inc(lo_evac_act, 1)
                phase_end(act, l, 4)

                with act.Fori(0, RWKV_HEADS // 2) as it:
                    g = act.snap(l * 4 + it)
                    KX = W_RAW[:, 0, :]
                    act.wait_ge(rw_clip, g * 2 + 1)
                    f(KX, KX, ACT.Ln)
                    act.drain()
                    f(KX, KX, ACT.Exp, scale=-0.5, bias=eps[:, 2:3])
                    act.wait_ge(rw_clip, g * 2 + 2)
                    f(WWA[:, 0, :], PZA[:, 0, :], ACT.Exp)
                    f(WWA[:, 1, :], PZA[:, 0, :], ACT.Exp, scale=-1.0)
                    f(PZA[:, 1, :], PZA[:, 1, :], ACT.Exp)
                    act.drain().then_inc(rw_exps, 1)

                    def bd(gr, slot, src):
                        copy(BD[gr][slot][0:64, :, 0:64], src[0:64])
                        copy(BD[gr][slot][64:128, :, 64:128], src[64:128])

                    def evac(s, gr):
                        X1, X2, Ao, GTt, HTt, Vt, Bt = range(7)
                        rt = X2

                        def bank(i, at):
                            return PS[:, 2 * gr + i, at:at + 192].rearrange("p (c n) -> p c n", c=3)

                        act.wait_ge(rw_mm[gr], g * 11 + s)
                        act.wait_ge(rw_ev[gr], g * 12 + s + 1)
                        if s in (1, 6, 10):
                            act.sem_inc(rw_eva[gr], 1)
                            return
                        if s == 2:
                            bd(gr, 6, bank(1, 192))
                            bd(gr, 7, bank(0, 192))
                            bd(gr, 0, PL[gr][X1])
                        if s == 3:
                            bd(gr, 8, bank(0, 192))
                            bd(gr, 2, bank(1, 0))
                            bd(gr, 3, bank(1, 192))
                            bd(gr, 4, PL[gr][Ao])
                        if s == 4:
                            bd(gr, 0, PS[:, 2 * gr, 0:384].rearrange("p (c n) -> p c n", c=3)[:, :, 0:64])
                            bd(gr, 1, bank(1, 0))
                        if s == 5:
                            bd(gr, 2, bank(1, 0))
                        if s == 7:
                            bd(gr, 1, bank(0, 0))
                            bd(gr, 2, bank(0, 192))
                        if s == 8:
                            bd(gr, 3, bank(0, 0))
                        if s == 9:
                            bd(gr, 0, WW[gr][:, :, 0:64])
                            bd(gr, 1, WW[gr][:, :, 64:128])
                        act.drain().then_inc(rw_eva[gr], 1)

                    for gr in range(3):
                        act.wait_ge(rw_ev[gr], g * 12 + 1)
                        bd(gr, 0, BE[:, 3 * gr:3 * gr + 3, :])
                        bd(gr, 1, KH[:, 3 * gr:3 * gr + 3, :])
                        act.drain().then_inc(rw_eva[gr], 1)
                    for s in range(1, 11):
                        for gr in range(3):
                            evac(s, gr)
                    for gr in range(3):
                        act.sem_inc(rw_eva[gr], 1)
                    act.wait_ge(rw_final, g + 1)
                    copy(XS.rearrange("p a b -> p (a b)"), PS[:, 7, 0:2 * P])
                    act.drain().then_inc(rw_fin, 1)
                    act.wait_ge(rp_yc, g + 1)
                    f(W_RAW[:, 0, :], Yx, ACT.Square).then_inc(rp_sq, 1)
                    act.wait_ge(rp_var, g + 1)
                    for s in range(2):
                        f(W_RAW[:, 0, s * (TP // 2):(s + 1) * (TP // 2)], PS[:, 6 + s, 0:TP // 2], ACT.Ln,
                          scale=1.0 / HEAD_DIM, bias=eps[:, 1:2])
                    act.drain()
                    f(W_RAW[:, 0, :], W_RAW[:, 0, :], ACT.Exp, scale=-0.5)
                    act.drain().then_inc(rp_rs, 1)
                phase_end(act, l, 5)

                with act.Fori(0, 2) as it:
                    for s in range(0, 12, 2):
                        for m in range(2):
                            n = 2 * s + m
                            tile(l, G_MERGE + n, it, 24)
                            for h in range(2):
                                ins = f(half(SG[:, (s + m) % 4, :], h), PS[:, 2 * (n % 4) + h, 0:HT], ACT.Sigmoid)
                            act.drain().then_inc(tile_freed_act, 1 if m == 0 else 3)
                for n in range(N_OUT):
                    tile(l, G_OUT + n)
                    copy(half(hT[:, n, :], 0), PS[:, 2 * (n % 4), 0:HT]).then_inc(tile_freed_act, 1)
                phase_end(act, l, 6)
                norm_squares(l, 1, hT)
                norm_rstd(l, 1)
                act.wait_ge(x_updated, l * 3 + 1)
                norm_squares(l, 2, xT)
                norm_rstd(l, 2)

                for n in range(N_MEMKV):
                    s, t = divmod(n, 2)
                    tile(l, G_MEM + n)
                    copy(MKV[:, t, 256 * s:256 * s + 256], PS[:, 2 * (n % 4), 0:256]).then_inc(tile_freed_act, 1)
                for n in range(N_XQ):
                    tile(l, G_XQ + n)
                    f(half(QX[:, n, :], 0), PS[:, 2 * (n % 4), 0:HT], ACT.Copy, scale=X_DIM ** -0.5) \
                        .then_inc(tile_freed_act, 1)
                phase_end(act, l, 7)
                for j in range(8):
                    act.wait_ge(xa_turned, l * 28 + j + 1)
                    copy(MKT[:, j // 4, j % 4, :], PS[:, 4 + j % 2, 0:N_MEM]).then_inc(xa_put, 1)
                for k in range(21):
                    if k < 20:
                        m = P if k % 5 < 4 else DEC_SEQ
                        act.wait_ge(xa_max, l * 20 + k + 1)
                        f(XP[0:m, k % 2, :], PS[0:m, 2 * (k % 2), 0:N_MEM], ACT.Exp, bias=XST[0:m, k % 2, 0:1],
                          accum_out=XST[0:m, k % 2, 1:2])
                        act.drain().then_inc(xa_exp, 1)
                    if k >= 1:
                        m = P if (k - 1) % 5 < 4 else DEC_SEQ
                        act.wait_ge(xa_turned, l * 28 + 8 + k)
                        b = PS[:, 4 + (k - 1) % 2, 0:2 * P].rearrange("p (t n) -> p t n", t=2)[:, :, 0:m]
                        copy(XPT[:, (k - 1) % 2, :].rearrange("p (t n) -> p t n", t=2)[:, :, 0:m], b) \
                            .then_inc(xa_put, 1)
                for n in range(N_XO):
                    tile(l, G_XO + n)
                    copy(half(hT[:, n, :], 0), PS[:, 2 * (n % 4), 0:HT]).then_inc(tile_freed_act, 1)
                phase_end(act, l, 8)
                norm_squares(l, 3, hT)
                norm_rstd(l, 3)
                act.wait_ge(x_updated, l * 3 + 2)
                norm_squares(l, 4, xT)
                norm_rstd(l, 4)

                def sigmoids(it, s0, n_slots):
                    for s in range(s0, s0 + n_slots, 2):
                        for m in range(2):
                            n = 2 * s + m
                            tile(l, G_FFI + n, it, 8)
                            for h in range(2):
                                f(half(SGF[:, (s + m) % 4, :], h), PS[:, 2 * (n % 4) + h, 0:HT], ACT.Sigmoid)
                            act.drain().then_inc(tile_freed_act, 1 if m == 0 else 3)

                with act.Fori(0, 5) as it:
                    sigmoids(it, 0, 4)
                sigmoids(0, 20, 2)
                with act.Fori(0, 4) as it:
                    for m in range(2):
                        tile(l, G_FFO + m, it, 2)
                        copy(hT[:, ds(it * 2 + m, 1), 0:HT], mid(PS[:, 2 * m, 0:HT], HT)).then_inc(tile_freed_act, 1)
                phase_end(act, l, 9)
                norm_squares(l, 5, hT)
                norm_rstd(l, 5)
                act.wait_ge(x_updated, l * 3 + 3)

            for b in range(5):
                w = P if b < 4 else DEC_SEQ
                for c in range(2):
                    j = 2 * b + c
                    act.wait_ge(end_turned, j + 1)
                    copy(otok[0:w, b, c * 512:(c + 1) * 512], PS[0:w, j % 4, :])
                    act.drain().then_inc(end_put, 1)

        @block.vector
        def _(dve):
            tt, ts, stt, copy = dve.tensor_tensor, dve.tensor_scalar, dve.scalar_tensor_tensor, dve.tensor_copy

            dve.memset(ones[:, :], 1.0)
            dve.memset(eps[:, 0:1], RMS_EPS)
            dve.memset(eps[:, 1:2], GN_EPS)
            dve.memset(eps[:, 2:3], 10.0 * math.log(2.0))
            dve.sem_inc(tile_freed_dve, 4)
            dve.sem_inc(fx_evac, 2)
            dve.sem_inc(df_evac, 1)
            dve.wait_ge(consts_loaded, 16)
            copy(identb[:, :], const("ident"))
            copy(mfoxb[:, :], const("mfox"))
            copy(mdiffb[:, :], const("mdiff"))
            dve.drain().then_inc(consts_ready, 1)
            dve.wait_ge(setup_act, 1)
            sm = small[:, 0:4].rearrange("p (t h) -> p t h", t=2)
            tt(small[:, 4:6], sm[:, :, 0], sm[:, :, 1], ALU.add)
            dve.drain().then_inc(setup_act, 1)
            dve.wait_ge(setup_act, 3)
            for t in range(2):
                ts(mtok[:, t, :], mtok[:, t, :], small[:, 8 + t:9 + t], None, ALU.mult)
            dve.drain().then_inc(mem_scaled, 1)
            for a in range(KM):
                dve.wait_ge(setup_pe, a + 1)
                copy(xT[:, a, 2 * P:T], PS[:, 2 * (a % 4) + 1, 0:T - 2 * P]).then_inc(x_put_dve, 1)
            for a in range(KM):
                dve.wait_ge(setup_pe, KM + a + 1)
                copy(mnT[:, a, P:2 * P], PS[:, 2 * (a % 4) + 1, 0:P]).then_inc(x_put_dve, 1)

            def norm_squares(l, k, src):
                for a in range(1, KM, 2):
                    tt(SQ[:, a, :], src[:, a, :], src[:, a, :], ALU.mult).then_inc(sq_dve, 1)

            def prenorm(l, k, gain):
                dve.wait_ge(rstd_ready, l * 6 + k + 1)
                for a in range(KM):
                    stt(hT[:, a, :], xT[:, a, :], vec(gain, a), RS, ALU.mult, ALU.mult).then_inc(h_ready, 1)

            def postnorm(l, k, gain):
                dve.wait_ge(rstd_ready, l * 6 + k + 1)
                for a in range(KM):
                    stt(hT[:, a, :], hT[:, a, :], vec(gain, a), RS, ALU.mult, ALU.mult)
                dve.drain()
                for a in range(KM):
                    tt(xT[:, a, :], xT[:, a, :], hT[:, a, :], ALU.add)
                dve.drain().then_inc(x_updated, 1)

            def tile(l, g, it=0, per=0):
                dve.wait_ge(tile_done, l * TILES + g + 1 + it * per)

            with dve.Fori(0, DEPTH) as l:
                dve.wait_ge(vec_loaded, (l + 1) * 16 * 19)
                tt(lamp[:, :, :], lam4[:, 0:4:2, :], lam4[:, 1:4:2, :], ALU.mult)
                dve.drain()
                dve.tensor_reduce(small[:, 12:14], lamp[:, :, :], AX.X, ALU.add)
                dve.drain().then_inc(lam_summed, 1)
                dve.wait_ge(vec_ready, l + 1)
                c0 = _c["lam"][0]
                tt(small[:, 16:17], small[:, 15:16], small[:, 14:15], ALU.subtract)
                dve.drain()
                tt(small[:, 16:17], small[:, 16:17], CB[:, ds(l + c0, 1)], ALU.subtract)
                tt(small[:, 17:18], vec("diff_subln", 0), CB[:, ds(l + (c0 + 2), 1)], ALU.mult)
                dve.drain()
                norm_squares(l, 0, xT)
                prenorm(l, 0, "norm_mix_pre")
                phase_end(dve, l, 0)

                def in_tiles(it, j0, n):
                    for j in range(n):
                        s = j % 2
                        dve.wait_ge(est_stored[s], 16 * (l * (10 - s) + (j0 + j) // 2 + it * 2))
                        for m in range(2):
                            n_ = 2 * (j0 + j) + m
                            tile(l, G_IN + n_, it, 8)
                            copy(half(EST[:, s, m, :], 1), PS[:, 2 * ((2 * j + m) % 4) + 1, 0:HT]) \
                                .then_inc(tile_freed_dve, 1)

                with dve.Fori(0, 4) as it:
                    in_tiles(it, 0, 4)
                in_tiles(0, 16, 3)
                dve.memset(ONES, 1.0)
                tile(l, G_IN + 38)
                for h in range(2):
                    ts(half(TZ[0:8, 0, :], h), PS[0:8, 4 + h, 0:HT], small[0:8, 20:21], None, ALU.add)
                dve.drain().then_inc(lf_ready_z, 1)
                dve.wait_ge(tile_freed_act, l * TILES + G_IN + 39 + 4)
                stt(AF[0:8, :], TZ[0:8, 0, :], 0.0, TZ[0:8, 1, :], ALU.min, ALU.subtract)
                dve.drain().then_inc(lf_ready, 1)
                dve.wait_ge(lf_turned, 2 * l + 1)
                copy(LFX[0:8, T:T + PAST], PS[0:8, 0, :])
                copy(LFX[0:8, 0:T], AF[0:8, :])
                dve.drain()
                ones_row = ONES[0:8, :]
                dve.tensor_tensor_scan(DC[0:8, 0:SEQ], ones_row[:, 0:SEQ], LFX[0:8, 0:SEQ], 0.0, ALU.mult, ALU.add)
                dve.tensor_tensor_scan(DC[0:8, T:T + PAST], ones_row[:, 0:PAST], LFX[0:8, T:T + PAST], 0.0, ALU.mult,
                                       ALU.add)
                dve.drain()
                dve.tensor_tensor_scan(DC[0:8, SEQ:T], ones_row[:, 0:DEC_SEQ], LFX[0:8, SEQ:T],
                                       DC[0:8, T + PAST - 1:T + PAST], ALU.mult, ALU.add)
                dve.drain()
                ts(NDC[0:8, :], DC[0:8, :], -1.0, None, ALU.mult)
                dve.drain().then_inc(dc_ready, 1)
                dve.sem_inc(tile_freed_dve, 1)
                phase_end(dve, l, 1)

                dve.memset(FQ[64:66, :, :], 1.0)
                dve.memset(FK[64:66, :, :], 1.0)
                dve.drain().then_inc(fx_rows, 1)
                with dve.Fori(0, FOX_HEADS // 2) as it:
                    g = dve.snap(l * 4 + it)

                    def fox_max(k):
                        h, i = divmod(k, 5)
                        m, n = (P, (i + 1) * P) if i < 4 else (DEC_SEQ, T)
                        dve.wait_ge(fx_scores, g * 10 + k + 1)
                        dve.tensor_reduce(FST[0:m, k % 2, 0:1], pair(k % 2)[0:m, 0:n], AX.X, ALU.max,
                                          negate=True).then_inc(fx_max, 1)

                    def fox_norm(k):
                        h, i = divmod(k, 5)
                        m, n = (P, (i + 1) * P) if i < 4 else (DEC_SEQ, T)
                        dve.wait_ge(fx_exp, g * 10 + k + 1)
                        dve.reciprocal(FST[0:m, k % 2, 2:3], FST[0:m, k % 2, 1:2])
                        dve.drain()
                        ts(FP[0:m, k % 2, 0:n], FP[0:m, k % 2, 0:n], FST[0:m, k % 2, 2:3], None, ALU.mult) \
                            .then_inc(fx_norm, 1)

                    def fox_scale(h):
                        dve.wait_ge(fx_loaded[h], (g + 1) * 16 * 7)
                        ts(FQ[0:64, h, :], FQ[0:64, h, :], HEAD_DIM ** -0.5, None, ALU.mult).then_inc(fx_scaled, 1)

                    def fox_evac(h):
                        dve.wait_ge(fx_out, g * 2 + h + 1)
                        r = slice(64 * h, 64 * h + 64)
                        copy(brT[r, ds(it, 1), :], mid(pair(3)[r, 0:T], T)).then_inc(fx_evac, 1)

                    for k in range(11):
                        if k == 0:
                            fox_scale(0)
                        if k == 3:
                            fox_scale(1)
                        if k < 10:
                            fox_max(k)
                        if k == 8:
                            fox_evac(0)
                        if k >= 1:
                            fox_norm(k - 1)
                    fox_evac(1)
                phase_end(dve, l, 2)

                dve.wait_ge(rope_loaded, 16 * (l + 1))
                settle(dve)
                with dve.Fori(0, DIFF_HEADS // 2) as it:
                    g = dve.snap(l * 2 + it)
                    for h in range(2):
                        for i, x in enumerate((DQ, DK)):
                            dve.wait_ge(df_rot, g * 4 + 2 * h + i + 1)
                            for s in range(2):
                                tt(half(DTMP, s), PS[:, 2 * i + s, 0:HT], half(ROPE[:, 1, :], s), ALU.mult)
                            tt(x[:, h, 0:T], x[:, h, 0:T], ROPE[:, 0, :], ALU.mult)
                            dve.drain()
                            tt(x[:, h, 0:T], x[:, h, 0:T], DTMP, ALU.add)
                            dve.drain()
                            if i == 0:
                                ts(x[:, h, :], x[:, h, :], HEAD_DIM ** -0.5, None, ALU.mult)
                                dve.drain()
                            dve.sem_inc(df_rotated, 1)
                        for k in range(6):
                            if k < 5:
                                m, n = (P, (k + 1) * P) if k < 4 else (DEC_SEQ, T)
                                for c in range(2):
                                    dve.wait_ge(df_scores, g * 20 + 10 * h + 2 * k + c + 1)
                                    dve.tensor_reduce(DST[0:m, k % 2, c:c + 1], pair(c)[0:m, 0:n], AX.X, ALU.max,
                                                      negate=True).then_inc(df_max, 1)
                            if k >= 1:
                                i = k - 1
                                m, n = (P, (i + 1) * P) if i < 4 else (DEC_SEQ, T)
                                st = DST[0:m, i % 2, :]
                                dve.wait_ge(df_exp, g * 20 + 10 * h + 2 * i + 2)
                                dve.reciprocal(st[:, 4:6], st[:, 2:4])
                                dve.drain()
                                tt(st[:, 6:7], st[:, 5:6], small[0:m, 16:17], ALU.mult)
                                ts(DPB[0:m, i % 2, 0, 0:n], DPB[0:m, i % 2, 0, 0:n], st[:, 4:5], None, ALU.mult)
                                dve.drain()
                                stt(DPB[0:m, i % 2, 0, 0:n], DPB[0:m, i % 2, 1, 0:n], st[:, 6:7],
                                    DPB[0:m, i % 2, 0, 0:n], ALU.mult, ALU.add).then_inc(df_comb, 1)
                        dve.wait_ge(df_rs, g * 2 + h + 1)
                        stt(brT[:, ds(it * 2 + (4 + h), 1), :], mid(pair(3)[:, 0:T], T), small[:, 17:18],
                            mid(DRS, T), ALU.mult, ALU.mult).then_inc(df_evac, 1)
                phase_end(dve, l, 3)

                dve.memset(LX[:, :, 0:1], 0.0)
                dve.wait_ge(lo_loaded, (l + 1) * 16 * 5)
                sh = _v["state_rwkv_shift"]
                for i in range(2):
                    copy(LX[:, i, SEQ + 1:SEQ + 2], VT[:, sh + 12 + i:sh + 13 + i])
                dve.drain()
                for i in range(2):
                    tt(LT[:, i, :], LX[:, i, 0:T + 1], LX[:, i, 1:T + 2], ALU.subtract)
                dve.drain()
                for i in range(2):
                    mu = vec("rwkv_mu", 12 + i)
                    stt(LXS[:, i, 0:SEQ], LT[:, i, 0:SEQ], mu, LX[:, i, 1:SEQ + 1], ALU.mult, ALU.add)
                    stt(LXS[:, i, SEQ:T], LT[:, i, SEQ + 1:T + 1], mu, LX[:, i, SEQ + 2:T + 2], ALU.mult, ALU.add)
                dve.drain().then_inc(lo_mixed, 1)
                dve.wait_ge(lo_evac_act, l * 12 + 12)
                ts(LO[:, 0:4, :], LO[:, 0:4, :], -math.exp(-0.5), None, ALU.mult)
                dve.drain().then_inc(lo_evac_dve, 1)
                phase_end(dve, l, 4)

                for t in (Rx, Kx, Vx, LWx, Ax):
                    dve.memset(t[:, T:TP], 0.0)
                with dve.Fori(0, RWKV_HEADS // 2) as it:
                    g = dve.snap(l * 4 + it)
                    X = (Rx, Kx, Vx)
                    DIF = KR.rearrange("p a b -> p (a b)")
                    BEf, KHf = (z.rearrange("p a b -> p (a b)") for z in (BE, KH))
                    T0, T1, T2 = (W_RAW[:, i, :] for i in range(3))
                    L, LM = PZA[:, 0, :], PZA[:, 1, :]
                    EL, EN, EM = WWA[:, 0, :], WWA[:, 1, :], PZA[:, 1, :]

                    def dvec(name, i):
                        return VT[:, ds(it + (_v[name] + i), 1)]

                    dve.wait_ge(rw_loaded, (g + 1) * 16 * RW_LOADS)
                    dve.memset(W_RAW[:, :, 0:1], 0.0)
                    for i in range(3):
                        copy(W_RAW[:, i, SEQ + 1:SEQ + 2], dvec("state_rwkv_shift", 4 * i))
                    dve.drain()
                    for i in range(3):
                        raw = W_RAW[:, i, :]
                        tt(DIF[:, 0:T + 1], raw[:, 0:T + 1], raw[:, 1:T + 2], ALU.subtract)
                        dve.drain()
                        mu = dvec("rwkv_mu", 4 * i)
                        stt(X[i][:, 0:SEQ], DIF[:, 0:SEQ], mu, raw[:, 1:SEQ + 1], ALU.mult, ALU.add)
                        stt(X[i][:, SEQ:T], DIF[:, SEQ + 1:T + 1], mu, raw[:, SEQ + 2:T + 2], ALU.mult, ALU.add)
                        dve.drain()
                    ts(BEf, Kx, dvec("rwkv_kk_scale", 0), None, ALU.mult)
                    dve.tensor_tensor_scan(L, const("reset"), LWx, 0.0, ALU.mult, ALU.add)
                    dve.drain()
                    tt(T0, BEf, BEf, ALU.mult)
                    tt(LM, L, LWx, ALU.subtract)
                    dve.drain().then_inc(rw_in, 1)
                    ts(T1, Ax, -1.0, dvec("rwkv_ka", 0), ALU.add, ALU.mult)
                    dve.drain()
                    stt(T1, T1, 1.0, Kx, ALU.add, ALU.mult)
                    dve.drain()
                    stt(T2, Rx, dvec("rwkv_rk", 0), T1, ALU.mult, ALU.mult)
                    dve.wait_ge(rw_sum, g * 2 + 1)
                    for s in range(2):
                        c = slice(s * (TP // 2), (s + 1) * (TP // 2))
                        ts(T0[:, c], PS[:, 6 + s, 0:TP // 2], 1e-24, 2.0 ** 20, ALU.max, ALU.mult)
                    dve.drain().then_inc(rw_clip, 2)
                    dve.sem_inc(rw_in, 1)
                    dve.wait_ge(rw_exps, g + 1)
                    copy(DCOL, EL.rearrange("p (c n) -> p c n", c=9)[:, :, CHUNK - 1])
                    tt(BEf, BEf, T0, ALU.mult)
                    tt(KHf, T1, EN, ALU.mult)
                    c9 = lambda z: z.rearrange("p (c n) -> p c n", c=9)
                    tt(KR[:, :, CHUNK:], c9(Rx), c9(EL), ALU.mult)
                    dve.drain()
                    tt(KR[:, :, 0:CHUNK], BE, c9(EM), ALU.mult)
                    tt(T1, BEf, Ax, ALU.mult)
                    dve.drain()
                    tt(BEf, T1, EN, ALU.mult)
                    dve.wait_ge(rw_sum, g * 2 + 2)
                    for s in range(2):
                        c = slice(s * (TP // 2), (s + 1) * (TP // 2))
                        tt(Ax[:, c], PS[:, 6 + s, 0:TP // 2], Vx[:, c], ALU.mult)
                    dve.drain()
                    for gr in range(3):
                        dve.sem_inc(rw_ev[gr], 1)

                    def evac(s, gr):
                        X1, X2, Ao, GTt, HTt, Vt, Bt = range(7)
                        rt = X2
                        pl, wy, nz = PL[gr], WW[gr], PZ[gr]
                        lo, hi = slice(0, 64), slice(64, 128)

                        def v3(a):
                            return a.rearrange("p (c n) -> p c n", c=3)

                        def c3(name):
                            return v3(const(name))

                        def bank(i, at, n=64):
                            return v3(PS[:, 2 * gr + i, at:at + 3 * n])

                        dve.wait_ge(rw_mm[gr], g * 11 + s)
                        if s == 1:
                            b0, b1 = bank(0, 0, 128), bank(1, 0, 128)
                            tt(pl[X1], b0[:, :, 0:64], c3("up_d"), ALU.mult)
                            tt(pl[GTt], b0[:, :, 64:128], c3("up_i"), ALU.mult)
                            tt(pl[HTt], b1[:, :, 64:128], c3("up_i"), ALU.mult)
                            tt(BD[gr][5][lo, :, 0:64], b1[lo, :, 0:64], c3("up_s")[lo], ALU.mult)
                            tt(BD[gr][5][hi, :, 64:128], b1[hi, :, 0:64], c3("up_s")[hi], ALU.mult)
                        if s == 2:
                            a = bank(0, 0)
                            tt(pl[X2], a, c3("lo_d"), ALU.mult)
                            tt(pl[Ao], a, c3("lo_o"), ALU.mult)
                            tt(BD[gr][3][lo, :, 0:64], a[lo], c3("lo_d")[lo], ALU.mult)
                            tt(BD[gr][3][hi, :, 64:128], a[hi], c3("lo_d")[hi], ALU.mult)
                            copy(pl[Vt], bank(0, 192))
                            copy(wy[:, :, 0:64], bank(1, 0))
                            copy(pl[Bt], bank(1, 192))
                        if s == 3:
                            copy(wy[:, :, 64:128], bank(0, 0))
                            copy(nz[:, :, 0:64], bank(1, 0))
                            tt(nz[:, :, 64:128], pl[X1], c3("stack"), ALU.add)
                            copy(pl[X2], bank(1, 192))
                        if s == 4:
                            tt(nz[:, :, 64:128], bank(0, 0, 128)[:, :, 64:128], nz[:, :, 64:128], ALU.add)
                            copy(pl[X2], bank(1, 0))
                        if s == 5:
                            tt(nz[:, :, 64:128], bank(0, 0), nz[:, :, 64:128], ALU.add)
                        if s == 6:
                            z = nz[:, :, 64:128]
                            tt(BD[gr][0][lo, :, 0:64], bank(0, 0)[lo], z[lo], ALU.add)
                            tt(BD[gr][0][hi, :, 64:128], bank(0, 0)[hi], z[hi], ALU.add)
                            dve.drain()
                            tt(z, bank(0, 0), z, ALU.add)
                        if s == 7:
                            copy(pl[X1], bank(0, 0))
                            copy(wy, bank(1, 0, 128))
                        if s == 8:
                            tt(wy, wy, bank(1, 0, 128), ALU.subtract)
                        if s == 9:
                            stt(wy, bank(1, 0, 128), -1.0, wy, ALU.mult, ALU.subtract)
                        if s == 10:
                            tt(pl[rt], bank(0, 0), KR[:, 3 * gr:3 * gr + 3, CHUNK:], ALU.add)
                            m = bank(0, 192)
                            tt(BD[gr][2][lo, :, 0:64], m[lo], c3("stack")[lo], ALU.add)
                            tt(BD[gr][2][hi, :, 64:128], m[hi], c3("stack")[hi], ALU.add)
                        if s == 11:
                            copy(Yx[:, 192 * gr:192 * gr + 192], PS[:, 2 * gr + 1, 0:192])
                        dve.drain().then_inc(rw_ev[gr], 1)

                    for s in range(1, 11):
                        for gr in range(3):
                            evac(s, gr)
                    dve.wait_ge(rw_state, g * 10 + 1)
                    copy(BDS[:, 8, :], PS[:, 7, 256:384]).then_inc(rw_chain, 1)
                    for c in range(9):
                        dve.wait_ge(rw_state, g * 10 + c + 2)
                        to = c + 1 if c < 7 else c + 2
                        ts(BDS[:, to, :], PS[:, 6 + c % 2, 0:P], DCOL[:, c:c + 1], None, ALU.mult) \
                            .then_inc(rw_chain, 1)
                    for gr in range(3):
                        evac(11, gr)
                    dve.sem_inc(rp_y, 1)
                    dve.wait_ge(rp_mean, g + 1)
                    for s in range(2):
                        c = slice(s * (TP // 2), (s + 1) * (TP // 2))
                        stt(Yx[:, c], PS[:, 6 + s, 0:TP // 2], -1.0 / HEAD_DIM, Yx[:, c], ALU.mult, ALU.add)
                    dve.drain().then_inc(rp_yc, 1)
                    dve.wait_ge(rp_rs, g + 1)
                    stt(Yx, Yx, dvec("rwkv_ln_gain", 0), T0, ALU.mult, ALU.mult)
                    dve.drain()
                    stt(Yx, Yx, dvec("rwkv_ln_bias", 0), Ax, ALU.add, ALU.add)
                    dve.drain()
                    tt(brT[:, ds(it + 8, 1), :], mid(Yx[:, 0:T], T), mid(Gx[:, 0:T], T), ALU.mult)
                    dve.memset(Ax[:, T:TP], 0.0)
                    dve.memset(Kx[:, T:TP], 0.0)
                    dve.drain().then_inc(rp_done, 1)
                phase_end(dve, l, 5)

                with dve.Fori(0, 2) as it:
                    for s in range(1, 12, 2):
                        i = s % 6 // 2
                        for m in range(2):
                            n = 2 * s + m
                            sg, to = SG[:, (s - 1 + m) % 4, :], YT[:, ds(it * 4 + (2 * (s // 6) + m), 1), :]
                            tile(l, G_MERGE + n, it, 24)
                            dve.wait_ge(tile_freed_act, l * TILES + G_MERGE + n - 2 + 5 + it * 24)
                            for h in range(2):
                                dst = to[:, :, h * HT:(h + 1) * HT] if i == 0 else mid(half(TM[:, m, :], h), HT)
                                tt(dst, mid(PS[:, 2 * (n % 4) + h, 0:HT], HT), mid(half(sg, h), HT), ALU.mult)
                            dve.drain().then_inc(tile_freed_dve, 1 if m == 0 else 3)
                            if i > 0:
                                tt(to, to, mid(TM[:, m, :], T), ALU.add)
                                dve.drain()
                dve.drain().then_inc(y_ready, 1)
                for n in range(N_OUT):
                    tile(l, G_OUT + n)
                    copy(half(hT[:, n, :], 1), PS[:, 2 * (n % 4) + 1, 0:HT]).then_inc(tile_freed_dve, 1)
                phase_end(dve, l, 6)
                norm_squares(l, 1, hT)
                postnorm(l, 1, "norm_mix_post")
                norm_squares(l, 2, xT)
                prenorm(l, 2, "norm_x_pre")

                dve.wait_ge(memn_loaded, 16 * (l + 1))
                for a in range(KM):
                    ts(MNT[:, a, :], MNT[:, a, :], vec("norm_mem", a), None, ALU.mult)
                dve.drain().then_inc(mem_scaled, 1)
                dve.sem_inc(tile_freed_dve, N_MEMKV)
                for n in range(N_XQ):
                    tile(l, G_XQ + n)
                    ts(half(QX[:, n, :], 1), PS[:, 2 * (n % 4) + 1, 0:HT], X_DIM ** -0.5, None, ALU.mult) \
                        .then_inc(tile_freed_dve, 1)
                phase_end(dve, l, 7)

                def x_evac(h):
                    dve.wait_ge(xa_out, l * 4 + h + 1)
                    copy(OX[:, h, :], pair(3)[:, 0:T]).then_inc(xa_evac, 1)

                for k in range(21):
                    if k < 20:
                        m = P if k % 5 < 4 else DEC_SEQ
                        dve.wait_ge(xa_scores, l * 20 + k + 1)
                        dve.tensor_reduce(XST[0:m, k % 2, 0:1], PS[0:m, 2 * (k % 2), 0:N_MEM], AX.X, ALU.max,
                                          negate=True).then_inc(xa_max, 1)
                    if k >= 1:
                        j = k - 1
                        m = P if j % 5 < 4 else DEC_SEQ
                        dve.wait_ge(xa_exp, l * 20 + j + 1)
                        dve.reciprocal(XST[0:m, j % 2, 2:3], XST[0:m, j % 2, 1:2])
                        dve.drain()
                        ts(XP[0:m, j % 2, :], XP[0:m, j % 2, :], XST[0:m, j % 2, 2:3], None, ALU.mult) \
                            .then_inc(xa_norm, 1)
                    if k in (7, 12, 17):
                        x_evac((k - 7) // 5)
                x_evac(3)
                for n in range(N_XO):
                    tile(l, G_XO + n)
                    copy(half(hT[:, n, :], 1), PS[:, 2 * (n % 4) + 1, 0:HT]).then_inc(tile_freed_dve, 1)
                phase_end(dve, l, 8)
                norm_squares(l, 3, hT)
                postnorm(l, 3, "norm_x_post")
                norm_squares(l, 4, xT)
                prenorm(l, 4, "norm_ffn_pre")

                def products(it, s0, n_slots):
                    for s in range(s0, s0 + n_slots, 2):
                        for m in range(2):
                            n = 2 * s + m
                            sg = SGF[:, (s + m) % 4, :]
                            tile(l, G_FFI + n + 2, it, 8)
                            dve.wait_ge(tile_freed_act, l * TILES + G_FFI + n + 1 + 4 + it * 8)
                            for h in range(2):
                                tt(half(sg, h), PS[:, 2 * (n % 4) + h, 0:HT], half(sg, h), ALU.mult)
                            dve.drain()
                            for h in range(2):
                                tt(GT[:, ds(it * 4 + (s + m), 1), h * HT:(h + 1) * HT]
                                   if not isinstance(it, int) else GT[:, s + m:s + m + 1, h * HT:(h + 1) * HT],
                                   mid(PS[:, 2 * ((n + 2) % 4) + h, 0:HT], HT), mid(half(sg, h), HT), ALU.mult)
                            dve.drain().then_inc(tile_freed_dve, 1 if m == 0 else 3)

                with dve.Fori(0, 5) as it:
                    products(it, 0, 4)
                products(0, 20, 2)
                dve.drain().then_inc(g_ready, 1)
                with dve.Fori(0, 4) as it:
                    for m in range(2):
                        tile(l, G_FFO + m, it, 2)
                        copy(hT[:, ds(it * 2 + m, 1), HT:T], mid(PS[:, 2 * m + 1, 0:HT], HT)) \
                            .then_inc(tile_freed_dve, 1)
                phase_end(dve, l, 9)
                norm_squares(l, 5, hT)
                postnorm(l, 5, "norm_ffn_post")
                dve.sem_inc(x_done, 1)

        @block.gpsimd
        def _(pool):
            dma = pool.dma_start

            def wait(sem_, value):
                pool.wait_ge(sem_, value)
                settle(pool)

            dma(CB[:, :], C_const).then_inc(consts_loaded, 16)
            dma(xtok[:, 0:4, :], A["x_prompt"].rearrange("b (t p) d -> p (b t) d", p=P)).then_inc(x_loaded, 16)
            dma(xtok[0:DEC_SEQ, 4, :], A["x_sample"].rearrange("b t d -> (b t) d")).then_inc(x_loaded, 16)
            dma(mtok[:, :, :], A["mem_prompt"].rearrange("b (t p) d -> p (b t) d", p=P)).then_inc(x_loaded, 16)
            pool.wait_ge(x_put_act, 2 * KM)
            pool.wait_ge(x_put_dve, 2 * KM)
            dma(memn_d, mnT.rearrange("p a b -> p (a b)")).then_inc(memn_stored, 16)
            pool.wait_ge(memn_stored, 16)

            with pool.Fori(0, DEPTH) as l:
                for name, row in _v.items():
                    a = A[name][ds(l, 1)]
                    n = NVEC_OF[name]
                    if name == "rwkv_rk":
                        src = a.rearrange("l (r h) d -> (l r) (h d)", r=4)
                    elif name == "state_rwkv_shift":
                        src = a.rearrange("l b (r c) -> (l b r) c", c=P)
                    else:
                        src = a.rearrange("l (r c) -> (l r) c", c=P)
                    dma(VR[row:row + n, :], src).then_inc(vec_loaded, 16)
                dma(small[0:8, 20:21], A["fox_forget_bias"][ds(l, 1)].rearrange("l h -> h l"),
                    allow_slow_non_contiguous=True).then_inc(vec_loaded, 16)
                dma(lam4[:, :, :].rearrange("p a b -> p (a b)"),
                    A["diff_lambda"][ds(l, 1)].rearrange("l a b -> l (a b)").to_broadcast([P, 256])) \
                    .then_inc(vec_loaded, 16)
                dma(PLF[:, :, :], A["cache_fox_logf"][ds(l, 1)].rearrange("l b (t p) h -> p (l b t) h", p=P)) \
                    .then_inc(plf_loaded, 16)
                wait(vec_loaded, (l + 1) * 16 * 19)
                wait(plf_loaded, (l + 1) * 16)
                phase_end(pool, l, 0)

                def store_tiles(it, j0, n):
                    for j in range(n):
                        c = l * TILES + G_IN + 2 * (j0 + j) + 2 + 4 + it * 8
                        wait(tile_freed_act, c)
                        wait(tile_freed_dve, c)
                        rows = proj_d[ds(it * 1024 + (j0 + j) * 256, 256), :] if not isinstance(it, int) else \
                            proj_d[(j0 + j) * 256:(j0 + j) * 256 + 256, :]
                        dma(rows.rearrange("(m p) t -> p m t", p=P), EST[:, j % 2, :, :]) \
                            .then_inc(est_stored[j % 2], 16)

                with pool.Fori(0, 4) as it:
                    store_tiles(it, 0, 4)
                store_tiles(0, 16, 3)
                wait(dc_ready, l + 1)
                dma(dcum_d[0], DC[0:8, :]).then_inc(lf_stored, 16)
                dma(dcum_d[1], NDC[0:8, :]).then_inc(lf_stored, 16)
                wait(lf_put, l + 1)
                dma(p_fox_logf[ds(l, 1)].rearrange("l b (t p) h -> p (l b t) h", p=P), LFT[:, 0:4, :]) \
                    .then_inc(lf_stored, 16)
                dma(s_fox_logf[ds(l, 1)].rearrange("l b t h -> (l b t) h"), LFT[0:DEC_SEQ, 4, :]).then_inc(lf_stored, 16)
                wait(lf_stored, (l + 1) * 64)
                for s in range(2):
                    wait(est_stored[s], 16 * (l + 1) * (10 - s))
                for src, to in ((SEQ - 1, p_shift), (T - 1, s_shift)):
                    dma(to[ds(l, 1)].rearrange("l b c -> (l b c)").rearrange("(c o) -> c o", o=1),
                        proj_d[R_RW:R_RW + RWKV_IN, src:src + 1], allow_slow_non_contiguous=True).then_inc(shift_stored, 16)
                wait(shift_stored, (l + 1) * 32)
                phase_end(pool, l, 1)

                wait(fx_rows, l + 1)
                with pool.Fori(0, FOX_HEADS // 2) as it:
                    g = pool.snap(l * 4 + it)
                    for h in range(2):
                        s = fx_loaded[h]
                        rows = lambda r: proj_d[ds(it * P + (r + 64 * h), 64), :]
                        hd = lambda name: A[name][ds(l, 1), :, :, ds(it * 2 + h, 1), :] \
                            .rearrange("l b (t p) h d -> p (l b t h) d", p=P)
                        dma(FQ[0:64, h, :], rows(R_FQ)).then_inc(s, 16)
                        dma(FK[0:64, h, 0:T], rows(R_FK)).then_inc(s, 16)
                        dma(FVR[0:64, h, :], rows(R_FV)).then_inc(s, 16)
                        dma(FPK[:, h, :, :], hd("cache_fox_k")).then_inc(s, 16)
                        dma(FVT[:, h, 5:9, :], hd("cache_fox_v")).then_inc(s, 16)
                        dma(FQ[64:65, h, :], dcum_d[0, ds(it * 2 + h, 1), 0:T]).then_inc(s, 16)
                        dma(FK[65:66, h, :], dcum_d[1, ds(it * 2 + h, 1), :]).then_inc(s, 16)
                    for h in range(2):
                        wait(fx_put, g * 16 + (3, 8)[h] + 2)
                        for t, op, os_ in ((FVT, p_fox_v, s_fox_v), (FKT, p_fox_k, s_fox_k)):
                            dma(op[ds(l, 1), :, :, ds(it * 2 + h, 1), :].rearrange("l b (t p) h d -> p (l b t h) d", p=P),
                                t[:, h, 0:4, :]).then_inc(fx_stored[h], 16)
                            dma(os_[ds(l, 1), :, :, ds(it * 2 + h, 1), :].rearrange("l b t h d -> (l b t h) d"),
                                t[0:DEC_SEQ, h, 4, :]).then_inc(fx_stored[h], 16)
                    wait(fx_evac, g * 2 + 4)
                    for h in range(2):
                        wait(fx_stored[h], (g + 1) * 64)
                phase_end(pool, l, 2)

                dma(ROPE, C_rope).then_inc(rope_loaded, 16)
                with pool.Fori(0, DIFF_HEADS // 2) as it:
                    g = pool.snap(l * 2 + it)
                    for h in range(2):
                        s = df_loaded[h]
                        rows = lambda r: proj_d[ds(it * 256 + (r + P * h), P), :]
                        dma(DQ[:, h, :], rows(R_DQ)).then_inc(s, 16)
                        dma(DK[:, h, 0:T], rows(R_DK)).then_inc(s, 16)
                        dma(DVR[:, h, :], rows(R_DV)).then_inc(s, 16)
                        dma(DPK[:, h, :, :], A["cache_diff_k"][ds(l, 1), :, :, ds(it * 2 + h, 1), :, :]
                            .rearrange("l b (t p) h c d -> p (l b t h) (c d)", p=P)).then_inc(s, 16)
                        dma(DVT[:, h, 5:9, :], A["cache_diff_v"][ds(l, 1), :, :, ds(it * 2 + h, 1), :]
                            .rearrange("l b (t p) h d -> p (l b t h) d", p=P)).then_inc(s, 16)
                    for h in range(2):
                        wait(df_put, g * 18 + 9 * h + 4)
                        dma(p_diff_v[ds(l, 1), :, :, ds(it * 2 + h, 1), :]
                            .rearrange("l b (t p) h d -> p (l b t h) d", p=P), DVT[:, h, 0:4, :]) \
                            .then_inc(df_stored[h], 16)
                        dma(s_diff_v[ds(l, 1), :, :, ds(it * 2 + h, 1), :].rearrange("l b t h d -> (l b t h) d"),
                            DVT[0:DEC_SEQ, h, 4, :]).then_inc(df_stored[h], 16)
                        dma(p_diff_k[ds(l, 1), :, :, ds(it * 2 + h, 1), :, :]
                            .rearrange("l b (t p) h c d -> p (l b t h) (c d)", p=P), DKT[:, h, 0:4, :]) \
                            .then_inc(df_stored[h], 16)
                        dma(s_diff_k[ds(l, 1), :, :, ds(it * 2 + h, 1), :, :]
                            .rearrange("l b t h c d -> (l b t h) (c d)"), DKT[0:DEC_SEQ, h, 4, :]) \
                            .then_inc(df_stored[h], 16)
                    wait(df_evac, g * 2 + 3)
                    for h in range(2):
                        wait(df_stored[h], (g + 1) * 64)
                phase_end(pool, l, 3)

                for i in range(2):
                    r = R_RW + 1536 + P * i
                    dma(LX[:, i, 1:SEQ + 1], proj_d[r:r + P, 0:SEQ]).then_inc(lo_loaded, 16)
                    if i == 0:
                        dma(LX[:, :, SEQ + 2:T + 2], proj_d[r:r + 2 * P, SEQ:T].rearrange("(i p) t -> p i t", i=2)) \
                            .then_inc(lo_loaded, 16)
                dma(LW2[0:64, :], A["rwkv_w2"][ds(l, 1)].rearrange("l k n -> (l k) n")).then_inc(lo_w_loaded, 16)
                dma(LW2[64:128, :], A["rwkv_a2"][ds(l, 1)].rearrange("l k n -> (l k) n")).then_inc(lo_loaded, 16)
                dma(LG2, A["rwkv_g2"][ds(l, 1)].rearrange("l k n -> (l k) n")).then_inc(lo_loaded, 16)
                wait(lo_evac_dve, l + 1)
                dma(proj_d[R_LW:R_END, :].rearrange("(a p) t -> p a t", p=P), LO).then_inc(lo_stored, 16)
                wait(lo_stored, 16 * (l + 1))
                phase_end(pool, l, 4)

                pool.memset(BDALL, 0.0)
                with pool.Fori(0, RWKV_HEADS // 2) as it:
                    g = pool.snap(l * 4 + it)
                    ld = rw_loaded
                    for i in range(3):
                        rows = proj_d[ds(it * P + (R_RW + 512 * i), P), :]
                        dma(W_RAW[:, i, 1:SEQ + 1], rows[:, 0:SEQ]).then_inc(ld, 16)
                        dma(W_RAW[:, i, SEQ + 2:T + 2], rows[:, SEQ:T]).then_inc(ld, 16)
                    for i, t in enumerate((LWx, Ax, Gx)):
                        dma(t[:, 0:T], proj_d[ds(it * P + (R_LW + 512 * i), P), :]).then_inc(ld, 16)
                    pool.drain()
                    for h in range(2):
                        r = slice(64 * h, 64 * h + 64)
                        dma(BDS[r, 11, 64 * h:64 * h + 64], A["state_rwkv"][ds(l, 1), :, ds(it * 2 + h, 1), :, :]
                            .rearrange("l b h v k -> (l b h v) k")).then_inc(ld, 16)
                    for gr in range(3):
                        wait(rw_ev[gr], g * 12 + 1)
                        for slot, src in ((2, KR[:, 3 * gr:3 * gr + 3, 0:CHUNK]),
                                          (3, Vx.rearrange("p (c n) -> p c n", c=9)[:, 3 * gr:3 * gr + 3, :])):
                            pool.tensor_copy(BD[gr][slot][0:64, :, 0:64], src[0:64])
                            pool.tensor_copy(BD[gr][slot][64:128, :, 64:128], src[64:128])
                        pool.drain().then_inc(rw_bd, 1)
                    wait(rw_fin, g + 1)
                    for h in range(2):
                        r = slice(64 * h, 64 * h + 64)
                        for i, o in enumerate((p_state, s_state)):
                            dma(o[ds(l, 1), :, ds(it * 2 + h, 1), :, :].rearrange("l b h v k -> (l b h v) k"),
                                XS[r, i, 64 * h:64 * h + 64]).then_inc(rw_stored, 16)
                    wait(rw_stored, (g + 1) * 64)
                    wait(rp_done, g + 1)
                phase_end(pool, l, 5)
                phase_end(pool, l, 6)

                dma(MNT.rearrange("p a b -> p (a b)"), memn_d).then_inc(memn_loaded, 16)
                for t, name in ((CKT, "cache_mem_k"), (CVT, "cache_mem_v")):
                    dma(t, A[name][ds(l, 1)].rearrange("l b (t p) h d -> p (l b t) (h d)", p=P)).then_inc(xa_loaded, 16)
                phase_end(pool, l, 7)
                for t, o in ((0, p_mem_k), (512, p_mem_v)):
                    dma(o[ds(l, 1)].rearrange("l b (t p) h d -> p (l b t) (h d)", p=P), MKV[:, :, t:t + 512]) \
                        .then_inc(xa_stored, 16)
                wait(xa_stored, (l + 1) * 32)
                phase_end(pool, l, 8)
                phase_end(pool, l, 9)

            for b in range(5):
                pool.wait_ge(end_put, 2 * b + 2)
                if b < 4:
                    dma(y_prompt[0, b * P:(b + 1) * P, :], otok[:, b, :]).then_inc(end_stored, 16)
                else:
                    dma(y_sample[0, :, :], otok[0:DEC_SEQ, 4, :]).then_inc(end_stored, 16)
            pool.wait_ge(end_stored, 5 * 16)


_INS = ['x_prompt', 'x_sample', 'mem_prompt', 'cache_fox_k', 'cache_fox_v', 'cache_fox_logf', 'cache_diff_k',
        'cache_diff_v', 'state_rwkv', 'state_rwkv_shift', 'cache_mem_k', 'cache_mem_v', 'norm_mix_pre',
        'norm_mix_post', 'w_in', 'fox_forget_bias', 'diff_lambda', 'diff_subln', 'rwkv_mu', 'rwkv_w0', 'rwkv_w2',
        'rwkv_a0', 'rwkv_a2', 'rwkv_g2', 'rwkv_kk_scale', 'rwkv_ka', 'rwkv_rk', 'rwkv_ln_gain', 'rwkv_ln_bias',
        'w_branch', 'w_out', 'norm_x_pre', 'norm_x_post', 'norm_mem', 'w_xq', 'w_xkv', 'w_xo', 'norm_ffn_pre',
        'norm_ffn_post', 'w_ffn_in', 'w_ffn_out']
_L = DEPTH
_OUTS = [(1, SEQ, D_MODEL), (1, DEC_SEQ, D_MODEL),
         (_L, 1, SEQ, 8, 64), (_L, 1, SEQ, 8, 64), (_L, 1, SEQ, 8), (_L, 1, SEQ, 4, 2, 64), (_L, 1, SEQ, 4, 128),
         (_L, 1, 8, 64, 64), (_L, 1, RWKV_IN), (_L, 1, N_MEM, 4, 128), (_L, 1, N_MEM, 4, 128),
         (_L, 1, DEC_SEQ, 8, 64), (_L, 1, DEC_SEQ, 8, 64), (_L, 1, DEC_SEQ, 8), (_L, 1, DEC_SEQ, 4, 2, 64),
         (_L, 1, DEC_SEQ, 4, 128), (_L, 1, 8, 64, 64), (_L, 1, RWKV_IN)]


def kernel(**inputs):
    import numpy as _np
    import concourse.bacc as _bacc
    from concourse import mybir as _mybir
    from concourse.bass_utils import run_bass_kernel_spmd as _run

    nc = _bacc.Bacc("TRN2", target_bir_lowering=False, num_devices=1)
    arrays, args = {}, {}
    for name in _INS:
        a = _np.ascontiguousarray(inputs[name])
        arrays[f"in_{name}_dram"] = a
        args[name] = nc.dram_tensor(f"in_{name}_dram", a.shape, _mybir.dt.from_np(a.dtype), kind="ExternalInput").ap()
    tables = []
    for name, a in zip(("const", "rope"), constants()):
        arrays[f"in_{name}_dram"] = a
        tables.append(nc.dram_tensor(f"in_{name}_dram", a.shape, _mybir.dt.from_np(a.dtype), kind="ExternalInput").ap())
    outs = [nc.dram_tensor(f"out_{i}_dram", shape, _mybir.dt.float32, kind="ExternalOutput").ap()
            for i, shape in enumerate(_OUTS)]
    build_program(nc, args, *tables, outs)
    r = _run(nc, [arrays], core_ids=[0])
    return tuple(r.results[0][f"out_{i}_dram"] for i in range(len(_OUTS)))
```

```python
from contextlib import ExitStack
import math

import numpy as np

import concourse.bass as bass
from concourse import mybir

F32 = mybir.dt.float32
BF16 = mybir.dt.bfloat16
F32R = mybir.dt.float32r
ACT = mybir.ActivationFunctionType
ALU = mybir.AluOpType
AX = mybir.AxisListType
ds = bass.ds

D_MODEL, SEQ, DEPTH, DEC_SEQ, PAST = 1024, 512, 2, 32, 512
CHUNK, HEAD_DIM, FOX_HEADS, DIFF_HEADS, RWKV_HEADS = 64, 64, 8, 4, 8
BRANCH_W, N_MEM, X_HEADS, X_DIM = 512, 256, 4, 128
FFN = -(-8 * D_MODEL // (3 * 256)) * 256
RWKV_IN = 3 * 512 + 64 + 64 + 128
IN_WIDTH = 3 * 512 + FOX_HEADS + 3 * 512 + RWKV_IN + 3 * D_MODEL
ROPE_THETA, RMS_EPS, GN_EPS = 500000.0, 1e-6, 64e-5
P = 128
T = SEQ + DEC_SEQ
HT = T // 2
KM = D_MODEL // P
TP = 9 * CHUNK
KF = FFN // P

RING = 4
FFO_SPLIT = (8, 7, 7)
U_IN, U_FORGET, U_MERGE, U_OUT, U_MEM, U_XQ, U_XO, U_FFI, U_FFO = 0, 38, 39, 87, 95, 103, 107, 115, 159
UNITS = U_FFO + 8 * len(FFO_SPLIT)
USES = [(UNITS - p + RING - 1) // RING for p in range(RING)]
V_MERGE, V_OUT, V_FFI, V_FFO = 38, 86, 94, 138
SPLITS = V_FFO + 8 * len(FFO_SPLIT)
X_SPLITS = 4 + 4 + 6 + 4


def unit_of(v):
    return v if v < V_MERGE else v + U_MERGE - V_MERGE if v < V_FFI else v + U_FFI - V_FFI


def depth_of(v):
    if V_MERGE <= v < V_OUT:
        return 8 if (v - V_MERGE) % 4 < 2 else 4
    return FFO_SPLIT[(v - V_FFO) % 3] if v >= V_FFO else 8

N_IN, N_MERGE, N_OUT, N_MEMKV, N_XQ, N_XO, N_FFI, N_FFO = 39, 48, 8, 8, 4, 8, 44, 8
G_IN = 0
G_MERGE = G_IN + N_IN
G_OUT = G_MERGE + N_MERGE
G_MEM = G_OUT + N_OUT
G_XQ = G_MEM + N_MEMKV
G_XO = G_XQ + N_XQ
G_FFI = G_XO + N_XO
G_FFO = G_FFI + N_FFI
TILES = G_FFO + N_FFO

R_FQ, R_FK, R_FV, R_DQ, R_DK, R_DV = (i * 512 for i in range(6))
R_RW = 3072
R_LW = R_RW + RWKV_IN
R_END = R_LW + 3 * 512

_c = {}
_n = 0
for _name, _w in (("ident", 128), ("stack", 192), ("bdones", 128), ("rot", 128), ("mfox", 128), ("mdiff", 128),
                  ("up_d", 192), ("up_s", 192), ("up_i", 192), ("lo_d", 192), ("lo_o", 192), ("reset", TP), ("lam", 4)):
    _c[_name] = (_n, _n + _w)
    _n += _w
NCONST = _n

_v = {}
NVEC_OF = {}
_n = 0
for _name, _w in (("norm_mix_pre", 8), ("norm_mix_post", 8), ("norm_x_pre", 8), ("norm_x_post", 8), ("norm_mem", 8),
                  ("norm_ffn_pre", 8), ("norm_ffn_post", 8), ("rwkv_mu", 14), ("rwkv_w0", 4), ("rwkv_a0", 4),
                  ("rwkv_kk_scale", 4), ("rwkv_ka", 4), ("rwkv_rk", 4), ("rwkv_ln_gain", 4), ("rwkv_ln_bias", 4),
                  ("diff_subln", 1), ("state_rwkv_shift", 14)):
    _v[_name], NVEC_OF[_name] = _n, _w
    _n += _w
NVEC = _n
RW_LOADS = 11


def constants():
    c = np.zeros((P, NCONST), np.float32)

    def put(name, a):
        c[:, _c[name][0]:_c[name][1]] = a

    i64 = np.eye(64, dtype=np.float32)
    put("ident", np.eye(P))
    put("stack", np.tile(np.vstack([i64, i64]), (1, 3)))
    put("bdones", np.kron(np.eye(2), np.ones((64, 64))))
    rot = np.zeros((P, P), np.float32)
    for b in (0, 64):
        for j in range(8):
            rot[b + j + 8, b + j] = -1.0
            rot[b + j, b + j + 8] = 1.0
    put("rot", rot)
    q, k = np.arange(P)[:, None], np.arange(P)[None, :]
    put("mfox", np.where(k <= q, 0.0, -1e30))
    put("mdiff", np.where(k // CHUNK <= q // CHUNK, 0.0, -1e30))
    r, s = np.arange(64)[:, None], np.arange(64)[None, :]
    same = r // 16 == s // 16
    for name, m in (("up_d", -1.0 * ((r < s) & same)), ("up_s", r < s), ("up_i", r <= s),
                    ("lo_d", -1.0 * ((r > s) & same)), ("lo_o", (r > s) & ~same)):
        put(name, np.tile(np.vstack([m, m]), (1, 3)))
    put("reset", (np.arange(TP) % CHUNK != 0)[None, :])
    lam = [0.8 - 0.6 * math.exp(-0.3 * l) for l in range(DEPTH)]
    put("lam", np.array([lam[0], lam[1], 1 - lam[0], 1 - lam[1]])[None, :])
    half = 8
    inv = (np.float32(ROPE_THETA) ** (-np.arange(half, dtype=np.float32) / np.float32(half))).astype(np.float32)
    pos = np.concatenate([np.arange(SEQ), PAST + np.arange(DEC_SEQ)]).astype(np.float32)
    ang = (pos[None, :] * inv[:, None]).astype(np.float32)
    rope = np.zeros((P, 2, T), np.float32)
    rope[:, 0] = 1.0
    for b in (0, 8, 64, 72):
        rope[b:b + 8, 0] = np.cos(ang)
        rope[b:b + 8, 1] = np.sin(ang)
    return c, rope


def build_program(nc, A, C_const, C_rope, O):
    (y_prompt, y_sample, p_fox_k, p_fox_v, p_fox_logf, p_diff_k, p_diff_v, p_state, p_shift, p_mem_k, p_mem_v,
     s_fox_k, s_fox_v, s_fox_logf, s_diff_k, s_diff_v, s_state, s_shift) = O
    proj_d = nc.dram_tensor("proj_scratch", (R_END, T), F32).ap()
    memn_d = nc.dram_tensor("memn_scratch", (P, KM * N_MEM), F32).ap()
    dcum_d = nc.dram_tensor("dcum_scratch", (2, FOX_HEADS, T + PAST), F32).ap()

    with ExitStack() as ctx:
        def sb(name, shape, dt=F32):
            return ctx.enter_context(nc.sbuf_tensor(name, shape, dt))

        def twins(name, shape):
            at = -(-nc.sbuf_base // 32) * 32
            t = sb(name, shape)
            return t, nc.alloc_sbuf_tensor_at(name + "_r", shape, F32R, offset=at)

        def sem(name):
            return ctx.enter_context(nc.semaphore(name))

        xT = sb("xT", [P, KM, T])
        hT, hTR = twins("hT", [P, KM, T])
        ring = sb("ring", [P, RING, 8, P])
        WHI = sb("WHI", [P, 2, 8, P], F32R)
        WLO = sb("WLO", [P, 2, 8, P], F32R)
        brT, brTR = twins("brT", [P, 12, T])
        CB = sb("CB", [P, NCONST])
        identb = sb("identb", [P, P], BF16)
        mfoxb = sb("mfoxb", [P, P], BF16)
        mdiffb = sb("mdiffb", [P, P], BF16)
        ones = sb("ones", [P, P])
        VT = sb("VT", [P, P])
        small = sb("small", [P, 64])
        eps = sb("eps", [P, 4])
        lam4 = sb("lam4", [P, 4, HEAD_DIM])
        lamp = sb("lamp", [P, 2, HEAD_DIM])
        VR = sb("VR", [P, P])
        PLF = sb("PLF", [P, 4, 8])
        NU = 25990
        U, UR = twins("U", [P, NU])
        PS = ctx.enter_context(nc.psum_tensor("PS", [P, 8, 512], F32))

        def const(name):
            return CB[:, _c[name][0]:_c[name][1]]

        def vec(name, i):
            return VT[:, _v[name] + i:_v[name] + i + 1]

        def pair(q):
            return PS[:, 2 * q:2 * q + 2, :].rearrange("p a n -> p (a n)")

        def carver(start=0):
            at = [start]

            def carve(*dims, of=U):
                n = int(np.prod(dims))
                v = of[:, at[0]:at[0] + n]
                at[0] += n
                assert at[0] <= NU, at[0]
                if len(dims) == 1:
                    return v
                names = " ".join("abc"[:len(dims)])
                return v.rearrange(f"p ({names}) -> p {names}", **{"abc"[i]: d for i, d in enumerate(dims)})
            return carve

        cv = carver(0)
        SQ, RS = cv(KM, T), cv(T)
        xtok = cv(5, D_MODEL)
        mtok = cv(2, D_MODEL)
        mnT = cv(KM, N_MEM)
        cv = carver(KM * T + T)
        EST = cv(2, 2, T)
        AF = cv(T)
        DC = cv(T + PAST)
        LFT = cv(5, 8)
        LFX = cv(T + PAST)
        NDC = cv(T + PAST)
        TZ = cv(2, T)
        ONES = cv(SEQ)
        HH, HL = cv(KM, T, of=UR), cv(KM, T, of=UR)
        cv = carver(0)
        FQ, FK = cv(2, T), cv(2, T + PAST)
        FVR, FPK = cv(2, T), cv(2, 4, HEAD_DIM)
        FVT, FKT = cv(2, 9, HEAD_DIM), cv(2, 5, HEAD_DIM)
        FP, FPT = cv(2, T), cv(2, 5 * P)
        FST = cv(2, 4)
        cv = carver(0)
        ROPE = cv(2, T)
        DQ, DK = cv(2, T), cv(2, T + PAST)
        DVR, DPK = cv(2, T), cv(2, 4, P)
        DVT, DKT = cv(2, 9, P), cv(2, 5, P)
        DPB = cv(2, 2, T)
        DPT = cv(2, 5 * P)
        DTMP, DO, DRS = cv(T), cv(T), cv(T)
        DST = cv(2, 8)
        cv = carver(0)
        LX = cv(2, T + 2)
        LT = cv(2, T + 1)
        LXS = cv(2, T)
        LW2, LG2 = cv(512), cv(512)
        LO = cv(12, T)
        cv = carver(0)
        W_RAW = cv(3, TP)
        Rx, Kx, Vx, LWx, Ax, Gx = (cv(TP) for _ in range(6))
        KR = cv(9, 2 * CHUNK)
        BE, KH = cv(9, CHUNK), cv(9, CHUNK)
        PL = [[cv(3, CHUNK) for _ in range(7)] for _ in range(3)]
        PZA, WWA = cv(2, TP), cv(2, TP)
        PZ, WW = ([a.rearrange("p a b -> p (a b)")[:, g * 384:(g + 1) * 384].rearrange("p (c n) -> p c n", c=3)
                   for g in range(3)] for a in (PZA, WWA))
        DCOL = cv(9)
        XS = W_RAW[:, 1, 0:2 * P].rearrange("p (a b) -> p a b", a=2)
        bd_words = 27 * 3 * P + 12 * P
        BDALL = cv(bd_words)
        BD = [[BDALL[:, (g * 9 + s) * 3 * P:(g * 9 + s + 1) * 3 * P].rearrange("p (c n) -> p c n", c=3)
               for s in range(9)] for g in range(3)]
        BDS = BDALL[:, 27 * 3 * P:].rearrange("p (c n) -> p c n", c=12)
        Yx = Kx
        cv = carver(KM * T + T)
        YT, YL = cv(KM, T), carver(KM * T + T)(KM, T, of=UR)
        SG = cv(4, T)
        TM = cv(2, T)
        HX = cv(KM, T, of=UR)
        BH = cv(12, T, of=UR)
        YH = carver(0)(KM, T, of=UR)
        cv = carver(KM * T + T)
        MNT = cv(KM, N_MEM)
        MKV = cv(2, 2 * 512)
        CKT, CVT = cv(2, 512), cv(2, 512)
        MKT = cv(2, X_HEADS, N_MEM)
        QX = cv(X_HEADS, T)
        OX = cv(X_HEADS, T)
        XP, XPT = cv(2, N_MEM), cv(2, 2 * P)
        XST = cv(2, 4)
        cv = carver(0)
        GH, GL = cv(KF, T, of=UR), cv(KF, T, of=UR)
        HF, SGF = brTR[:, 0:KM, :], brT[:, KM:KM + 4, :]
        cv = carver(0)
        otok = cv(5, D_MODEL)

        consts_loaded, x_loaded, x_put_act, x_put_dve, setup_pe, setup_act, memn_stored = (
            sem(n) for n in ("consts_loaded", "x_loaded", "x_put_act", "x_put_dve", "setup_pe", "setup_act", "memn_stored"))
        consts_ready = sem("consts_ready")
        mem_scaled = sem("mem_scaled")
        slot_loaded = [sem(f"slot_loaded{i}") for i in range(RING)]
        split_done, part_used, x_split = sem("split_done"), sem("part_used"), sem("x_split")
        tile_done, tile_freed_act, tile_freed_dve = sem("tile_done"), sem("tile_freed_act"), sem("tile_freed_dve")
        bar = sem("phase_ended")
        vec_loaded, vec_turned, vec_ready = sem("vec_loaded"), sem("vec_turned"), sem("vec_ready")
        sq_act, sq_dve, sums_done, rstd_ready, h_ready = (
            sem(n) for n in ("sq_act", "sq_dve", "sums_done", "rstd_ready", "h_ready"))
        est_stored, est_free = [sem("est_stored0"), sem("est_stored1")], sem("est_free")
        fx_free, df_free = ([sem(f"{n}_free{h}") for h in range(2)] for n in ("fx", "df"))
        rw_free, rw_cleared = sem("rw_free"), sem("rw_cleared")
        lf_ready, lf_turned, lf_put, lf_stored, dc_ready = (
            sem(n) for n in ("lf_ready", "lf_turned", "lf_put", "lf_stored", "dc_ready"))
        plf_loaded = sem("plf_loaded")
        fx_loaded = [sem("fx_loaded0"), sem("fx_loaded1")]
        fx_stored = [sem("fx_stored0"), sem("fx_stored1")]
        fx_scaled, fx_scores, fx_max, fx_exp, fx_norm, fx_turned, fx_put, fx_out, fx_evac = (
            sem("fx_" + n) for n in ("scaled", "scores", "max", "exp", "norm", "turned", "put", "out", "evac"))
        rope_loaded = sem("rope_loaded")
        df_loaded = [sem("df_loaded0"), sem("df_loaded1")]
        df_stored = [sem("df_stored0"), sem("df_stored1")]
        (df_rot, df_rotated, df_scores, df_max, df_exp, df_comb, df_turned, df_put, df_out, df_sq, df_sum, df_rs,
         df_evac) = (sem("df_" + n) for n in ("rot", "rotated", "scores", "max", "exp", "comb", "turned", "put",
                                             "out", "sq", "sum", "rs", "evac"))
        lo_loaded, lo_mixed, lo_act, lo_done, lo_evac_act, lo_evac_dve, lo_stored = (
            sem("lo_" + n) for n in ("loaded", "mixed", "act", "done", "evac_act", "evac_dve", "stored"))
        (rw_loaded, rw_in, rw_sum, rw_clip, rw_exps, rw_bd, rw_chain, rw_state, rw_final, rw_fin, rw_stored) = (
            sem("rw_" + n) for n in ("loaded", "in", "sum", "clip", "exps", "bd", "chain", "state", "final", "fin",
                                     "stored"))
        rp_y, rp_mean, rp_yc, rp_sq, rp_var, rp_rs, rp_done = (
            sem("rp_" + n) for n in ("y", "mean", "yc", "sq", "var", "rs", "done"))
        rw_mm, rw_ev, rw_eva = ([sem(f"rw_{n}{g}") for g in range(3)] for n in ("mm", "ev", "eva"))
        xa_loaded, xa_stored, xa_scores, xa_max, xa_exp, xa_norm, xa_turned, xa_put, xa_out, xa_evac = (
            sem("xa_" + n) for n in ("loaded", "stored", "scores", "max", "exp", "norm", "turned", "put", "out",
                                     "evac"))
        end_turned, end_put, end_stored, end_put2 = (
            sem("end_" + n) for n in ("turned", "put", "stored", "put2"))
        fx_rows, shift_stored, memn_loaded, lo_w_loaded = (
            sem(n) for n in ("fx_rows", "shift_stored", "memn_loaded", "lo_w_loaded"))
        lam_summed, lf_ready_z, x_updated = sem("lam_summed"), sem("lf_ready_z"), sem("x_updated")
        y_ready, g_ready, x_done = sem("y_ready"), sem("g_ready"), sem("x_done")

        settled = sem("settled")
        NBAR = 10

        def settle(eng):
            eng.sem_inc(settled, 1)

        def phase_end(eng, l, k):
            settle(eng)
            eng.drain().then_inc(bar, 1)
            eng.wait_ge(bar, (l * NBAR + k + 1) * 4)
            settle(eng)

        def half(t, h):
            return t[:, h * HT:(h + 1) * HT]

        def mid(ap, n):
            return ap.rearrange("p (a n) -> p a n", a=1)

        block = ctx.enter_context(nc.Block())

        @block.sync
        def _(sp):
            with sp.Fori(0, DEPTH) as l:
                n = [0]
                last_use = [(split_done, l * SPLITS + 1)] * RING

                def unit(name, row, kn, col, use, width=P, branch=None):
                    pos = n[0] % RING
                    n[0] += 1
                    sp.wait_ge(*last_use[pos])
                    last_use[pos] = use
                    if branch is not None:
                        src = A[name][ds(l, 1), branch:branch + 1].rearrange("l i (k p) n -> p (l i k) n", p=P)
                    else:
                        src = A[name][ds(l, 1)].rearrange("l (k p) n -> p (l k) n", p=P)
                    sp.dma_start(ring[:, pos, 0:kn, 0:width],
                                 src[:, row:row + kn, col:col + width]).then_inc(slot_loaded[pos], 16)

                load = sp.dma_start

                def after_phase(k):
                    sp.wait_ge(bar, (l * NBAR + k + 1) * 4)

                def branch_loads():
                    sp.wait_ge(fx_rows, l + 1)
                    settle(sp)
                    with sp.Fori(0, FOX_HEADS // 2) as it:
                        g = sp.snap(l * 4 + it)
                        for h in range(2):
                            s = fx_loaded[h]
                            rows = lambda r: proj_d[ds(it * P + (r + 64 * h), 64), :]
                            hd = lambda name: A[name][ds(l, 1), :, :, ds(it * 2 + h, 1), :] \
                                .rearrange("l b (t p) h d -> p (l b t h) d", p=P)
                            sp.wait_ge(fx_free[h], g + 1)
                            load(FQ[0:64, h, :], rows(R_FQ)).then_inc(s, 16)
                            load(FQ[64:65, h, :], dcum_d[0, ds(it * 2 + h, 1), 0:T]).then_inc(s, 16)
                            load(FVR[0:64, h, :], rows(R_FV)).then_inc(s, 16)
                            load(FK[0:64, h, 0:T], rows(R_FK)).then_inc(s, 16)
                            load(FPK[:, h, :, :], hd("cache_fox_k")).then_inc(s, 16)
                            load(FK[65:66, h, :], dcum_d[1, ds(it * 2 + h, 1), :]).then_inc(s, 16)
                            load(FVT[:, h, 5:9, :], hd("cache_fox_v")).then_inc(s, 16)
                    after_phase(2)
                    load(ROPE, C_rope).then_inc(rope_loaded, 16)
                    with sp.Fori(0, DIFF_HEADS // 2) as it:
                        g = sp.snap(l * 2 + it)
                        for h in range(2):
                            s = df_loaded[h]
                            rows = lambda r: proj_d[ds(it * 256 + (r + P * h), P), :]
                            sp.wait_ge(df_free[h], g + 1)
                            load(DQ[:, h, :], rows(R_DQ)).then_inc(s, 16)
                            load(DK[:, h, 0:T], rows(R_DK)).then_inc(s, 16)
                            load(DVR[:, h, :], rows(R_DV)).then_inc(s, 16)
                            load(DPK[:, h, :, :], A["cache_diff_k"][ds(l, 1), :, :, ds(it * 2 + h, 1), :, :]
                                 .rearrange("l b (t p) h c d -> p (l b t h) (c d)", p=P)).then_inc(s, 16)
                            load(DVT[:, h, 5:9, :], A["cache_diff_v"][ds(l, 1), :, :, ds(it * 2 + h, 1), :]
                                 .rearrange("l b (t p) h d -> p (l b t h) d", p=P)).then_inc(s, 16)
                    after_phase(3)
                    for i in range(2):
                        r = R_RW + 1536 + P * i
                        load(LX[:, i, 1:SEQ + 1], proj_d[r:r + P, 0:SEQ]).then_inc(lo_loaded, 16)
                    r = R_RW + 1536
                    load(LX[:, :, SEQ + 2:T + 2], proj_d[r:r + 2 * P, SEQ:T].rearrange("(i p) t -> p i t", i=2)) \
                        .then_inc(lo_loaded, 16)
                    load(LW2[0:64, :], A["rwkv_w2"][ds(l, 1)].rearrange("l k n -> (l k) n")).then_inc(lo_w_loaded, 16)
                    load(LW2[64:128, :], A["rwkv_a2"][ds(l, 1)].rearrange("l k n -> (l k) n")) \
                        .then_inc(lo_w_loaded, 16)
                    load(LG2, A["rwkv_g2"][ds(l, 1)].rearrange("l k n -> (l k) n")).then_inc(lo_w_loaded, 16)
                    after_phase(4)
                    settle(sp)
                    with sp.Fori(0, RWKV_HEADS // 2) as it:
                        g = sp.snap(l * 4 + it)
                        sp.wait_ge(rw_free, g + 1)
                        for i in range(3):
                            rows = proj_d[ds(it * P + (R_RW + 512 * i), P), :]
                            load(W_RAW[:, i, 1:SEQ + 1], rows[:, 0:SEQ]).then_inc(rw_loaded, 16)
                            load(W_RAW[:, i, SEQ + 2:T + 2], rows[:, SEQ:T]).then_inc(rw_loaded, 16)
                        for i, t in enumerate((LWx, Ax, Gx)):
                            load(t[:, 0:T], proj_d[ds(it * P + (R_LW + 512 * i), P), :]).then_inc(rw_loaded, 16)
                        sp.wait_ge(rw_cleared, l + 1)
                        for h in range(2):
                            r = slice(64 * h, 64 * h + 64)
                            load(BDS[r, 11, 64 * h:64 * h + 64],
                                 A["state_rwkv"][ds(l, 1), :, ds(it * 2 + h, 1), :, :]
                                 .rearrange("l b h v k -> (l b h v) k")).then_inc(rw_loaded, 16)

                def tiles(g):
                    return tile_done, l * TILES + g

                def split(v):
                    return split_done, l * SPLITS + v + 2

                for j in range(38):
                    unit("w_in", 0, 8, P * j + (FOX_HEADS if j >= 12 else 0), split(j))
                unit("w_in", 0, 8, 1536, tiles(G_IN + 39), width=FOX_HEADS)
                gates = IN_WIDTH - 3 * D_MODEL
                for j in range(4):
                    for i in range(3):
                        v = V_MERGE + 12 * j + 4 * i
                        for m in range(2):
                            unit("w_in", 0, 8, gates + i * D_MODEL + 256 * j + P * m, split(v + m))
                        if (j, i) == (0, 1):
                            branch_loads()
                        for m in range(2):
                            unit("w_branch", 0, 4, 256 * j + P * m, split(v + 2 + m), branch=i)
                for j in range(8):
                    unit("w_out", 0, 8, P * j, split(V_OUT + j))
                for j in range(8):
                    unit("w_xkv", 0, 8, P * j, tiles(G_MEM + 2 * (j // 2) + 2))
                for j in range(4):
                    unit("w_xq", 0, 8, P * j, tiles(G_XQ + j + 1))
                for j in range(8):
                    unit("w_xo", 0, 4, P * j, tiles(G_XO + j + 1))
                for j in range(11):
                    for m in range(4):
                        unit("w_ffn_in", 0, 8, (m // 2) * FFN + 256 * j + P * (m % 2), split(V_FFI + 4 * j + m))
                for j in range(8):
                    k = 0
                    for part, kn in enumerate(FFO_SPLIT):
                        unit("w_ffn_out", k, kn, P * j, split(V_FFO + 3 * j + part))
                        k += kn
                assert n[0] == UNITS

        @block.tensor
        def _(pe):
            mm, tr = pe.matmul, pe.transpose
            pe.wait_ge(consts_loaded, 16)
            pe.wait_ge(consts_ready, 1)
            ident = const("ident")

            def setup():
                pe.wait_ge(x_loaded, 48)
                for a in range(KM):
                    if a >= 4:
                        pe.wait_ge(x_put_act, a - 3)
                        pe.wait_ge(x_put_dve, a - 3)
                    q = 2 * (a % 4)
                    for b in range(4):
                        tr(PS[:, q + b // 2, b % 2 * P:(b % 2 + 1) * P], xtok[:, b, a * P:(a + 1) * P], ident)
                    tr(PS[:, q + 1, 2 * P:2 * P + DEC_SEQ], xtok[0:DEC_SEQ, 4, a * P:(a + 1) * P],
                       ident[0:DEC_SEQ, 0:DEC_SEQ]).then_inc(setup_pe, 1)
                pe.wait_ge(mem_scaled, 1)
                for a in range(KM):
                    pe.wait_ge(x_put_act, KM + a - 3)
                    pe.wait_ge(x_put_dve, KM + a - 3)
                    for b in range(2):
                        ins = tr(PS[:, 2 * (a % 4) + b, 0:P], mtok[:, b, a * P:(a + 1) * P], ident)
                    ins.then_inc(setup_pe, 1)

            setup()

            def norm_sums(l, k):
                for h in range(2):
                    for a in range(KM):
                        if h == 0 and a % 2 == 0:
                            pe.wait_ge(sq_act, l * 24 + 4 * k + a // 2 + 1)
                        if h == 0 and a % 2 == 1:
                            pe.wait_ge(sq_dve, l * 24 + 4 * k + a // 2 + 1)
                        ins = mm(half(PS[:, h, :], 0), ones[:, :], half(SQ[:, a, :], h),
                                 start=(a == 0), stop=(a == KM - 1))
                ins.then_inc(sums_done, 1)

            def use_slot(l, n):
                pe.wait_ge(slot_loaded[n % RING], 16 * (l * USES[n % RING] + n // RING + 1))

            def freed(l, g, it=0, per=0):
                pe.wait_ge(tile_freed_act, l * TILES + g + 1 + it * per)
                pe.wait_ge(tile_freed_dve, l * TILES + g + 1 + it * per)

            def dense(l, g, q, n, kn, rhs, width=P):
                use_slot(l, n)
                freed(l, g)
                for k in range(kn):
                    for h in range(2):
                        ins = mm(PS[0:width, 2 * q + h, 0:HT], ring[:, n % RING, k, 0:width], rhs(k, h),
                                 start=(k == 0), stop=(k == kn - 1))
                ins.then_inc(tile_done, 1)

            def dense_split(l, g, q, v, rhs, first=True, last=True, it=0, per=0, per_v=None, need=None):
                pe.wait_ge(split_done, l * SPLITS + v + 2 + it * (per if per_v is None else per_v))
                if first:
                    freed(l, g, it, per)
                kn = depth_of(v)
                for k in range(kn):
                    if need is not None and k % 2 == 0:
                        pe.wait_ge(x_split, l * X_SPLITS + need + k // 2 + 1)
                    whi, wlo = (w[:, v % 2, k, :] for w in (WHI, WLO))
                    xhi, xlo = rhs(k)
                    for n, (w, x) in enumerate(((whi, xhi), (whi, xlo), (wlo, xhi))):
                        for h in range(2):
                            ins = mm(PS[:, 2 * q + h, 0:HT], w, half(x, h), start=(first and k == 0 and n == 0),
                                     stop=(last and k == kn - 1 and n == 2))
                ins.then_inc(tile_done if last else part_used, 1)

            def of_h(k, h):
                return half(hT[:, k, :], h)

            with pe.Fori(0, DEPTH) as l:
                pe.wait_ge(vec_loaded, (l + 1) * 16 * 19)
                tr(PS[:, 7, 0:NVEC], VR[0:NVEC, :], ident[0:NVEC, 0:NVEC]).then_inc(vec_turned, 1)
                norm_sums(l, 0)
                pe.wait_ge(h_ready, l * 24 + 8)
                phase_end(pe, l, 0)

                def in_tiles(it, j0, n):
                    for j in range(j0, j0 + n):
                        dense_split(l, G_IN + j, j % 4, j, lambda k: (HH[:, k, :], HL[:, k, :]), it=it, per=8,
                                    need=0 if j == 0 else None)

                with pe.Fori(0, 4) as it:
                    in_tiles(it, 0, 8)
                in_tiles(0, 32, 6)
                dense(l, G_IN + 38, 2, U_FORGET, 8, of_h, width=FOX_HEADS)
                pe.wait_ge(tile_freed_act, l * TILES + G_IN + 36 + 5)
                pe.wait_ge(tile_freed_dve, l * TILES + G_IN + 36 + 5)
                pe.wait_ge(plf_loaded, 16 * (l + 1))
                for b in range(4):
                    ins = tr(PS[0:8, 0, b * P:(b + 1) * P], PLF[:, b, :], ident)
                ins.then_inc(lf_turned, 1)
                pe.wait_ge(lf_ready, l + 1)
                settle(pe)
                for b in range(4):
                    tr(PS[:, 1, b * 8:(b + 1) * 8], AF[0:8, b * P:(b + 1) * P], ident[0:8, 0:8])
                tr(PS[0:DEC_SEQ, 1, 32:40], AF[0:8, SEQ:T], ident[0:8, 0:8]).then_inc(lf_turned, 1)
                phase_end(pe, l, 1)

                with pe.Fori(0, FOX_HEADS // 2) as it:
                    g = pe.snap(l * 4 + it)
                    job = [0]

                    def put_bank():
                        j = job[0]
                        job[0] += 1
                        pe.wait_ge(fx_put, g * 16 + j + 1)
                        settle(pe)
                        return PS[:, 4 + j % 2, :]

                    def fox_prologue(h):
                        pe.wait_ge(fx_loaded[h], (g + 1) * 16 * 7)
                        b = put_bank()
                        for t in range(5):
                            w = P if t < 4 else DEC_SEQ
                            ins = tr(b[0:w, t * 64:(t + 1) * 64], FVR[0:64, h, t * P:t * P + w], ident[0:64, 0:64])
                        ins.then_inc(fx_turned, 1)
                        b = put_bank()
                        for t in range(5):
                            w = P if t < 4 else DEC_SEQ
                            ins = tr(b[0:w, t * 64:(t + 1) * 64], FK[0:64, h, t * P:t * P + w], ident[0:64, 0:64])
                        ins.then_inc(fx_turned, 1)
                        b = put_bank()
                        for t in range(4):
                            ins = tr(b[0:64, t * P:(t + 1) * P], FPK[:, h, t, :], ident)
                        ins.then_inc(fx_turned, 1)

                    def fox_scores(k):
                        h, i = divmod(k, 5)
                        if i == 0:
                            pe.wait_ge(fx_scaled, g * 2 + h + 1)
                            pe.wait_ge(fx_put, g * 16 + (3, 8)[h] + 2)
                        if k >= 2:
                            pe.wait_ge(fx_exp, g * 10 + k - 1)
                        b = 2 * (k % 2)
                        if i < 4:
                            n = (i + 1) * P
                            q = FQ[0:66, h, i * P:(i + 1) * P]
                            mm(PS[:, b, 0:n], q, FK[0:66, h, 0:n], start=True, stop=False)
                            ins = mm(PS[:, b, n - P:n], identb[:, :], mfoxb[:, :], start=False, stop=True)
                        else:
                            q = FQ[0:66, h, SEQ:T]
                            mm(PS[0:32, b, :], q, FK[0:66, h, T:T + PAST], start=True, stop=True)
                            mm(PS[0:32, b + 1, 0:32], q, FK[0:66, h, SEQ:T], start=True, stop=False)
                            ins = mm(PS[0:32, b + 1, 0:32], identb[0:32, 0:32], mfoxb[0:32, 0:32], start=False,
                                     stop=True)
                        ins.then_inc(fx_scores, 1)

                    def fox_turn(k):
                        i = k % 5
                        pe.wait_ge(fx_norm, g * 10 + k + 1)
                        b = put_bank()
                        if i < 4:
                            for t in range(i + 1):
                                ins = tr(b[:, t * P:(t + 1) * P], FP[:, k % 2, t * P:(t + 1) * P], ident)
                        else:
                            for t in range(5):
                                w = P if t < 4 else DEC_SEQ
                                ins = tr(b[0:w, t * 32:(t + 1) * 32], FP[0:32, k % 2, t * P:t * P + w],
                                         ident[0:32, 0:32])
                        ins.then_inc(fx_turned, 1)

                    jobs_of = []

                    def fox_values(k):
                        h, i = divmod(k, 5)
                        pe.wait_ge(fx_put, g * 16 + jobs_of[k] + 1 + 2)
                        if i == 0:
                            pe.wait_ge(fx_evac, g * 2 + h + 1)
                        o = slice(64 * h, 64 * h + 64)
                        if i < 4:
                            for t in range(i + 1):
                                ins = mm(PS[o, 6, i * P:(i + 1) * P], FVT[:, h, t, :],
                                         FPT[:, k % 2, t * P:(t + 1) * P], start=(t == 0), stop=(t == i))
                        else:
                            for t in range(4):
                                mm(PS[o, 7, 0:32], FVT[:, h, 5 + t, :], FPT[:, k % 2, t * 32:(t + 1) * 32],
                                   start=(t == 0), stop=False)
                            ins = mm(PS[o, 7, 0:32], FVT[0:32, h, 4, :], FPT[0:32, k % 2, 128:160], start=False,
                                     stop=True)
                            ins.then_inc(fx_out, 1)

                    for k in range(12):
                        if k == 0:
                            fox_prologue(0)
                        if k == 3:
                            fox_prologue(1)
                        if k < 10:
                            fox_scores(k)
                        if 1 <= k <= 10:
                            jobs_of.append(job[0])
                            fox_turn(k - 1)
                        if k >= 2:
                            fox_values(k - 2)
                phase_end(pe, l, 2)

                with pe.Fori(0, DIFF_HEADS // 2) as it:
                    g = pe.snap(l * 2 + it)
                    for h in range(2):
                        pe.wait_ge(df_loaded[h], (g + 1) * 16 * 5)
                        for i, src in enumerate((DQ, DK)):
                            if i == 0:
                                pe.wait_ge(df_evac, g * 2 + h + 1)
                            for s in range(2):
                                ins = mm(PS[:, 2 * i + s, 0:HT], const("rot"), half(src[:, h, :], s), start=True,
                                         stop=True)
                            ins.then_inc(df_rot, 1)
                        for t in range(4):
                            ins = tr(PS[:, 4, t * P:(t + 1) * P], DVR[:, h, t * P:(t + 1) * P], ident)
                        ins.then_inc(df_turned, 1)
                        for t in range(4):
                            ins = tr(PS[:, 5, t * P:(t + 1) * P], DPK[:, h, t, :], ident)
                        ins.then_inc(df_turned, 1)
                        pe.wait_ge(df_rotated, g * 4 + 2 * h + 2)
                        pe.wait_ge(df_put, g * 18 + 9 * h + 1)
                        for t in range(4):
                            ins = tr(PS[:, 4, t * P:(t + 1) * P], DK[:, h, t * P:(t + 1) * P], ident)
                        ins.then_inc(df_turned, 1)
                        pe.wait_ge(df_put, g * 18 + 9 * h + 2)
                        tr(PS[0:32, 5, 0:P], DVR[:, h, SEQ:T], ident)
                        tr(PS[0:32, 5, P:2 * P], DK[:, h, SEQ:T], ident).then_inc(df_turned, 1)
                        pe.wait_ge(df_put, g * 18 + 9 * h + 4)

                        def scores(i):
                            if i >= 1:
                                pe.wait_ge(df_exp, g * 20 + 10 * h + 2 * i)
                                settle(pe)
                            for c in range(2):
                                r = slice(64 * c, 64 * c + 64)
                                b = 2 * c
                                if i < 4:
                                    n = (i + 1) * P
                                    mm(PS[:, b, 0:n], DQ[r, h, i * P:(i + 1) * P], DK[r, h, 0:n], start=True,
                                       stop=False)
                                    ins = mm(PS[:, b, n - P:n], identb[:, :], mdiffb[:, :], start=False, stop=True)
                                else:
                                    mm(PS[0:32, b, :], DQ[r, h, SEQ:T], DK[r, h, T:T + PAST], start=True, stop=True)
                                    ins = mm(PS[0:32, b + 1, 0:32], DQ[r, h, SEQ:T], DK[r, h, SEQ:T], start=True,
                                             stop=True)
                                ins.then_inc(df_scores, 1)

                        def turn(i):
                            pe.wait_ge(df_comb, g * 10 + 5 * h + i + 1)
                            pe.wait_ge(df_put, g * 18 + 9 * h + 4 + max(i - 1, 0))
                            settle(pe)
                            b = PS[:, 4 + i % 2, :]
                            if i < 4:
                                for t in range(i + 1):
                                    ins = tr(b[:, t * P:(t + 1) * P], DPB[:, i % 2, 0, t * P:(t + 1) * P], ident)
                            else:
                                for t in range(5):
                                    w = P if t < 4 else DEC_SEQ
                                    ins = tr(b[0:w, t * 32:(t + 1) * 32], DPB[0:32, 0, 0, t * P:t * P + w],
                                             ident[0:32, 0:32])
                            ins.then_inc(df_turned, 1)

                        def values(i):
                            pe.wait_ge(df_put, g * 18 + 9 * h + 4 + i + 1)
                            if i < 4:
                                for t in range(i + 1):
                                    ins = mm(PS[:, 6, i * P:(i + 1) * P], DVT[:, h, t, :],
                                             DPT[:, i % 2, t * P:(t + 1) * P], start=(t == 0), stop=(t == i))
                            else:
                                for t in range(4):
                                    mm(PS[:, 7, 0:32], DVT[:, h, 5 + t, :], DPT[:, 0, t * 32:(t + 1) * 32],
                                       start=(t == 0), stop=False)
                                ins = mm(PS[:, 7, 0:32], DVT[0:32, h, 4, :], DPT[0:32, 0, 128:160], start=False,
                                         stop=True)
                                ins.then_inc(df_out, 1)

                        for k in range(7):
                            if k < 5:
                                scores(k)
                            if 1 <= k <= 5:
                                turn(k - 1)
                            if k >= 2:
                                values(k - 2)
                        pe.wait_ge(df_sq, g * 2 + h + 1)
                        for s in range(2):
                            ins = mm(PS[:, s, 0:HT], ones[:, :], half(DTMP, s), start=True, stop=True)
                        ins.then_inc(df_sum, 1)
                phase_end(pe, l, 3)

                pe.wait_ge(lo_act, l + 1)
                pe.wait_ge(lo_loaded, (l + 1) * 16 * 3)
                pe.wait_ge(lo_w_loaded, (l + 1) * 16 * 3)
                for p in range(4):
                    c = slice(p * P, (p + 1) * P)
                    for i, (w, x) in enumerate(((LW2[0:64, c], LXS[0:64, 0, :]), (LW2[64:128, c], LXS[64:128, 0, :]),
                                                (LG2[:, c], LXS[:, 1, :]))):
                        j = 3 * p + i
                        if j >= 4:
                            pe.wait_ge(lo_evac_act, l * 12 + j - 3)
                        for s in range(2):
                            ins = mm(PS[:, 2 * (j % 4) + s, 0:HT], w, half(x, s), start=True, stop=True)
                        ins.then_inc(lo_done, 1)
                phase_end(pe, l, 4)

                with pe.Fori(0, RWKV_HEADS // 2) as it:
                    g = pe.snap(l * 4 + it)
                    hp = TP // 2

                    def sums(src):
                        for s in range(2):
                            ins = mm(PS[:, 6 + s, 0:hp], const("bdones"), src[:, s * hp:(s + 1) * hp], start=True,
                                     stop=True)
                        return ins

                    pe.wait_ge(rw_in, g * 2 + 1)
                    sums(W_RAW[:, 0, :]).then_inc(rw_sum, 1)
                    pe.wait_ge(rw_in, g * 2 + 2)
                    sums(W_RAW[:, 2, :]).then_inc(rw_sum, 1)

                    def three(gr, bank, at, step, pairs):
                        for c in range(3):
                            for n, (w, x) in enumerate(pairs):
                                x_c = x(c)
                                ins = mm(PS[:, bank, at + step * c:at + step * c + x_c.shape[-1]], w(c), x_c,
                                         start=(n == 0), stop=(n == len(pairs) - 1))
                        return ins

                    def stage(s, gr):
                        bd = lambda i: (lambda c: BD[gr][i][:, c, :])
                        pl = lambda i: (lambda c: PL[gr][i][:, c, :])
                        X1, X2, Ao, GTt, HTt, Vt, Bt = range(7)
                        rt = X2
                        b0, b1 = 2 * gr, 2 * gr + 1
                        ch = lambda c: 3 * gr + c
                        pe.wait_ge(rw_ev[gr], g * 12 + s)
                        pe.wait_ge(rw_eva[gr], g * 12 + s)
                        if s == 1:
                            pe.wait_ge(rw_bd, g * 3 + gr + 1)
                            three(gr, b0, 0, 128, [(bd(0), lambda c: KR[:, ch(c), :])])
                            ins = three(gr, b1, 0, 128, [(bd(1), lambda c: KR[:, ch(c), :])])
                        st = lambda c: const("stack")[:, 0:64]
                        if s == 2:
                            three(gr, b0, 0, 64, [(bd(2), lambda c: BE[:, ch(c), :])])
                            three(gr, b0, 192, 64, [(bd(3), st)])
                            three(gr, b1, 0, 64, [(bd(2), st)])
                            ins = three(gr, b1, 192, 64, [(bd(0), st)])
                        if s == 3:
                            three(gr, b0, 0, 64, [(bd(5), pl(Vt))])
                            three(gr, b0, 192, 64, [(bd(1), st)])
                            three(gr, b1, 0, 64, [(bd(3), pl(X1))])
                            ins = three(gr, b1, 192, 64, [(bd(0), pl(X2))])
                        if s == 4:
                            three(gr, b0, 0, 128, [(bd(3), lambda c: PZ[gr][:, c, :])])
                            ins = three(gr, b1, 0, 64, [(bd(2), pl(X2))])
                        if s == 5:
                            three(gr, b0, 0, 64, [(bd(1), lambda c: PZ[gr][:, c, 64:128])])
                            ins = three(gr, b1, 0, 64, [(bd(0), pl(X2))])
                        if s == 6:
                            ins = three(gr, b0, 0, 64, [(bd(2), lambda c: PZ[gr][:, c, 64:128])])
                        if s == 7:
                            three(gr, b0, 0, 64, [(bd(4), lambda c: PZ[gr][:, c, 64:128])])
                            three(gr, b0, 192, 64, [(bd(0), pl(Ao))])
                            ins = three(gr, b1, 0, 128, [(bd(0), lambda c: WW[gr][:, c, :])])
                        if s == 8:
                            three(gr, b0, 0, 64, [(bd(2), pl(X1))])
                            ins = three(gr, b1, 0, 128, [(bd(1), lambda c: WW[gr][:, c, :])])
                        if s == 9:
                            ins = three(gr, b1, 0, 128, [(bd(3), lambda c: WW[gr][:, c, :])])
                        if s == 10:
                            three(gr, b0, 0, 64, [(bd(0), pl(GTt))])
                            ins = three(gr, b0, 192, 64, [(bd(0), pl(Bt))])
                        if s == 11:
                            ins = three(gr, b1, 0, 64, [(bd(1), pl(GTt)), (bd(7), pl(HTt)),
                                                        (lambda c: BDS[:, ch(c), :], pl(rt))])
                        ins.then_inc(rw_mm[gr], 1)

                    for s in range(1, 11):
                        for gr in range(3):
                            stage(s, gr)
                    tr(PS[:, 7, 256:384], BDS[:, 11, :], ident).then_inc(rw_state, 1)
                    for c in range(9):
                        gr, cc = divmod(c, 3)
                        if cc == 0:
                            pe.wait_ge(rw_ev[gr], g * 12 + 11)
                            pe.wait_ge(rw_eva[gr], g * 12 + 11)
                        if c >= 1:
                            pe.wait_ge(rw_chain, g * 10 + c)
                        o = PS[:, 6 + c % 2, 0:P]
                        mm(o, BD[gr][6][:, cc, :], BD[gr][1][:, cc, :], start=True, stop=False)
                        mm(o, BD[gr][8][:, cc, :], BD[gr][7][:, cc, :], start=False, stop=False)
                        if 1 <= c < 8:
                            pe.wait_ge(rw_chain, g * 10 + c + 1)
                        mm(o, BD[gr][2][:, cc, :], BDS[:, c, :], start=False, stop=True).then_inc(rw_state, 1)
                    for gr in range(3):
                        stage(11, gr)
                    pe.wait_ge(rw_chain, g * 10 + 10)
                    tr(PS[:, 7, 0:P], BDS[:, 9, :], ident)
                    tr(PS[:, 7, P:2 * P], BDS[:, 10, :], ident).then_inc(rw_final, 1)
                    pe.wait_ge(rw_fin, g + 1)
                    pe.wait_ge(rp_y, g + 1)
                    sums(Yx).then_inc(rp_mean, 1)
                    pe.wait_ge(rp_sq, g + 1)
                    sums(W_RAW[:, 0, :]).then_inc(rp_var, 1)
                    pe.wait_ge(rp_done, g + 1)
                phase_end(pe, l, 5)

                def of_branch(i):
                    return lambda k: (BH[:, 4 * i + k, :], brTR[:, 4 * i + k, :])

                with pe.Fori(0, 2) as it:
                    for n in range(24):
                        i = n % 12 // 4
                        if n % 4 < 2:
                            dense_split(l, G_MERGE + n, n % 4, V_MERGE + n, lambda k: (HX[:, k, :], hTR[:, k, :]),
                                        it=it, per=24, need=4 if n == 0 else None)
                        else:
                            dense_split(l, G_MERGE + n, n % 4, V_MERGE + n, of_branch(i), it=it, per=24,
                                        need=8 + 2 * i if n % 4 == 2 and n < 12 else None)
                pe.wait_ge(y_ready, l + 1)
                for n in range(N_OUT):
                    dense_split(l, G_OUT + n, n % 4, V_OUT + n, lambda k: (YH[:, k, :], YL[:, k, :]))
                phase_end(pe, l, 6)
                norm_sums(l, 1)
                pe.wait_ge(rstd_ready, l * 6 + 2)
                norm_sums(l, 2)

                pe.wait_ge(mem_scaled, l + 2)
                pe.wait_ge(h_ready, l * 24 + 16)
                for s in range(4):
                    for u in range(2):
                        use_slot(l, U_MEM + 2 * s + u)
                    for t in range(2):
                        n = 2 * s + t
                        freed(l, G_MEM + n)
                        for u in range(2):
                            for k in range(8):
                                ins = mm(PS[:, 2 * (n % 4), u * P:(u + 1) * P], MNT[:, k, t * P:(t + 1) * P],
                                         ring[:, (U_MEM + 2 * s + u) % RING, k, :], start=(k == 0), stop=(k == 7))
                        ins.then_inc(tile_done, 1)
                for n in range(N_XQ):
                    dense(l, G_XQ + n, n % 4, U_XQ + n, 8, of_h)
                phase_end(pe, l, 7)
                pe.wait_ge(xa_loaded, (l + 1) * 32)
                for j in range(8):
                    grp, h = divmod(j, 4)
                    if j >= 2:
                        pe.wait_ge(xa_put, l * 28 + j - 1)
                    for t in range(2):
                        src = MKV[:, t, h * P:(h + 1) * P] if grp == 0 else CKT[:, t, h * P:(h + 1) * P]
                        ins = tr(PS[:, 4 + j % 2, t * P:(t + 1) * P], src, ident)
                    ins.then_inc(xa_turned, 1)
                pe.wait_ge(xa_put, l * 28 + 8)

                def x_scores(k):
                    h, i = divmod(k, 5)
                    if k >= 2:
                        pe.wait_ge(xa_exp, l * 20 + k - 1)
                    b, m = 2 * (k % 2), (P if i < 4 else DEC_SEQ)
                    mm(PS[0:m, b, 0:N_MEM], QX[:, h, i * P:i * P + m], MKT[:, i // 4, h, :], start=True,
                       stop=True).then_inc(xa_scores, 1)

                def x_turn(k):
                    pe.wait_ge(xa_norm, l * 20 + k + 1)
                    pe.wait_ge(xa_put, l * 28 + 8 + max(k - 1, 0))
                    settle(pe)
                    m = P if k % 5 < 4 else DEC_SEQ
                    for t in range(2):
                        ins = tr(PS[:, 4 + k % 2, t * P:t * P + m], XP[0:m, k % 2, t * P:(t + 1) * P],
                                 ident[0:m, 0:m])
                    ins.then_inc(xa_turned, 1)

                def x_values(k):
                    h, i = divmod(k, 5)
                    pe.wait_ge(xa_put, l * 28 + 8 + k + 1)
                    if i == 0 and h >= 1:
                        pe.wait_ge(xa_evac, l * 4 + h)
                    m = P if i < 4 else DEC_SEQ
                    for t in range(2):
                        v = MKV[:, t, 512 + h * P:512 + (h + 1) * P] if i < 4 else CVT[:, t, h * P:(h + 1) * P]
                        ins = mm(PS[:, 6 + i // 4, (i % 4) * P:(i % 4) * P + m], v, XPT[:, k % 2, t * P:t * P + m],
                                 start=(t == 0), stop=(t == 1))
                    if i == 4:
                        ins.then_inc(xa_out, 1)

                for k in range(22):
                    if k < 20:
                        x_scores(k)
                    if 1 <= k <= 20:
                        x_turn(k - 1)
                    if k >= 2:
                        x_values(k - 2)
                pe.wait_ge(xa_evac, l * 4 + 4)
                for n in range(N_XO):
                    dense(l, G_XO + n, n % 4, U_XO + n, 4, lambda k, h: half(OX[:, k, :], h))
                phase_end(pe, l, 8)
                norm_sums(l, 3)
                pe.wait_ge(rstd_ready, l * 6 + 4)
                norm_sums(l, 4)

                def ffn_in(it, n0, n_tiles):
                    for n in range(n0, n0 + n_tiles):
                        dense_split(l, G_FFI + n, n % 4, V_FFI + n, lambda k: (HF[:, k, :], hTR[:, k, :]), it=it, per=8,
                                    need=14 if n == 0 else None)

                with pe.Fori(0, 5) as it:
                    ffn_in(it, 0, 8)
                ffn_in(0, 40, 4)
                pe.wait_ge(g_ready, l + 1)
                settle(pe)
                with pe.Fori(0, 2) as it:
                    for n in range(4):
                        k0 = 0
                        for part, kn in enumerate(FFO_SPLIT):
                            dense_split(l, G_FFO + n, n, V_FFO + 3 * n + part,
                                        lambda k, k0=k0: (GH[:, k0 + k, :], GL[:, k0 + k, :]), first=(part == 0),
                                        last=(part == 2), it=it, per=4, per_v=12)
                            k0 += kn
                phase_end(pe, l, 9)
                norm_sums(l, 5)
                pe.wait_ge(x_done, l + 1)
                settle(pe)

            for b in range(5):
                w = P if b < 4 else DEC_SEQ
                for c in range(2):
                    j = 2 * b + c
                    if j >= 4:
                        pe.wait_ge(end_put, j - 3)
                    for a in range(4):
                        ins = tr(PS[0:w, j % 4, a * P:(a + 1) * P], xT[:, 4 * c + a, b * P:b * P + w], ident)
                    ins.then_inc(end_turned, 1)

        @block.scalar
        def _(act):
            def f(out, in_, func, **kw):
                return act.activation(out, in_, func, **kw)

            def copy(out, in_):
                return act.copy(out, in_)

            act.sem_inc(tile_freed_act, 4)
            act.sem_inc(fx_put, 2)
            act.wait_ge(consts_ready, 1)
            act.wait_ge(x_loaded, 48)
            for t in range(2):
                f(SQ[:, 2 * t, :], mtok[:, t, 0:T], ACT.Square,
                  accum_out=small[:, 2 * t:2 * t + 1])
                f(SQ[:, 2 * t + 1, 0:D_MODEL - T], mtok[:, t, T:D_MODEL], ACT.Square,
                  accum_out=small[:, 2 * t + 1:2 * t + 2])
            act.drain().then_inc(setup_act, 1)
            act.wait_ge(setup_act, 2)
            f(small[:, 6:8], small[:, 4:6], ACT.Ln, scale=1.0 / D_MODEL, bias=eps[:, 0:1])
            act.drain()
            f(small[:, 8:10], small[:, 6:8], ACT.Exp, scale=-0.5)
            act.drain().then_inc(setup_act, 1)
            for a in range(KM):
                act.wait_ge(setup_pe, a + 1)
                copy(xT[:, a, 0:2 * P], PS[:, 2 * (a % 4), 0:2 * P]).then_inc(x_put_act, 1)
            for a in range(KM):
                act.wait_ge(setup_pe, KM + a + 1)
                copy(mnT[:, a, 0:P], PS[:, 2 * (a % 4), 0:P]).then_inc(x_put_act, 1)

            def norm_squares(l, k, src):
                for a in range(0, KM, 2):
                    f(SQ[:, a, :], src[:, a, :], ACT.Square).then_inc(sq_act, 1)

            def norm_rstd(l, k):
                act.wait_ge(sums_done, l * 6 + k + 1)
                for h in range(2):
                    f(half(RS, h), PS[:, h, 0:HT], ACT.Ln, scale=1.0 / D_MODEL, bias=eps[:, 0:1])
                act.drain()
                f(RS, RS, ACT.Exp, scale=-0.5)
                act.drain().then_inc(rstd_ready, 1)

            def tile(l, g, it=0, per=0):
                act.wait_ge(tile_done, l * TILES + g + 1 + it * per)

            with act.Fori(0, DEPTH) as l:
                act.wait_ge(vec_turned, l + 1)
                copy(VT[:, 0:NVEC], PS[:, 7, 0:NVEC])
                act.wait_ge(lam_summed, l + 1)
                f(small[:, 14:16], small[:, 12:14], ACT.Exp)
                act.drain().then_inc(vec_ready, 1)
                norm_squares(l, 0, xT)
                norm_rstd(l, 0)
                phase_end(act, l, 0)
                def in_tiles(it, j0, n):
                    for j in range(n):
                        s = j % 2
                        act.wait_ge(est_free, l * 19 + j0 + j + 1 + it * 4)
                        for m in range(2):
                            n_ = 2 * (j0 + j) + m
                            tile(l, G_IN + n_, it, 8)
                            copy(half(EST[:, s, m, :], 0), PS[:, 2 * ((2 * j + m) % 4), 0:HT]) \
                                .then_inc(tile_freed_act, 1)

                with act.Fori(0, 4) as it:
                    in_tiles(it, 0, 4)
                in_tiles(0, 16, 3)
                act.wait_ge(lf_ready_z, l + 1)
                f(TZ[0:8, 1, :], TZ[0:8, 0, :], ACT.Abs)
                act.drain()
                f(TZ[0:8, 1, :], TZ[0:8, 1, :], ACT.Exp, scale=-1.0)
                act.drain()
                f(TZ[0:8, 1, :], TZ[0:8, 1, :], ACT.Ln, bias=1.0)
                act.drain().then_inc(tile_freed_act, 1)
                act.wait_ge(lf_turned, 2 * l + 2)
                copy(LFT[:, 0:4, :].rearrange("p a b -> p (a b)"), PS[:, 1, 0:32])
                copy(LFT[0:DEC_SEQ, 4, :], PS[0:DEC_SEQ, 1, 32:40])
                act.drain().then_inc(lf_put, 1)
                phase_end(act, l, 1)

                with act.Fori(0, FOX_HEADS // 2) as it:
                    g = act.snap(l * 4 + it)
                    job = [0]

                    def next_job():
                        j = job[0]
                        job[0] += 1
                        act.wait_ge(fx_turned, g * 16 + j + 1)
                        return PS[:, 4 + j % 2, :]

                    def fox_prologue(h):
                        for to in (FVT, FKT):
                            b = next_job()
                            copy(to[:, h, 0:4, :].rearrange("p a b -> p (a b)"), b[:, 0:256])
                            copy(to[0:DEC_SEQ, h, 4, :], b[0:DEC_SEQ, 256:320])
                            act.drain().then_inc(fx_put, 1)
                        b = next_job()
                        copy(FK[0:64, h, T:T + PAST], b[0:64, :]).then_inc(fx_put, 1)

                    def fox_exp(k):
                        i = k % 5
                        act.wait_ge(fx_max, g * 10 + k + 1)
                        m, n = (P, (i + 1) * P) if i < 4 else (DEC_SEQ, T)
                        f(FP[0:m, k % 2, 0:n], pair(k % 2)[0:m, 0:n], ACT.Exp, bias=FST[0:m, k % 2, 0:1],
                          accum_out=FST[0:m, k % 2, 1:2])
                        act.drain().then_inc(fx_exp, 1)

                    def fox_put(k):
                        i = k % 5
                        b = next_job()
                        if i < 4:
                            copy(FPT[:, k % 2, 0:(i + 1) * P], b[:, 0:(i + 1) * P]).then_inc(fx_put, 1)
                        else:
                            copy(FPT[:, k % 2, 0:P], b[:, 0:P])
                            copy(FPT[0:32, k % 2, P:P + 32], b[0:32, P:P + 32])
                            act.drain().then_inc(fx_put, 1)

                    for k in range(11):
                        if k == 0:
                            fox_prologue(0)
                        if k == 3:
                            fox_prologue(1)
                        if k < 10:
                            fox_exp(k)
                        if k >= 1:
                            fox_put(k - 1)
                phase_end(act, l, 2)

                with act.Fori(0, DIFF_HEADS // 2) as it:
                    g = act.snap(l * 2 + it)
                    for h in range(2):
                        act.wait_ge(df_turned, g * 18 + 9 * h + 1)
                        copy(DVT[:, h, 0:4, :].rearrange("p a b -> p (a b)"), PS[:, 4, :]).then_inc(df_put, 1)
                        act.wait_ge(df_turned, g * 18 + 9 * h + 2)
                        copy(DK[:, h, T:T + PAST], PS[:, 5, :]).then_inc(df_put, 1)
                        act.wait_ge(df_turned, g * 18 + 9 * h + 3)
                        copy(DKT[:, h, 0:4, :].rearrange("p a b -> p (a b)"), PS[:, 4, :]).then_inc(df_put, 1)
                        act.wait_ge(df_turned, g * 18 + 9 * h + 4)
                        copy(DVT[0:32, h, 4, :], PS[0:32, 5, 0:P])
                        copy(DKT[0:32, h, 4, :], PS[0:32, 5, P:2 * P])
                        act.drain().then_inc(df_put, 1)
                        for k in range(6):
                            if k < 5:
                                m, n = (P, (k + 1) * P) if k < 4 else (DEC_SEQ, T)
                                for c in range(2):
                                    act.wait_ge(df_max, g * 20 + 10 * h + 2 * k + c + 1)
                                    f(DPB[0:m, k % 2, c, 0:n], pair(c)[0:m, 0:n], ACT.Exp,
                                      bias=DST[0:m, k % 2, c:c + 1], accum_out=DST[0:m, k % 2, 2 + c:3 + c])
                                    act.drain().then_inc(df_exp, 1)
                            if k >= 1:
                                i = k - 1
                                act.wait_ge(df_turned, g * 18 + 9 * h + 4 + k)
                                b = PS[:, 4 + i % 2, :]
                                if i < 4:
                                    copy(DPT[:, i % 2, 0:(i + 1) * P], b[:, 0:(i + 1) * P]).then_inc(df_put, 1)
                                else:
                                    copy(DPT[:, 0, 0:P], b[:, 0:P])
                                    copy(DPT[0:32, 0, P:P + 32], b[0:32, P:P + 32])
                                    act.drain().then_inc(df_put, 1)
                        act.wait_ge(df_out, g * 2 + h + 1)
                        f(DTMP, pair(3)[:, 0:T], ACT.Square).then_inc(df_sq, 1)
                        act.wait_ge(df_sum, g * 2 + h + 1)
                        for s in range(2):
                            f(half(DRS, s), PS[:, s, 0:HT], ACT.Ln, scale=1.0 / P, bias=eps[:, 0:1])
                        act.drain()
                        f(DRS, DRS, ACT.Exp, scale=-0.5)
                        act.drain().then_inc(df_rs, 1)
                phase_end(act, l, 3)

                act.wait_ge(lo_mixed, l + 1)
                f(LXS[0:64, 0, :], LXS[0:64, 0, :], ACT.Tanh)
                f(LXS[:, 1, :], LXS[:, 1, :], ACT.Sigmoid)
                act.drain().then_inc(lo_act, 1)
                for p in range(4):
                    for i in range(3):
                        j = 3 * p + i
                        act.wait_ge(lo_done, l * 12 + j + 1)
                        for s in range(2):
                            src, to = PS[:, 2 * (j % 4) + s, 0:HT], half(LO[:, 4 * i + p, :], s)
                            if i == 0:
                                f(to, src, ACT.Sigmoid, bias=vec("rwkv_w0", p))
                            elif i == 1:
                                f(to, src, ACT.Sigmoid, bias=vec("rwkv_a0", p))
                            else:
                                copy(to, src)
                        act.drain().then_inc(lo_evac_act, 1)
                phase_end(act, l, 4)

                with act.Fori(0, RWKV_HEADS // 2) as it:
                    g = act.snap(l * 4 + it)
                    KX = W_RAW[:, 0, :]
                    act.wait_ge(rw_clip, g * 2 + 1)
                    f(KX, KX, ACT.Ln)
                    act.drain()
                    f(KX, KX, ACT.Exp, scale=-0.5, bias=eps[:, 2:3])
                    act.wait_ge(rw_clip, g * 2 + 2)
                    f(WWA[:, 0, :], PZA[:, 0, :], ACT.Exp)
                    f(WWA[:, 1, :], PZA[:, 0, :], ACT.Exp, scale=-1.0)
                    f(PZA[:, 1, :], PZA[:, 1, :], ACT.Exp)
                    act.drain().then_inc(rw_exps, 1)

                    def bd(gr, slot, src):
                        copy(BD[gr][slot][0:64, :, 0:64], src[0:64])
                        copy(BD[gr][slot][64:128, :, 64:128], src[64:128])

                    def evac(s, gr):
                        X1, X2, Ao, GTt, HTt, Vt, Bt = range(7)
                        rt = X2

                        def bank(i, at):
                            return PS[:, 2 * gr + i, at:at + 192].rearrange("p (c n) -> p c n", c=3)

                        act.wait_ge(rw_mm[gr], g * 11 + s)
                        act.wait_ge(rw_ev[gr], g * 12 + s + 1)
                        if s in (1, 6, 10):
                            act.sem_inc(rw_eva[gr], 1)
                            return
                        if s == 2:
                            bd(gr, 6, bank(1, 192))
                            bd(gr, 7, bank(0, 192))
                            bd(gr, 0, PL[gr][X1])
                        if s == 3:
                            bd(gr, 8, bank(0, 192))
                            bd(gr, 2, bank(1, 0))
                            bd(gr, 3, bank(1, 192))
                            bd(gr, 4, PL[gr][Ao])
                        if s == 4:
                            bd(gr, 0, PS[:, 2 * gr, 0:384].rearrange("p (c n) -> p c n", c=3)[:, :, 0:64])
                            bd(gr, 1, bank(1, 0))
                        if s == 5:
                            bd(gr, 2, bank(1, 0))
                        if s == 7:
                            bd(gr, 1, bank(0, 0))
                            bd(gr, 2, bank(0, 192))
                        if s == 8:
                            bd(gr, 3, bank(0, 0))
                        if s == 9:
                            bd(gr, 0, WW[gr][:, :, 0:64])
                            bd(gr, 1, WW[gr][:, :, 64:128])
                        act.drain().then_inc(rw_eva[gr], 1)

                    for gr in range(3):
                        act.wait_ge(rw_ev[gr], g * 12 + 1)
                        bd(gr, 0, BE[:, 3 * gr:3 * gr + 3, :])
                        bd(gr, 1, KH[:, 3 * gr:3 * gr + 3, :])
                        act.drain().then_inc(rw_eva[gr], 1)
                    for s in range(1, 11):
                        for gr in range(3):
                            evac(s, gr)
                    for gr in range(3):
                        act.sem_inc(rw_eva[gr], 1)
                    act.wait_ge(rw_final, g + 1)
                    copy(XS.rearrange("p a b -> p (a b)"), PS[:, 7, 0:2 * P])
                    act.drain().then_inc(rw_fin, 1)
                    act.wait_ge(rp_yc, g + 1)
                    f(W_RAW[:, 0, :], Yx, ACT.Square).then_inc(rp_sq, 1)
                    act.wait_ge(rp_var, g + 1)
                    for s in range(2):
                        f(W_RAW[:, 0, s * (TP // 2):(s + 1) * (TP // 2)], PS[:, 6 + s, 0:TP // 2], ACT.Ln,
                          scale=1.0 / HEAD_DIM, bias=eps[:, 1:2])
                    act.drain()
                    f(W_RAW[:, 0, :], W_RAW[:, 0, :], ACT.Exp, scale=-0.5)
                    act.drain().then_inc(rp_rs, 1)
                phase_end(act, l, 5)

                with act.Fori(0, 2) as it:
                    for s in range(0, 12, 2):
                        for m in range(2):
                            n = 2 * s + m
                            tile(l, G_MERGE + n, it, 24)
                            for h in range(2):
                                ins = f(half(SG[:, (s + m) % 4, :], h), PS[:, 2 * (n % 4) + h, 0:HT], ACT.Sigmoid)
                            act.drain().then_inc(tile_freed_act, 1 if m == 0 else 3)
                for n in range(N_OUT):
                    tile(l, G_OUT + n)
                    copy(half(hT[:, n, :], 0), PS[:, 2 * (n % 4), 0:HT]).then_inc(tile_freed_act, 1)
                phase_end(act, l, 6)
                norm_squares(l, 1, hT)
                norm_rstd(l, 1)
                act.wait_ge(x_updated, l * 3 + 1)
                norm_squares(l, 2, xT)
                norm_rstd(l, 2)

                for n in range(N_MEMKV):
                    s, t = divmod(n, 2)
                    tile(l, G_MEM + n)
                    copy(MKV[:, t, 256 * s:256 * s + 256], PS[:, 2 * (n % 4), 0:256]).then_inc(tile_freed_act, 1)
                for n in range(N_XQ):
                    tile(l, G_XQ + n)
                    f(half(QX[:, n, :], 0), PS[:, 2 * (n % 4), 0:HT], ACT.Copy, scale=X_DIM ** -0.5) \
                        .then_inc(tile_freed_act, 1)
                phase_end(act, l, 7)
                for j in range(8):
                    act.wait_ge(xa_turned, l * 28 + j + 1)
                    copy(MKT[:, j // 4, j % 4, :], PS[:, 4 + j % 2, 0:N_MEM]).then_inc(xa_put, 1)
                for k in range(21):
                    if k < 20:
                        m = P if k % 5 < 4 else DEC_SEQ
                        act.wait_ge(xa_max, l * 20 + k + 1)
                        f(XP[0:m, k % 2, :], PS[0:m, 2 * (k % 2), 0:N_MEM], ACT.Exp, bias=XST[0:m, k % 2, 0:1],
                          accum_out=XST[0:m, k % 2, 1:2])
                        act.drain().then_inc(xa_exp, 1)
                    if k >= 1:
                        m = P if (k - 1) % 5 < 4 else DEC_SEQ
                        act.wait_ge(xa_turned, l * 28 + 8 + k)
                        b = PS[:, 4 + (k - 1) % 2, 0:2 * P].rearrange("p (t n) -> p t n", t=2)[:, :, 0:m]
                        copy(XPT[:, (k - 1) % 2, :].rearrange("p (t n) -> p t n", t=2)[:, :, 0:m], b) \
                            .then_inc(xa_put, 1)
                for n in range(N_XO):
                    tile(l, G_XO + n)
                    copy(half(hT[:, n, :], 0), PS[:, 2 * (n % 4), 0:HT]).then_inc(tile_freed_act, 1)
                phase_end(act, l, 8)
                norm_squares(l, 3, hT)
                norm_rstd(l, 3)
                act.wait_ge(x_updated, l * 3 + 2)
                norm_squares(l, 4, xT)
                norm_rstd(l, 4)

                def sigmoids(it, s0, n_slots):
                    for s in range(s0, s0 + n_slots, 2):
                        for m in range(2):
                            n = 2 * s + m
                            tile(l, G_FFI + n, it, 8)
                            for h in range(2):
                                f(half(SGF[:, (s + m) % 4, :], h), PS[:, 2 * (n % 4) + h, 0:HT], ACT.Sigmoid)
                            act.drain().then_inc(tile_freed_act, 1 if m == 0 else 3)

                with act.Fori(0, 5) as it:
                    sigmoids(it, 0, 4)
                sigmoids(0, 20, 2)
                with act.Fori(0, 2) as it:
                    for m in range(4):
                        tile(l, G_FFO + m, it, 4)
                        copy(hT[:, ds(it * 4 + m, 1), 0:HT], mid(PS[:, 2 * m, 0:HT], HT)).then_inc(tile_freed_act, 1)
                phase_end(act, l, 9)
                norm_squares(l, 5, hT)
                norm_rstd(l, 5)
                act.wait_ge(x_updated, l * 3 + 3)

            for b in range(5):
                w = P if b < 4 else DEC_SEQ
                for c in range(2):
                    j = 2 * b + c
                    act.wait_ge(end_turned, j + 1)
                    copy(otok[0:w, b, c * 512:(c + 1) * 512], PS[0:w, j % 4, :])
                    act.drain().then_inc(end_put, 1)

        @block.vector
        def _(dve):
            tt, ts, stt, copy = dve.tensor_tensor, dve.tensor_scalar, dve.scalar_tensor_tensor, dve.tensor_copy

            dve.memset(ones[:, :], 1.0)
            dve.memset(eps[:, 0:1], RMS_EPS)
            dve.memset(eps[:, 1:2], GN_EPS)
            dve.memset(eps[:, 2:3], 10.0 * math.log(2.0))
            dve.sem_inc(tile_freed_dve, 4)
            dve.sem_inc(split_done, 1)
            dve.sem_inc(fx_evac, 2)
            dve.sem_inc(df_evac, 1)
            dve.wait_ge(consts_loaded, 16)
            copy(identb[:, :], const("ident"))
            copy(mfoxb[:, :], const("mfox"))
            copy(mdiffb[:, :], const("mdiff"))
            dve.drain().then_inc(consts_ready, 1)
            dve.wait_ge(setup_act, 1)
            sm = small[:, 0:4].rearrange("p (t h) -> p t h", t=2)
            tt(small[:, 4:6], sm[:, :, 0], sm[:, :, 1], ALU.add)
            dve.drain().then_inc(setup_act, 1)
            dve.wait_ge(setup_act, 3)
            for t in range(2):
                ts(mtok[:, t, :], mtok[:, t, :], small[:, 8 + t:9 + t], None, ALU.mult)
            dve.drain().then_inc(mem_scaled, 1)
            for a in range(KM):
                dve.wait_ge(setup_pe, a + 1)
                copy(xT[:, a, 2 * P:T], PS[:, 2 * (a % 4) + 1, 0:T - 2 * P]).then_inc(x_put_dve, 1)
            for a in range(KM):
                dve.wait_ge(setup_pe, KM + a + 1)
                copy(mnT[:, a, P:2 * P], PS[:, 2 * (a % 4) + 1, 0:P]).then_inc(x_put_dve, 1)

            def norm_squares(l, k, src):
                for a in range(1, KM, 2):
                    tt(SQ[:, a, :], src[:, a, :], src[:, a, :], ALU.mult).then_inc(sq_dve, 1)

            def prenorm(l, k, gain):
                dve.wait_ge(rstd_ready, l * 6 + k + 1)
                for a in range(KM):
                    stt(hT[:, a, :], xT[:, a, :], vec(gain, a), RS, ALU.mult, ALU.mult).then_inc(h_ready, 1)

            def postnorm(l, k, gain):
                dve.wait_ge(rstd_ready, l * 6 + k + 1)
                for a in range(KM):
                    stt(hT[:, a, :], hT[:, a, :], vec(gain, a), RS, ALU.mult, ALU.mult)
                dve.drain()
                for a in range(KM):
                    tt(xT[:, a, :], xT[:, a, :], hT[:, a, :], ALU.add)
                dve.drain().then_inc(x_updated, 1)

            def tile(l, g, it=0, per=0):
                dve.wait_ge(tile_done, l * TILES + g + 1 + it * per)

            def take_high(hi, src):
                copy(hi, src)

            def split_unit(l, v, it=0, per=0):
                n, kn = unit_of(v), depth_of(v)
                hi, lo, w = (x.rearrange("p k n -> p (k n)")
                             for x in (WHI[:, v % 2, 0:kn, :], WLO[:, v % 2, 0:kn, :], ring[:, n % RING, 0:kn, :]))
                dve.wait_ge(slot_loaded[n % RING], 16 * (l * USES[n % RING] + n // RING + 1 + it * (per // RING)))
                take_high(hi, w)
                dve.drain()
                tt(lo, w, hi.bitcast(F32), ALU.subtract)
                dve.drain().then_inc(split_done, 1)

            def split_x(src, hi, lo, tiles):
                for a in range(0, tiles, 2):
                    hi_a, lo_a, src_a = (x[:, a:a + 2, :].rearrange("p a n -> p (a n)") for x in (hi, lo, src))
                    take_high(hi_a, src_a)
                    dve.drain()
                    tt(lo_a, src_a, hi_a.bitcast(F32), ALU.subtract).then_inc(x_split, 1)

            with dve.Fori(0, DEPTH) as l:
                dve.wait_ge(vec_loaded, (l + 1) * 16 * 19)
                tt(lamp[:, :, :], lam4[:, 0:4:2, :], lam4[:, 1:4:2, :], ALU.mult)
                dve.drain()
                dve.tensor_reduce(small[:, 12:14], lamp[:, :, :], AX.X, ALU.add)
                dve.drain().then_inc(lam_summed, 1)
                dve.wait_ge(vec_ready, l + 1)
                c0 = _c["lam"][0]
                tt(small[:, 16:17], small[:, 15:16], small[:, 14:15], ALU.subtract)
                dve.drain()
                tt(small[:, 16:17], small[:, 16:17], CB[:, ds(l + c0, 1)], ALU.subtract)
                tt(small[:, 17:18], vec("diff_subln", 0), CB[:, ds(l + (c0 + 2), 1)], ALU.mult)
                dve.drain()
                norm_squares(l, 0, xT)
                split_unit(l, 0)
                split_unit(l, 1)
                prenorm(l, 0, "norm_mix_pre")
                phase_end(dve, l, 0)
                split_x(hT, HH, HL, KM)

                def in_tiles(it, j0, n):
                    for j in range(n):
                        s = j % 2
                        dve.wait_ge(est_free, l * 19 + j0 + j + 1 + it * 4)
                        for m in range(2):
                            n_ = 2 * (j0 + j) + m
                            tile(l, G_IN + n_, it, 8)
                            split_unit(l, n_ + 2, it, 8)
                            copy(half(EST[:, s, m, :], 1), PS[:, 2 * ((2 * j + m) % 4) + 1, 0:HT]) \
                                .then_inc(tile_freed_dve, 1)

                with dve.Fori(0, 4) as it:
                    in_tiles(it, 0, 4)
                in_tiles(0, 16, 3)
                dve.memset(ONES, 1.0)
                tile(l, G_IN + 38)
                for h in range(2):
                    ts(half(TZ[0:8, 0, :], h), PS[0:8, 4 + h, 0:HT], small[0:8, 20:21], None, ALU.add)
                dve.drain().then_inc(lf_ready_z, 1)
                dve.wait_ge(tile_freed_act, l * TILES + G_IN + 39 + 4)
                stt(AF[0:8, :], TZ[0:8, 0, :], 0.0, TZ[0:8, 1, :], ALU.min, ALU.subtract)
                dve.drain().then_inc(lf_ready, 1)
                dve.wait_ge(lf_turned, 2 * l + 1)
                copy(LFX[0:8, T:T + PAST], PS[0:8, 0, :])
                copy(LFX[0:8, 0:T], AF[0:8, :])
                dve.drain()
                ones_row = ONES[0:8, :]
                dve.tensor_tensor_scan(DC[0:8, 0:SEQ], ones_row[:, 0:SEQ], LFX[0:8, 0:SEQ], 0.0, ALU.mult, ALU.add)
                dve.tensor_tensor_scan(DC[0:8, T:T + PAST], ones_row[:, 0:PAST], LFX[0:8, T:T + PAST], 0.0, ALU.mult,
                                       ALU.add)
                dve.drain()
                dve.tensor_tensor_scan(DC[0:8, SEQ:T], ones_row[:, 0:DEC_SEQ], LFX[0:8, SEQ:T],
                                       DC[0:8, T + PAST - 1:T + PAST], ALU.mult, ALU.add)
                dve.drain()
                ts(NDC[0:8, :], DC[0:8, :], -1.0, None, ALU.mult)
                dve.drain().then_inc(dc_ready, 1)
                dve.sem_inc(tile_freed_dve, 1)
                phase_end(dve, l, 1)

                dve.memset(FQ[64:66, :, :], 1.0)
                dve.memset(FK[64:66, :, :], 1.0)
                dve.drain().then_inc(fx_rows, 1)
                with dve.Fori(0, FOX_HEADS // 2) as it:
                    g = dve.snap(l * 4 + it)

                    def fox_max(k):
                        h, i = divmod(k, 5)
                        m, n = (P, (i + 1) * P) if i < 4 else (DEC_SEQ, T)
                        dve.wait_ge(fx_scores, g * 10 + k + 1)
                        dve.tensor_reduce(FST[0:m, k % 2, 0:1], pair(k % 2)[0:m, 0:n], AX.X, ALU.max,
                                          negate=True).then_inc(fx_max, 1)

                    def fox_norm(k):
                        h, i = divmod(k, 5)
                        m, n = (P, (i + 1) * P) if i < 4 else (DEC_SEQ, T)
                        dve.wait_ge(fx_exp, g * 10 + k + 1)
                        dve.reciprocal(FST[0:m, k % 2, 2:3], FST[0:m, k % 2, 1:2])
                        dve.drain()
                        ts(FP[0:m, k % 2, 0:n], FP[0:m, k % 2, 0:n], FST[0:m, k % 2, 2:3], None, ALU.mult) \
                            .then_inc(fx_norm, 1)

                    def fox_scale(h):
                        dve.wait_ge(fx_loaded[h], (g + 1) * 16 * 7)
                        ts(FQ[0:64, h, :], FQ[0:64, h, :], HEAD_DIM ** -0.5, None, ALU.mult).then_inc(fx_scaled, 1)

                    def fox_evac(h):
                        dve.wait_ge(fx_out, g * 2 + h + 1)
                        r = slice(64 * h, 64 * h + 64)
                        copy(brT[r, ds(it, 1), :], mid(pair(3)[r, 0:T], T)).then_inc(fx_evac, 1)

                    for k in range(11):
                        if k == 0:
                            fox_scale(0)
                        if k == 3:
                            fox_scale(1)
                        if k < 10:
                            fox_max(k)
                        if k == 8:
                            fox_evac(0)
                        if k >= 1:
                            fox_norm(k - 1)
                    fox_evac(1)
                phase_end(dve, l, 2)

                dve.wait_ge(rope_loaded, 16 * (l + 1))
                settle(dve)
                with dve.Fori(0, DIFF_HEADS // 2) as it:
                    g = dve.snap(l * 2 + it)
                    for h in range(2):
                        for i, x in enumerate((DQ, DK)):
                            dve.wait_ge(df_rot, g * 4 + 2 * h + i + 1)
                            for s in range(2):
                                tt(half(DTMP, s), PS[:, 2 * i + s, 0:HT], half(ROPE[:, 1, :], s), ALU.mult)
                            tt(x[:, h, 0:T], x[:, h, 0:T], ROPE[:, 0, :], ALU.mult)
                            dve.drain()
                            tt(x[:, h, 0:T], x[:, h, 0:T], DTMP, ALU.add)
                            dve.drain()
                            if i == 0:
                                ts(x[:, h, :], x[:, h, :], HEAD_DIM ** -0.5, None, ALU.mult)
                                dve.drain()
                            dve.sem_inc(df_rotated, 1)
                        for k in range(6):
                            if k < 5:
                                m, n = (P, (k + 1) * P) if k < 4 else (DEC_SEQ, T)
                                for c in range(2):
                                    dve.wait_ge(df_scores, g * 20 + 10 * h + 2 * k + c + 1)
                                    dve.tensor_reduce(DST[0:m, k % 2, c:c + 1], pair(c)[0:m, 0:n], AX.X, ALU.max,
                                                      negate=True).then_inc(df_max, 1)
                            if k >= 1:
                                i = k - 1
                                m, n = (P, (i + 1) * P) if i < 4 else (DEC_SEQ, T)
                                st = DST[0:m, i % 2, :]
                                dve.wait_ge(df_exp, g * 20 + 10 * h + 2 * i + 2)
                                dve.reciprocal(st[:, 4:6], st[:, 2:4])
                                dve.drain()
                                tt(st[:, 6:7], st[:, 5:6], small[0:m, 16:17], ALU.mult)
                                ts(DPB[0:m, i % 2, 0, 0:n], DPB[0:m, i % 2, 0, 0:n], st[:, 4:5], None, ALU.mult)
                                dve.drain()
                                stt(DPB[0:m, i % 2, 0, 0:n], DPB[0:m, i % 2, 1, 0:n], st[:, 6:7],
                                    DPB[0:m, i % 2, 0, 0:n], ALU.mult, ALU.add).then_inc(df_comb, 1)
                        dve.wait_ge(df_rs, g * 2 + h + 1)
                        stt(brT[:, ds(it * 2 + (4 + h), 1), :], mid(pair(3)[:, 0:T], T), small[:, 17:18],
                            mid(DRS, T), ALU.mult, ALU.mult).then_inc(df_evac, 1)
                phase_end(dve, l, 3)

                dve.memset(LX[:, :, 0:1], 0.0)
                dve.wait_ge(lo_loaded, (l + 1) * 16 * 3)
                sh = _v["state_rwkv_shift"]
                for i in range(2):
                    copy(LX[:, i, SEQ + 1:SEQ + 2], VT[:, sh + 12 + i:sh + 13 + i])
                dve.drain()
                for i in range(2):
                    tt(LT[:, i, :], LX[:, i, 0:T + 1], LX[:, i, 1:T + 2], ALU.subtract)
                dve.drain()
                for i in range(2):
                    mu = vec("rwkv_mu", 12 + i)
                    stt(LXS[:, i, 0:SEQ], LT[:, i, 0:SEQ], mu, LX[:, i, 1:SEQ + 1], ALU.mult, ALU.add)
                    stt(LXS[:, i, SEQ:T], LT[:, i, SEQ + 1:T + 1], mu, LX[:, i, SEQ + 2:T + 2], ALU.mult, ALU.add)
                dve.drain().then_inc(lo_mixed, 1)
                dve.wait_ge(lo_evac_act, l * 12 + 12)
                ts(LO[:, 0:4, :], LO[:, 0:4, :], -math.exp(-0.5), None, ALU.mult)
                dve.drain().then_inc(lo_evac_dve, 1)
                phase_end(dve, l, 4)

                for t in (Rx, Kx, Vx, LWx, Ax):
                    dve.memset(t[:, T:TP], 0.0)
                with dve.Fori(0, RWKV_HEADS // 2) as it:
                    g = dve.snap(l * 4 + it)
                    X = (Rx, Kx, Vx)
                    DIF = KR.rearrange("p a b -> p (a b)")
                    BEf, KHf = (z.rearrange("p a b -> p (a b)") for z in (BE, KH))
                    T0, T1, T2 = (W_RAW[:, i, :] for i in range(3))
                    L, LM = PZA[:, 0, :], PZA[:, 1, :]
                    EL, EN, EM = WWA[:, 0, :], WWA[:, 1, :], PZA[:, 1, :]

                    def dvec(name, i):
                        return VT[:, ds(it + (_v[name] + i), 1)]

                    dve.wait_ge(rw_loaded, (g + 1) * 16 * RW_LOADS)
                    dve.memset(W_RAW[:, :, 0:1], 0.0)
                    for i in range(3):
                        copy(W_RAW[:, i, SEQ + 1:SEQ + 2], dvec("state_rwkv_shift", 4 * i))
                    dve.drain()
                    for i in range(3):
                        raw = W_RAW[:, i, :]
                        tt(DIF[:, 0:T + 1], raw[:, 0:T + 1], raw[:, 1:T + 2], ALU.subtract)
                        dve.drain()
                        mu = dvec("rwkv_mu", 4 * i)
                        stt(X[i][:, 0:SEQ], DIF[:, 0:SEQ], mu, raw[:, 1:SEQ + 1], ALU.mult, ALU.add)
                        stt(X[i][:, SEQ:T], DIF[:, SEQ + 1:T + 1], mu, raw[:, SEQ + 2:T + 2], ALU.mult, ALU.add)
                        dve.drain()
                    ts(BEf, Kx, dvec("rwkv_kk_scale", 0), None, ALU.mult)
                    dve.tensor_tensor_scan(L, const("reset"), LWx, 0.0, ALU.mult, ALU.add)
                    dve.drain()
                    tt(T0, BEf, BEf, ALU.mult)
                    tt(LM, L, LWx, ALU.subtract)
                    dve.drain().then_inc(rw_in, 1)
                    ts(T1, Ax, -1.0, dvec("rwkv_ka", 0), ALU.add, ALU.mult)
                    dve.drain()
                    stt(T1, T1, 1.0, Kx, ALU.add, ALU.mult)
                    dve.drain()
                    stt(T2, Rx, dvec("rwkv_rk", 0), T1, ALU.mult, ALU.mult)
                    dve.wait_ge(rw_sum, g * 2 + 1)
                    for s in range(2):
                        c = slice(s * (TP // 2), (s + 1) * (TP // 2))
                        ts(T0[:, c], PS[:, 6 + s, 0:TP // 2], 1e-24, 2.0 ** 20, ALU.max, ALU.mult)
                    dve.drain().then_inc(rw_clip, 2)
                    dve.sem_inc(rw_in, 1)
                    dve.wait_ge(rw_exps, g + 1)
                    copy(DCOL, EL.rearrange("p (c n) -> p c n", c=9)[:, :, CHUNK - 1])
                    tt(BEf, BEf, T0, ALU.mult)
                    tt(KHf, T1, EN, ALU.mult)
                    c9 = lambda z: z.rearrange("p (c n) -> p c n", c=9)
                    tt(KR[:, :, CHUNK:], c9(Rx), c9(EL), ALU.mult)
                    dve.drain()
                    tt(KR[:, :, 0:CHUNK], BE, c9(EM), ALU.mult)
                    tt(T1, BEf, Ax, ALU.mult)
                    dve.drain()
                    tt(BEf, T1, EN, ALU.mult)
                    dve.wait_ge(rw_sum, g * 2 + 2)
                    for s in range(2):
                        c = slice(s * (TP // 2), (s + 1) * (TP // 2))
                        tt(Ax[:, c], PS[:, 6 + s, 0:TP // 2], Vx[:, c], ALU.mult)
                    dve.drain()
                    for gr in range(3):
                        dve.sem_inc(rw_ev[gr], 1)

                    def evac(s, gr):
                        X1, X2, Ao, GTt, HTt, Vt, Bt = range(7)
                        rt = X2
                        pl, wy, nz = PL[gr], WW[gr], PZ[gr]
                        lo, hi = slice(0, 64), slice(64, 128)

                        def v3(a):
                            return a.rearrange("p (c n) -> p c n", c=3)

                        def c3(name):
                            return v3(const(name))

                        def bank(i, at, n=64):
                            return v3(PS[:, 2 * gr + i, at:at + 3 * n])

                        dve.wait_ge(rw_mm[gr], g * 11 + s)
                        if s == 1:
                            b0, b1 = bank(0, 0, 128), bank(1, 0, 128)
                            tt(pl[X1], b0[:, :, 0:64], c3("up_d"), ALU.mult)
                            tt(pl[GTt], b0[:, :, 64:128], c3("up_i"), ALU.mult)
                            tt(pl[HTt], b1[:, :, 64:128], c3("up_i"), ALU.mult)
                            tt(BD[gr][5][lo, :, 0:64], b1[lo, :, 0:64], c3("up_s")[lo], ALU.mult)
                            tt(BD[gr][5][hi, :, 64:128], b1[hi, :, 0:64], c3("up_s")[hi], ALU.mult)
                        if s == 2:
                            a = bank(0, 0)
                            tt(pl[X2], a, c3("lo_d"), ALU.mult)
                            tt(pl[Ao], a, c3("lo_o"), ALU.mult)
                            tt(BD[gr][3][lo, :, 0:64], a[lo], c3("lo_d")[lo], ALU.mult)
                            tt(BD[gr][3][hi, :, 64:128], a[hi], c3("lo_d")[hi], ALU.mult)
                            copy(pl[Vt], bank(0, 192))
                            copy(wy[:, :, 0:64], bank(1, 0))
                            copy(pl[Bt], bank(1, 192))
                        if s == 3:
                            copy(wy[:, :, 64:128], bank(0, 0))
                            copy(nz[:, :, 0:64], bank(1, 0))
                            tt(nz[:, :, 64:128], pl[X1], c3("stack"), ALU.add)
                            copy(pl[X2], bank(1, 192))
                        if s == 4:
                            tt(nz[:, :, 64:128], bank(0, 0, 128)[:, :, 64:128], nz[:, :, 64:128], ALU.add)
                            copy(pl[X2], bank(1, 0))
                        if s == 5:
                            tt(nz[:, :, 64:128], bank(0, 0), nz[:, :, 64:128], ALU.add)
                        if s == 6:
                            z = nz[:, :, 64:128]
                            tt(BD[gr][0][lo, :, 0:64], bank(0, 0)[lo], z[lo], ALU.add)
                            tt(BD[gr][0][hi, :, 64:128], bank(0, 0)[hi], z[hi], ALU.add)
                            dve.drain()
                            tt(z, bank(0, 0), z, ALU.add)
                        if s == 7:
                            copy(pl[X1], bank(0, 0))
                            copy(wy, bank(1, 0, 128))
                        if s == 8:
                            tt(wy, wy, bank(1, 0, 128), ALU.subtract)
                        if s == 9:
                            stt(wy, bank(1, 0, 128), -1.0, wy, ALU.mult, ALU.subtract)
                        if s == 10:
                            tt(pl[rt], bank(0, 0), KR[:, 3 * gr:3 * gr + 3, CHUNK:], ALU.add)
                            m = bank(0, 192)
                            tt(BD[gr][2][lo, :, 0:64], m[lo], c3("stack")[lo], ALU.add)
                            tt(BD[gr][2][hi, :, 64:128], m[hi], c3("stack")[hi], ALU.add)
                        if s == 11:
                            copy(Yx[:, 192 * gr:192 * gr + 192], PS[:, 2 * gr + 1, 0:192])
                        dve.drain().then_inc(rw_ev[gr], 1)

                    for s in range(1, 11):
                        for gr in range(3):
                            evac(s, gr)
                    dve.wait_ge(rw_state, g * 10 + 1)
                    copy(BDS[:, 8, :], PS[:, 7, 256:384]).then_inc(rw_chain, 1)
                    for c in range(9):
                        dve.wait_ge(rw_state, g * 10 + c + 2)
                        to = c + 1 if c < 7 else c + 2
                        ts(BDS[:, to, :], PS[:, 6 + c % 2, 0:P], DCOL[:, c:c + 1], None, ALU.mult) \
                            .then_inc(rw_chain, 1)
                    for gr in range(3):
                        evac(11, gr)
                    dve.sem_inc(rp_y, 1)
                    dve.wait_ge(rp_mean, g + 1)
                    for s in range(2):
                        c = slice(s * (TP // 2), (s + 1) * (TP // 2))
                        stt(Yx[:, c], PS[:, 6 + s, 0:TP // 2], -1.0 / HEAD_DIM, Yx[:, c], ALU.mult, ALU.add)
                    dve.drain().then_inc(rp_yc, 1)
                    dve.wait_ge(rp_rs, g + 1)
                    stt(Yx, Yx, dvec("rwkv_ln_gain", 0), T0, ALU.mult, ALU.mult)
                    dve.drain()
                    stt(Yx, Yx, dvec("rwkv_ln_bias", 0), Ax, ALU.add, ALU.add)
                    dve.drain()
                    tt(brT[:, ds(it + 8, 1), :], mid(Yx[:, 0:T], T), mid(Gx[:, 0:T], T), ALU.mult)
                    dve.memset(Ax[:, T:TP], 0.0)
                    dve.memset(Kx[:, T:TP], 0.0)
                    dve.drain().then_inc(rp_done, 1)
                phase_end(dve, l, 5)

                split_x(hT, HX, hTR, KM)
                split_x(brT, BH, brTR, 12)
                with dve.Fori(0, 2) as it:
                    for s in range(1, 12, 2):
                        i = s % 6 // 2
                        for n in (2 * s - 2, 2 * s - 1):
                            tile(l, G_MERGE + n, it, 24)
                            split_unit(l, V_MERGE + n + 2, it, 24)
                        for m in range(2):
                            n = 2 * s + m
                            sg, to = SG[:, (s - 1 + m) % 4, :], YT[:, ds(it * 4 + (2 * (s // 6) + m), 1), :]
                            tile(l, G_MERGE + n, it, 24)
                            split_unit(l, V_MERGE + n + 2, it, 24)
                            dve.wait_ge(tile_freed_act, l * TILES + G_MERGE + n - 2 + 5 + it * 24)
                            for h in range(2):
                                dst = to[:, :, h * HT:(h + 1) * HT] if i == 0 else mid(half(TM[:, m, :], h), HT)
                                tt(dst, mid(PS[:, 2 * (n % 4) + h, 0:HT], HT), mid(half(sg, h), HT), ALU.mult)
                            dve.drain().then_inc(tile_freed_dve, 1 if m == 0 else 3)
                            if i > 0:
                                tt(to, to, mid(TM[:, m, :], T), ALU.add)
                                dve.drain()
                            if i == 2:
                                y_hi = YH[:, ds(it * 4 + (2 * (s // 6) + m), 1), :]
                                take_high(y_hi, to)
                                dve.drain()
                                tt(YL[:, ds(it * 4 + (2 * (s // 6) + m), 1), :], to, y_hi.bitcast(F32), ALU.subtract)
                                dve.drain()
                dve.drain().then_inc(y_ready, 1)
                for n in range(N_OUT):
                    tile(l, G_OUT + n)
                    if n + 2 < N_OUT:
                        split_unit(l, V_OUT + n + 2)
                    copy(half(hT[:, n, :], 1), PS[:, 2 * (n % 4) + 1, 0:HT]).then_inc(tile_freed_dve, 1)
                phase_end(dve, l, 6)
                norm_squares(l, 1, hT)
                postnorm(l, 1, "norm_mix_post")
                norm_squares(l, 2, xT)
                prenorm(l, 2, "norm_x_pre")

                dve.wait_ge(memn_loaded, 16 * (l + 1))
                for a in range(KM):
                    ts(MNT[:, a, :], MNT[:, a, :], vec("norm_mem", a), None, ALU.mult)
                dve.drain().then_inc(mem_scaled, 1)
                dve.sem_inc(tile_freed_dve, N_MEMKV)
                for n in range(N_XQ):
                    tile(l, G_XQ + n)
                    ts(half(QX[:, n, :], 1), PS[:, 2 * (n % 4) + 1, 0:HT], X_DIM ** -0.5, None, ALU.mult) \
                        .then_inc(tile_freed_dve, 1)
                phase_end(dve, l, 7)

                def x_evac(h):
                    dve.wait_ge(xa_out, l * 4 + h + 1)
                    copy(OX[:, h, :], pair(3)[:, 0:T]).then_inc(xa_evac, 1)

                for k in range(21):
                    if k < 20:
                        m = P if k % 5 < 4 else DEC_SEQ
                        dve.wait_ge(xa_scores, l * 20 + k + 1)
                        dve.tensor_reduce(XST[0:m, k % 2, 0:1], PS[0:m, 2 * (k % 2), 0:N_MEM], AX.X, ALU.max,
                                          negate=True).then_inc(xa_max, 1)
                    if k >= 1:
                        j = k - 1
                        m = P if j % 5 < 4 else DEC_SEQ
                        dve.wait_ge(xa_exp, l * 20 + j + 1)
                        dve.reciprocal(XST[0:m, j % 2, 2:3], XST[0:m, j % 2, 1:2])
                        dve.drain()
                        ts(XP[0:m, j % 2, :], XP[0:m, j % 2, :], XST[0:m, j % 2, 2:3], None, ALU.mult) \
                            .then_inc(xa_norm, 1)
                    if k in (7, 12, 17):
                        x_evac((k - 7) // 5)
                x_evac(3)
                for n in range(N_XO):
                    tile(l, G_XO + n)
                    copy(half(hT[:, n, :], 1), PS[:, 2 * (n % 4) + 1, 0:HT]).then_inc(tile_freed_dve, 1)
                phase_end(dve, l, 8)
                norm_squares(l, 3, hT)
                postnorm(l, 3, "norm_x_post")
                norm_squares(l, 4, xT)
                split_unit(l, V_FFI)
                split_unit(l, V_FFI + 1)
                prenorm(l, 4, "norm_ffn_pre")
                dve.drain()
                split_x(hT, HF, hTR, KM)

                def products(it, s0, n_slots):
                    for s in range(s0, s0 + n_slots, 2):
                        for n in (2 * s, 2 * s + 1):
                            tile(l, G_FFI + n, it, 8)
                            split_unit(l, V_FFI + n + 2, it, 8)
                        for m in range(2):
                            n = 2 * s + m
                            sg = SGF[:, (s + m) % 4, :]
                            tile(l, G_FFI + n + 2, it, 8)
                            split_unit(l, V_FFI + n + 4, it, 8)
                            dve.wait_ge(tile_freed_act, l * TILES + G_FFI + n + 1 + 4 + it * 8)
                            for h in range(2):
                                tt(half(sg, h), PS[:, 2 * (n % 4) + h, 0:HT], half(sg, h), ALU.mult)
                            dve.drain()
                            for h in range(2):
                                tt(half(sg, h), PS[:, 2 * ((n + 2) % 4) + h, 0:HT], half(sg, h), ALU.mult)
                            dve.drain().then_inc(tile_freed_dve, 1 if m == 0 else 3)
                            g_hi, g_lo = (x[:, s + m:s + m + 1, :] if isinstance(it, int) else
                                          x[:, ds(it * 4 + (s + m), 1), :] for x in (GH, GL))
                            take_high(g_hi, mid(sg, T))
                            dve.drain()
                            tt(g_lo, mid(sg, T), g_hi.bitcast(F32), ALU.subtract)

                with dve.Fori(0, 5) as it:
                    products(it, 0, 4)
                products(0, 20, 2)
                dve.drain().then_inc(g_ready, 1)
                for v in range(24):
                    n, part = divmod(v, 3)
                    if part == 2:
                        tile(l, G_FFO + n)
                    else:
                        dve.wait_ge(part_used, l * 16 + 2 * n + part + 1)
                    if v + 2 < 24:
                        split_unit(l, V_FFO + v + 2)
                    if part == 2:
                        copy(half(hT[:, n, :], 1), PS[:, 2 * (n % 4) + 1, 0:HT]).then_inc(tile_freed_dve, 1)
                phase_end(dve, l, 9)
                norm_squares(l, 5, hT)
                postnorm(l, 5, "norm_ffn_post")
                dve.sem_inc(x_done, 1)

        @block.gpsimd
        def _(pool):
            dma = pool.dma_start

            def wait(sem_, value):
                pool.wait_ge(sem_, value)
                settle(pool)

            for s_ in (est_free, est_free, *fx_free, *df_free, rw_free):
                pool.sem_inc(s_, 1)
            dma(CB[:, :], C_const).then_inc(consts_loaded, 16)
            dma(xtok[:, 0:4, :], A["x_prompt"].rearrange("b (t p) d -> p (b t) d", p=P)).then_inc(x_loaded, 16)
            dma(xtok[0:DEC_SEQ, 4, :], A["x_sample"].rearrange("b t d -> (b t) d")).then_inc(x_loaded, 16)
            dma(mtok[:, :, :], A["mem_prompt"].rearrange("b (t p) d -> p (b t) d", p=P)).then_inc(x_loaded, 16)
            pool.wait_ge(x_put_act, 2 * KM)
            pool.wait_ge(x_put_dve, 2 * KM)
            dma(memn_d, mnT.rearrange("p a b -> p (a b)")).then_inc(memn_stored, 16)
            pool.wait_ge(memn_stored, 16)

            with pool.Fori(0, DEPTH) as l:
                for name, row in _v.items():
                    a = A[name][ds(l, 1)]
                    n = NVEC_OF[name]
                    if name == "rwkv_rk":
                        src = a.rearrange("l (r h) d -> (l r) (h d)", r=4)
                    elif name == "state_rwkv_shift":
                        src = a.rearrange("l b (r c) -> (l b r) c", c=P)
                    else:
                        src = a.rearrange("l (r c) -> (l r) c", c=P)
                    dma(VR[row:row + n, :], src).then_inc(vec_loaded, 16)
                dma(small[0:8, 20:21], A["fox_forget_bias"][ds(l, 1)].rearrange("l h -> h l"),
                    allow_slow_non_contiguous=True).then_inc(vec_loaded, 16)
                dma(lam4[:, :, :].rearrange("p a b -> p (a b)"),
                    A["diff_lambda"][ds(l, 1)].rearrange("l a b -> l (a b)").to_broadcast([P, 256])) \
                    .then_inc(vec_loaded, 16)
                dma(PLF[:, :, :], A["cache_fox_logf"][ds(l, 1)].rearrange("l b (t p) h -> p (l b t) h", p=P)) \
                    .then_inc(plf_loaded, 16)
                wait(h_ready, l * 24 + 8)
                wait(vec_loaded, (l + 1) * 16 * 19)
                wait(plf_loaded, (l + 1) * 16)
                phase_end(pool, l, 0)

                def store_tiles(it, j0, n):
                    for j in range(n):
                        c = l * TILES + G_IN + 2 * (j0 + j) + 2 + 4 + it * 8
                        wait(tile_freed_act, c)
                        wait(tile_freed_dve, c)
                        rows = proj_d[ds(it * 1024 + (j0 + j) * 256, 256), :] if not isinstance(it, int) else \
                            proj_d[(j0 + j) * 256:(j0 + j) * 256 + 256, :]
                        dma(rows.rearrange("(m p) t -> p m t", p=P), EST[:, j % 2, :, :]) \
                            .then_inc(est_stored[j % 2], 16)
                        wait(est_stored[j % 2], 16 * (l * (10 - j % 2) + (j0 + j) // 2 + 1 + it * 2))
                        pool.sem_inc(est_free, 1)

                with pool.Fori(0, 4) as it:
                    store_tiles(it, 0, 4)
                store_tiles(0, 16, 3)
                wait(dc_ready, l + 1)
                dma(dcum_d[0], DC[0:8, :]).then_inc(lf_stored, 16)
                dma(dcum_d[1], NDC[0:8, :]).then_inc(lf_stored, 16)
                wait(lf_put, l + 1)
                dma(p_fox_logf[ds(l, 1)].rearrange("l b (t p) h -> p (l b t) h", p=P), LFT[:, 0:4, :]) \
                    .then_inc(lf_stored, 16)
                dma(s_fox_logf[ds(l, 1)].rearrange("l b t h -> (l b t) h"), LFT[0:DEC_SEQ, 4, :]).then_inc(lf_stored, 16)
                wait(lf_stored, (l + 1) * 64)
                for src, to in ((SEQ - 1, p_shift), (T - 1, s_shift)):
                    dma(to[ds(l, 1)].rearrange("l b c -> (l b c)").rearrange("(c o) -> c o", o=1),
                        proj_d[R_RW:R_RW + RWKV_IN, src:src + 1], allow_slow_non_contiguous=True).then_inc(shift_stored, 16)
                wait(shift_stored, (l + 1) * 32)
                phase_end(pool, l, 1)

                with pool.Fori(0, FOX_HEADS // 2) as it:
                    g = pool.snap(l * 4 + it)
                    for h in range(2):
                        wait(fx_put, g * 16 + (3, 8)[h] + 2)
                        for t, op, os_ in ((FVT, p_fox_v, s_fox_v), (FKT, p_fox_k, s_fox_k)):
                            dma(op[ds(l, 1), :, :, ds(it * 2 + h, 1), :].rearrange("l b (t p) h d -> p (l b t h) d", p=P),
                                t[:, h, 0:4, :]).then_inc(fx_stored[h], 16)
                            dma(os_[ds(l, 1), :, :, ds(it * 2 + h, 1), :].rearrange("l b t h d -> (l b t h) d"),
                                t[0:DEC_SEQ, h, 4, :]).then_inc(fx_stored[h], 16)
                    for h in range(2):
                        wait(fx_evac, g * 2 + h + 3)
                        wait(fx_stored[h], (g + 1) * 64)
                        pool.sem_inc(fx_free[h], 1)
                phase_end(pool, l, 2)

                with pool.Fori(0, DIFF_HEADS // 2) as it:
                    g = pool.snap(l * 2 + it)
                    for h in range(2):
                        wait(df_put, g * 18 + 9 * h + 4)
                        dma(p_diff_v[ds(l, 1), :, :, ds(it * 2 + h, 1), :]
                            .rearrange("l b (t p) h d -> p (l b t h) d", p=P), DVT[:, h, 0:4, :]) \
                            .then_inc(df_stored[h], 16)
                        dma(s_diff_v[ds(l, 1), :, :, ds(it * 2 + h, 1), :].rearrange("l b t h d -> (l b t h) d"),
                            DVT[0:DEC_SEQ, h, 4, :]).then_inc(df_stored[h], 16)
                        dma(p_diff_k[ds(l, 1), :, :, ds(it * 2 + h, 1), :, :]
                            .rearrange("l b (t p) h c d -> p (l b t h) (c d)", p=P), DKT[:, h, 0:4, :]) \
                            .then_inc(df_stored[h], 16)
                        dma(s_diff_k[ds(l, 1), :, :, ds(it * 2 + h, 1), :, :]
                            .rearrange("l b t h c d -> (l b t h) (c d)"), DKT[0:DEC_SEQ, h, 4, :]) \
                            .then_inc(df_stored[h], 16)
                        wait(df_evac, g * 2 + h + 2)
                        wait(df_stored[h], (g + 1) * 64)
                        pool.sem_inc(df_free[h], 1)
                phase_end(pool, l, 3)

                wait(lo_evac_dve, l + 1)
                dma(proj_d[R_LW:R_END, :].rearrange("(a p) t -> p a t", p=P), LO).then_inc(lo_stored, 16)
                wait(lo_stored, 16 * (l + 1))
                phase_end(pool, l, 4)

                pool.memset(BDALL, 0.0)
                pool.drain().then_inc(rw_cleared, 1)
                with pool.Fori(0, RWKV_HEADS // 2) as it:
                    g = pool.snap(l * 4 + it)
                    for gr in range(3):
                        wait(rw_ev[gr], g * 12 + 1)
                        for slot, src in ((2, KR[:, 3 * gr:3 * gr + 3, 0:CHUNK]),
                                          (3, Vx.rearrange("p (c n) -> p c n", c=9)[:, 3 * gr:3 * gr + 3, :])):
                            pool.tensor_copy(BD[gr][slot][0:64, :, 0:64], src[0:64])
                            pool.tensor_copy(BD[gr][slot][64:128, :, 64:128], src[64:128])
                        pool.drain().then_inc(rw_bd, 1)
                    wait(rw_fin, g + 1)
                    for h in range(2):
                        r = slice(64 * h, 64 * h + 64)
                        for i, o in enumerate((p_state, s_state)):
                            dma(o[ds(l, 1), :, ds(it * 2 + h, 1), :, :].rearrange("l b h v k -> (l b h v) k"),
                                XS[r, i, 64 * h:64 * h + 64]).then_inc(rw_stored, 16)
                    wait(rw_stored, (g + 1) * 64)
                    wait(rp_done, g + 1)
                    pool.sem_inc(rw_free, 1)
                phase_end(pool, l, 5)
                phase_end(pool, l, 6)

                dma(MNT.rearrange("p a b -> p (a b)"), memn_d).then_inc(memn_loaded, 16)
                for t, name in ((CKT, "cache_mem_k"), (CVT, "cache_mem_v")):
                    dma(t, A[name][ds(l, 1)].rearrange("l b (t p) h d -> p (l b t) (h d)", p=P)).then_inc(xa_loaded, 16)
                phase_end(pool, l, 7)
                for t, o in ((0, p_mem_k), (512, p_mem_v)):
                    dma(o[ds(l, 1)].rearrange("l b (t p) h d -> p (l b t) (h d)", p=P), MKV[:, :, t:t + 512]) \
                        .then_inc(xa_stored, 16)
                wait(xa_stored, (l + 1) * 32)
                phase_end(pool, l, 8)
                pool.drain().then_inc(bar, 1)

            for b in range(5):
                pool.wait_ge(end_put, 2 * b + 2)
                if b < 4:
                    dma(y_prompt[0, b * P:(b + 1) * P, :], otok[:, b, :]).then_inc(end_stored, 16)
                else:
                    dma(y_sample[0, :, :], otok[0:DEC_SEQ, 4, :]).then_inc(end_stored, 16)
            pool.wait_ge(end_stored, 5 * 16)


_INS = ['x_prompt', 'x_sample', 'mem_prompt', 'cache_fox_k', 'cache_fox_v', 'cache_fox_logf', 'cache_diff_k',
        'cache_diff_v', 'state_rwkv', 'state_rwkv_shift', 'cache_mem_k', 'cache_mem_v', 'norm_mix_pre',
        'norm_mix_post', 'w_in', 'fox_forget_bias', 'diff_lambda', 'diff_subln', 'rwkv_mu', 'rwkv_w0', 'rwkv_w2',
        'rwkv_a0', 'rwkv_a2', 'rwkv_g2', 'rwkv_kk_scale', 'rwkv_ka', 'rwkv_rk', 'rwkv_ln_gain', 'rwkv_ln_bias',
        'w_branch', 'w_out', 'norm_x_pre', 'norm_x_post', 'norm_mem', 'w_xq', 'w_xkv', 'w_xo', 'norm_ffn_pre',
        'norm_ffn_post', 'w_ffn_in', 'w_ffn_out']
_L = DEPTH
_OUTS = [(1, SEQ, D_MODEL), (1, DEC_SEQ, D_MODEL),
         (_L, 1, SEQ, 8, 64), (_L, 1, SEQ, 8, 64), (_L, 1, SEQ, 8), (_L, 1, SEQ, 4, 2, 64), (_L, 1, SEQ, 4, 128),
         (_L, 1, 8, 64, 64), (_L, 1, RWKV_IN), (_L, 1, N_MEM, 4, 128), (_L, 1, N_MEM, 4, 128),
         (_L, 1, DEC_SEQ, 8, 64), (_L, 1, DEC_SEQ, 8, 64), (_L, 1, DEC_SEQ, 8), (_L, 1, DEC_SEQ, 4, 2, 64),
         (_L, 1, DEC_SEQ, 4, 128), (_L, 1, 8, 64, 64), (_L, 1, RWKV_IN)]


def kernel(**inputs):
    import numpy as _np
    import concourse.bacc as _bacc
    from concourse import mybir as _mybir
    from concourse.bass_utils import run_bass_kernel_spmd as _run

    nc = _bacc.Bacc("TRN2", target_bir_lowering=False, num_devices=1)
    arrays, args = {}, {}
    for name in _INS:
        a = _np.ascontiguousarray(inputs[name])
        arrays[f"in_{name}_dram"] = a
        args[name] = nc.dram_tensor(f"in_{name}_dram", a.shape, _mybir.dt.from_np(a.dtype), kind="ExternalInput").ap()
    tables = []
    for name, a in zip(("const", "rope"), constants()):
        arrays[f"in_{name}_dram"] = a
        tables.append(nc.dram_tensor(f"in_{name}_dram", a.shape, _mybir.dt.from_np(a.dtype), kind="ExternalInput").ap())
    outs = [nc.dram_tensor(f"out_{i}_dram", shape, _mybir.dt.float32, kind="ExternalOutput").ap()
            for i, shape in enumerate(_OUTS)]
    build_program(nc, args, *tables, outs)
    r = _run(nc, [arrays], core_ids=[0])
    return tuple(r.results[0][f"out_{i}_dram"] for i in range(len(_OUTS)))
```
